# Optimizing a Trainium2 kernel written in Bass

```python
import jax, jax.numpy as jnp
from jax import lax
import numpy as np

D_MODEL = 1024
BATCH = 1
SEQ = 256
DEPTH = 1

POOL_WINDOWS = (2, 4, 8, 16)
POOL_GROUPS = len(POOL_WINDOWS)
POOL_GROUP_DIM = D_MODEL // 16
POOL_WIDTH = POOL_GROUPS * POOL_GROUP_DIM
ATTN_PATTERNS = ((128, 1), (512, 4), (2048, 16))
N_ATTN_GROUPS = len(ATTN_PATTERNS)
HEAD_DIM = 64
HEADS_PER_GROUP = 4
N_ATTN_HEADS = N_ATTN_GROUPS * HEADS_PER_GROUP
ATTN_WIDTH = N_ATTN_HEADS * HEAD_DIM
ATTN_OUT_WIDTH = HEADS_PER_GROUP * HEAD_DIM
ROPE_THETA = 10000.0
BLOCK = 128
N_BRANCHES = 2
IN_WIDTH = POOL_WIDTH + 3 * ATTN_WIDTH + N_BRANCHES * D_MODEL
D_FF = ((8 * D_MODEL // 3 + 255) // 256) * 256
N_MOD = 9
EPS = 1e-6


def rmsnorm(x, g):
    xf = x.astype(jnp.float32)
    y = xf * lax.rsqrt(jnp.mean(xf * xf, axis=-1, keepdims=True) + EPS)
    return (y * g.astype(jnp.float32)).astype(x.dtype)

def modulate(x, shift, scale):
    return x * (1 + scale) + shift

def swiglu(u, w_in, w_out):
    a, b = jnp.split(u @ w_in, 2, axis=-1)
    return (jax.nn.silu(a) * b) @ w_out

def rope_tables(positions, dtype):
    inv_freq = ROPE_THETA ** (-jnp.arange(0, HEAD_DIM, 2, dtype=jnp.float32) / HEAD_DIM)
    ang = positions.astype(jnp.float32)[..., None] * inv_freq
    return jnp.cos(ang)[:, :, None, :].astype(dtype), jnp.sin(ang)[:, :, None, :].astype(dtype)

def apply_rope(t, cos, sin):
    t1, t2 = jnp.split(t, 2, axis=-1)
    return jnp.concatenate([t1 * cos - t2 * sin, t2 * cos + t1 * sin], axis=-1)

def multiscale_pool(p, w_pool, pool_scale):
    B, S, _ = p.shape
    pf = p.astype(jnp.float32)
    cs = jnp.pad(jnp.cumsum(pf, axis=1), ((0, 0), (1, 0), (0, 0)))
    t = jnp.arange(S)
    outs = []
    for gi, w in enumerate(POOL_WINDOWS):
        sl = slice(gi * POOL_GROUP_DIM, (gi + 1) * POOL_GROUP_DIM)
        csg = cs[..., sl]
        lagged = jnp.pad(csg[:, :S + 1 - w], ((0, 0), (w - 1, 0), (0, 0)))
        count = jnp.minimum(t + 1, w).astype(jnp.float32)[None, :, None]
        outs.append((csg[:, 1:] - lagged) / count - pf[..., sl])
    d = jnp.stack(outs, axis=2).astype(p.dtype)
    y = jnp.einsum('bsgc,gcd->bsgd', d, w_pool)
    return y.reshape(B, S, POOL_WIDTH) * pool_scale

def dilated_window_attention(q, k, v, steps, dilation):
    B, S, H, Dh = q.shape
    L = S // dilation
    nb = -(-L // BLOCK)
    Lp = nb * BLOCK

    def to_strided(t):
        t = t.reshape(B, L, dilation, H, Dh).transpose(0, 3, 2, 1, 4)
        return jnp.pad(t, ((0, 0), (0, 0), (0, 0), (0, Lp - L), (0, 0)))

    qs, ks, vs = to_strided(q), to_strided(k), to_strided(v)
    qb = qs.reshape(B, H, dilation, nb, BLOCK, Dh)

    def band(t):
        tp = jnp.pad(t, ((0, 0), (0, 0), (0, 0), (BLOCK, 0), (0, 0)))
        prev = tp[..., :Lp, :].reshape(B, H, dilation, nb, BLOCK, Dh)
        cur = t.reshape(B, H, dilation, nb, BLOCK, Dh)
        return jnp.concatenate([prev, cur], axis=-2)

    kb, vb = band(ks), band(vs)
    a = jnp.arange(BLOCK)[:, None]
    cidx = jnp.arange(2 * BLOCK)[None, :]
    rel = a + BLOCK - cidx
    in_band = (rel >= 0) & (rel <= steps)
    key_pos = jnp.arange(nb)[:, None, None] * BLOCK - BLOCK + cidx[None]
    mask = in_band[None] & (key_pos >= 0)

    s = jnp.einsum('bhrnqd,bhrnkd->bhrnqk', qb, kb).astype(jnp.float32) * (HEAD_DIM ** -0.5)
    s = jnp.where(mask, s, -jnp.inf)
    lse = jax.nn.logsumexp(s, axis=-1)
    pr = jnp.exp(s - lse[..., None]).astype(v.dtype)
    o = jnp.einsum('bhrnqk,bhrnkd->bhrnqd', pr, vb)
    o = o.reshape(B, H, dilation, Lp, Dh)[:, :, :, :L]
    o = o.transpose(0, 3, 2, 1, 4).reshape(B, S, H, Dh)
    lse = lse.reshape(B, H, dilation, Lp)[:, :, :, :L].transpose(0, 3, 2, 1).reshape(B, S, H)
    return o, lse

def token_mixing(u, cos, sin, w_in, w_pool, pool_scale, w_pool_branch, w_attn_branch, w_out):
    B, S, _ = u.shape
    proj = u @ w_in
    cuts = [POOL_WIDTH, POOL_WIDTH + ATTN_WIDTH, POOL_WIDTH + 2 * ATTN_WIDTH,
            POOL_WIDTH + 3 * ATTN_WIDTH]
    p, q, k, v, gate_logits = jnp.split(proj, cuts, axis=-1)

    y_pool = multiscale_pool(p, w_pool, pool_scale)

    q = apply_rope(q.reshape(B, S, N_ATTN_HEADS, HEAD_DIM), cos, sin)
    k = apply_rope(k.reshape(B, S, N_ATTN_HEADS, HEAD_DIM), cos, sin)
    v = v.reshape(B, S, N_ATTN_HEADS, HEAD_DIM)
    outs, lses = [], []
    for gi, (window, dilation) in enumerate(ATTN_PATTERNS):
        hs = slice(gi * HEADS_PER_GROUP, (gi + 1) * HEADS_PER_GROUP)
        o, lse = dilated_window_attention(q[:, :, hs], k[:, :, hs], v[:, :, hs],
                                          window // dilation, dilation)
        outs.append(o)
        lses.append(lse)
    wts = jax.nn.softmax(jnp.stack(lses, axis=0), axis=0)
    y_attn = jnp.einsum('gbsh,gbshd->bshd', wts.astype(v.dtype), jnp.stack(outs, axis=0))
    y_attn = y_attn.reshape(B, S, ATTN_OUT_WIDTH)

    gates = jax.nn.sigmoid(gate_logits.astype(jnp.float32)).astype(u.dtype)
    g_pool, g_attn = jnp.split(gates, N_BRANCHES, axis=-1)
    merged = g_pool * (y_pool @ w_pool_branch) + g_attn * (y_attn @ w_attn_branch)
    return merged @ w_out

def first_inputs(seed: int = 0) -> dict:
    key = jax.random.key(seed)
    ks = jax.random.split(key, 20)
    f32 = jnp.float32

    def lin(k, shape, fan_in, scale=1.0):
        return jax.random.normal(k, shape, f32) * (scale * fan_in ** -0.5)

    def gain(k, shape):
        return 1.0 + 0.05 * jax.random.normal(k, shape, f32)

    x = jax.random.normal(ks[0], (BATCH, SEQ, D_MODEL), f32)
    c = jax.random.normal(ks[1], (BATCH, D_MODEL), f32)
    offset = jax.random.randint(ks[2], (BATCH, 1), 0, 1024, dtype=jnp.int32)
    positions = (jnp.arange(SEQ, dtype=jnp.int32)[None, :] + offset).astype(jnp.int32)
    return {
        "x": x,
        "c": c,
        "positions": positions,
        "w_ada": lin(ks[3], (DEPTH, D_MODEL, N_MOD * D_MODEL), D_MODEL, 0.5),
        "b_ada": 0.02 * jax.random.normal(ks[4], (DEPTH, N_MOD * D_MODEL), f32),
        "g_norm_ffn1": gain(ks[5], (DEPTH, D_MODEL)),
        "w_ffn1_in": lin(ks[6], (DEPTH, D_MODEL, 2 * D_FF), D_MODEL),
        "w_ffn1_out": lin(ks[7], (DEPTH, D_FF, D_MODEL), D_FF),
        "g_norm_mix": gain(ks[8], (DEPTH, D_MODEL)),
        "w_in": lin(ks[9], (DEPTH, D_MODEL, IN_WIDTH), D_MODEL),
        "w_pool": lin(ks[10], (DEPTH, POOL_GROUPS, POOL_GROUP_DIM, POOL_GROUP_DIM), POOL_GROUP_DIM),
        "pool_scale": 1.0 + 0.1 * jax.random.normal(ks[11], (DEPTH, POOL_WIDTH), f32),
        "w_pool_branch": lin(ks[12], (DEPTH, POOL_WIDTH, D_MODEL), POOL_WIDTH),
        "w_attn_branch": lin(ks[13], (DEPTH, ATTN_OUT_WIDTH, D_MODEL), ATTN_OUT_WIDTH),
        "w_out": lin(ks[14], (DEPTH, D_MODEL, D_MODEL), D_MODEL),
        "g_norm_ffn2": gain(ks[15], (DEPTH, D_MODEL)),
        "w_ffn2_in": lin(ks[16], (DEPTH, D_MODEL, 2 * D_FF), D_MODEL),
        "w_ffn2_out": lin(ks[17], (DEPTH, D_FF, D_MODEL), D_FF),
        "g_final": gain(ks[18], (D_MODEL,)),
    }

def first_block(x, c, positions, w_ada, b_ada, g_norm_ffn1, w_ffn1_in, w_ffn1_out,
              g_norm_mix, w_in, w_pool, pool_scale, w_pool_branch, w_attn_branch, w_out,
              g_norm_ffn2, w_ffn2_in, w_ffn2_out, g_final):
    cos, sin = rope_tables(positions, x.dtype)
    cond = jax.nn.silu(c)
    h = x
    for l in range(DEPTH):
        mod = cond @ w_ada[l] + b_ada[l]
        sh1, sc1, gt1, sh2, sc2, gt2, sh3, sc3, gt3 = [
            m[:, None, :] for m in jnp.split(mod, N_MOD, axis=-1)]
        u = modulate(rmsnorm(h, g_norm_ffn1[l]), sh1, sc1)
        h = h + 0.5 * gt1 * swiglu(u, w_ffn1_in[l], w_ffn1_out[l])
        u = modulate(rmsnorm(h, g_norm_mix[l]), sh2, sc2)
        h = h + gt2 * token_mixing(u, cos, sin, w_in[l], w_pool[l], pool_scale[l],
                                   w_pool_branch[l], w_attn_branch[l], w_out[l])
        u = modulate(rmsnorm(h, g_norm_ffn2[l]), sh3, sc3)
        h = h + 0.5 * gt3 * swiglu(u, w_ffn2_in[l], w_ffn2_out[l])
    return rmsnorm(h, g_final)


DEPTH_2 = 2


RET_HEADS = 4
RET_DK = 64
RET_DV = 64
RET_CHUNK = 128

SWA_Q_HEADS = 6
SWA_KV_HEADS = 2
SWA_WINDOW = 128
SWA_BLOCK = 128

MLA_HEADS = 6
MLA_Q_RANK = 384
MLA_KV_RANK = 256
MLA_NOPE = 64
MLA_ROPE = 32
MLA_V = 64
MLA_BLOCK = 128

RET_W = RET_HEADS * RET_DV
SWA_W = SWA_Q_HEADS * HEAD_DIM
MLA_W = MLA_HEADS * MLA_V
D_MIX = RET_W + SWA_W + MLA_W

IN_SIZES = (
    RET_HEADS * RET_DK,
    RET_HEADS * RET_DK,
    RET_W,
    RET_W,
    SWA_Q_HEADS * HEAD_DIM,
    SWA_KV_HEADS * HEAD_DIM,
    SWA_KV_HEADS * HEAD_DIM,
    MLA_Q_RANK,
    MLA_KV_RANK,
    MLA_ROPE,
)
IN_COLS = sum(IN_SIZES)

N_EXPERTS = 16
N_GROUPS = 4
EXPERTS_PER_GROUP = N_EXPERTS // N_GROUPS
TOP_K = 2
D_EXPERT = 256

DEEPNORM_ALPHA = (2 * DEPTH_2) ** 0.25
DEEPNORM_BETA = (8 * DEPTH_2) ** -0.25
LN_EPS = 1e-5
RMS_EPS = 1e-6
NEG_INF = -1e30


def _split_points():
    return [int(s) for s in np.cumsum(np.array(IN_SIZES))[:-1]]

def layer_norm(x, g, b):
    xf = x.astype(jnp.float32)
    mu = jnp.mean(xf, -1, keepdims=True)
    var = jnp.mean(jnp.square(xf - mu), -1, keepdims=True)
    return ((xf - mu) * lax.rsqrt(var + LN_EPS) * g + b).astype(x.dtype)

def rms_norm(x, g):
    xf = x.astype(jnp.float32)
    return (xf * lax.rsqrt(jnp.mean(xf * xf, -1, keepdims=True) + RMS_EPS) * g).astype(x.dtype)

def rope(x, pos):
    d = x.shape[-1]
    inv = ROPE_THETA ** (-jnp.arange(0, d, 2, dtype=jnp.float32) / d)
    ang = pos.astype(jnp.float32)[:, None] * inv[None, :]
    cos = jnp.cos(ang)[:, None, :]
    sin = jnp.sin(ang)[:, None, :]
    x1, x2 = x[..., : d // 2], x[..., d // 2:]
    return jnp.concatenate([x1 * cos - x2 * sin, x1 * sin + x2 * cos], -1).astype(x.dtype)

def retention(q, k, v, g, gn_w):
    B, S, H, dk = q.shape
    dv = RET_DV
    C = RET_CHUNK
    NC = S // C
    gamma = 1.0 - 2.0 ** (-5.0 - jnp.arange(H, dtype=jnp.float32))
    log_g = jnp.log(gamma)
    idx = jnp.arange(C, dtype=jnp.float32)
    rel = idx[:, None] - idx[None, :]
    decay_in = jnp.where(rel[None] >= 0,
                         jnp.exp(jnp.maximum(rel, 0.0)[None] * log_g[:, None, None]), 0.0)
    xi = jnp.exp((idx[None, :] + 1.0) * log_g[:, None]).T
    zeta = jnp.exp((C - 1.0 - idx[None, :]) * log_g[:, None]).T
    chunk_decay = jnp.exp(C * log_g)

    qc = q.reshape(B, NC, C, H, dk).astype(jnp.float32)
    kc = (k * (dk ** -0.5)).reshape(B, NC, C, H, dk).astype(jnp.float32)
    vc = v.reshape(B, NC, C, H, dv).astype(jnp.float32)

    scores = jnp.einsum('bnihd,bnjhd->bnhij', qc, kc) * decay_in[None, None]
    inner = jnp.einsum('bnhij,bnjhe->bnihe', scores, vc)

    upd = jnp.einsum('bnjhd,bnjhe->bnhde', kc * zeta[None, None, :, :, None], vc)

    def step(state, u):
        return chunk_decay[None, :, None, None] * state + u, state

    init = jnp.zeros((B, H, dk, dv), jnp.float32)
    _, prev_states = lax.scan(step, init, jnp.moveaxis(upd, 1, 0))
    prev_states = jnp.moveaxis(prev_states, 0, 1)
    cross = jnp.einsum('bnihd,bnhde->bnihe', qc * xi[None, None, :, :, None], prev_states)

    o = (inner + cross).reshape(B, S, H, dv)
    mu = jnp.mean(o, -1, keepdims=True)
    var = jnp.mean(jnp.square(o - mu), -1, keepdims=True)
    o = (o - mu) * lax.rsqrt(var + LN_EPS) * gn_w.astype(jnp.float32).reshape(H, dv)
    o = o.reshape(B, S, H * dv) * jax.nn.silu(g.astype(jnp.float32))
    return o.astype(q.dtype)

def sliding_window_sink_attention(q, k, v, sinks):
    B, S, Hq, d = q.shape
    Hkv = k.shape[2]
    G = Hq // Hkv
    L = SWA_BLOCK
    NB = S // L
    qb = q.reshape(B, NB, L, Hkv, G, d)
    kb = k.reshape(B, NB, L, Hkv, d)
    vb = v.reshape(B, NB, L, Hkv, d)
    pad = ((0, 0), (1, 0), (0, 0), (0, 0), (0, 0))
    kwin = jnp.concatenate([jnp.pad(kb, pad)[:, :NB], kb], axis=2)
    vwin = jnp.concatenate([jnp.pad(vb, pad)[:, :NB], vb], axis=2)

    s = jnp.einsum('bnihgd,bnjhd->bnhgij', qb, kwin).astype(jnp.float32) * (d ** -0.5)
    i = jnp.arange(L)[:, None]
    j = jnp.arange(2 * L)[None, :]
    band = (j <= i + L) & (j > i + L - SWA_WINDOW)
    blk = jnp.arange(NB)[:, None]
    valid = (blk > 0) | (jnp.arange(2 * L)[None, :] >= L)
    mask = band[None] & valid[:, None, :]
    s = jnp.where(mask[None, :, None, None], s, NEG_INF)

    sink = sinks.astype(jnp.float32).reshape(1, 1, Hkv, G, 1, 1)
    m = jnp.maximum(jnp.max(s, -1, keepdims=True), sink)
    p = jnp.exp(s - m)
    denom = jnp.sum(p, -1, keepdims=True) + jnp.exp(sink - m)
    o = jnp.einsum('bnhgij,bnjhd->bnihgd', (p / denom).astype(v.dtype), vwin)
    return o.reshape(B, S, Hq * d)

def latent_attention(c_q, c_kv, k_rope, q_norm_w, kv_norm_w, w_uq, w_ukv, pos):
    B, S, _ = c_q.shape
    H = MLA_HEADS
    dq = MLA_NOPE + MLA_ROPE
    q = (rms_norm(c_q, q_norm_w) @ w_uq).reshape(B, S, H, dq)
    q = jnp.concatenate([q[..., :MLA_NOPE], rope(q[..., MLA_NOPE:], pos)], -1)
    kv = (rms_norm(c_kv, kv_norm_w) @ w_ukv).reshape(B, S, H, MLA_NOPE + MLA_V)
    k_nope, v = kv[..., :MLA_NOPE], kv[..., MLA_NOPE:]
    k_pe = rope(k_rope[:, :, None, :], pos)
    k = jnp.concatenate([k_nope, jnp.broadcast_to(k_pe, (B, S, H, MLA_ROPE))], -1)
    scale = dq ** -0.5
    L = MLA_BLOCK
    NB = S // L
    qb = jnp.moveaxis(q.reshape(B, NB, L, H, dq), 1, 0)
    kpos = jnp.arange(S)

    def block(args):
        q_blk, n = args
        s = jnp.einsum('bihd,bjhd->bhij', q_blk, k).astype(jnp.float32) * scale
        qpos = n * L + jnp.arange(L)
        s = jnp.where(kpos[None, :] <= qpos[:, None], s, NEG_INF)
        p = jax.nn.softmax(s, axis=-1)
        return jnp.einsum('bhij,bjhe->bihe', p.astype(v.dtype), v)

    o = lax.map(block, (qb, jnp.arange(NB)))
    return jnp.moveaxis(o, 0, 1).reshape(B, S, H * MLA_V)

def grouped_moe(x, router_w, router_bias, w_gate_up, w_down):
    B, S, D = x.shape
    t = x.reshape(-1, D)
    T = t.shape[0]
    scores = jax.nn.sigmoid((t @ router_w).astype(jnp.float32))
    biased = scores + router_bias.astype(jnp.float32)
    grp = biased.reshape(T, N_GROUPS, EXPERTS_PER_GROUP)
    grp_score = jnp.sum(lax.top_k(grp, TOP_K)[0], -1)
    sel_group = jnp.argmax(grp_score, -1)
    in_group = jnp.repeat(jax.nn.one_hot(sel_group, N_GROUPS) > 0, EXPERTS_PER_GROUP, axis=-1)
    _, top_idx = lax.top_k(jnp.where(in_group, biased, -jnp.inf), TOP_K)
    sel = jnp.take_along_axis(scores, top_idx, -1)
    weights = sel / jnp.sum(sel, -1, keepdims=True)
    gates = jnp.sum(jax.nn.one_hot(top_idx, N_EXPERTS, dtype=jnp.float32) * weights[..., None], 1)
    h = jnp.einsum('td,edf->tef', t, w_gate_up)
    a = jax.nn.silu(h[..., :D_EXPERT]) * h[..., D_EXPERT:] * gates[..., None].astype(h.dtype)
    y = jnp.einsum('tef,efd->td', a, w_down)
    return y.reshape(B, S, D)

def second_inputs(seed: int = 0) -> dict:
    key = jax.random.key(seed)
    ks = jax.random.split(key, 20)
    f32 = jnp.float32
    nrm = lambda k, shape, s: jax.random.normal(k, shape, f32) * s
    return {
        "x": nrm(ks[0], (BATCH, SEQ, D_MODEL), 1.0),
        "w_in": nrm(ks[1], (DEPTH_2, D_MODEL, IN_COLS), D_MODEL ** -0.5),
        "ret_gn_w": 1.0 + nrm(ks[2], (DEPTH_2, RET_W), 0.02),
        "swa_sinks": nrm(ks[3], (DEPTH_2, SWA_Q_HEADS), 0.5),
        "mla_q_norm_w": 1.0 + nrm(ks[4], (DEPTH_2, MLA_Q_RANK), 0.02),
        "mla_kv_norm_w": 1.0 + nrm(ks[5], (DEPTH_2, MLA_KV_RANK), 0.02),
        "mla_w_uq": nrm(ks[6], (DEPTH_2, MLA_Q_RANK, MLA_HEADS * (MLA_NOPE + MLA_ROPE)), MLA_Q_RANK ** -0.5),
        "mla_w_ukv": nrm(ks[7], (DEPTH_2, MLA_KV_RANK, MLA_HEADS * (MLA_NOPE + MLA_V)), MLA_KV_RANK ** -0.5),
        "w_out": nrm(ks[8], (DEPTH_2, D_MIX, D_MODEL), DEEPNORM_BETA * D_MIX ** -0.5),
        "ln1_g": 1.0 + nrm(ks[9], (DEPTH_2, D_MODEL), 0.02),
        "ln1_b": nrm(ks[10], (DEPTH_2, D_MODEL), 0.02),
        "router_w": nrm(ks[11], (D_MODEL, N_EXPERTS), D_MODEL ** -0.5),
        "router_bias": nrm(ks[12], (N_EXPERTS,), 0.01),
        "exp_w_gate_up": nrm(ks[13], (DEPTH_2, N_EXPERTS, D_MODEL, 2 * D_EXPERT), D_MODEL ** -0.5),
        "exp_w_down": nrm(ks[14], (DEPTH_2, N_EXPERTS, D_EXPERT, D_MODEL), DEEPNORM_BETA * D_EXPERT ** -0.5),
        "ln2_g": 1.0 + nrm(ks[15], (DEPTH_2, D_MODEL), 0.02),
        "ln2_b": nrm(ks[16], (DEPTH_2, D_MODEL), 0.02),
    }

def second_block(x, w_in, ret_gn_w, swa_sinks, mla_q_norm_w, mla_kv_norm_w, mla_w_uq, mla_w_ukv,
              w_out, ln1_g, ln1_b, router_w, router_bias, exp_w_gate_up, exp_w_down, ln2_g, ln2_b):
    B, S, _ = x.shape
    pos = jnp.arange(S)
    splits = _split_points()
    for l in range(DEPTH_2):
        (r_q, r_k, r_v, r_g, s_q, s_k, s_v, c_q, c_kv, k_rope) = jnp.split(x @ w_in[l], splits, axis=-1)
        rq = rope(r_q.reshape(B, S, RET_HEADS, RET_DK), pos)
        rk = rope(r_k.reshape(B, S, RET_HEADS, RET_DK), pos)
        ret_o = retention(rq, rk, r_v, r_g, ret_gn_w[l])
        swa_o = sliding_window_sink_attention(
            s_q.reshape(B, S, SWA_Q_HEADS, HEAD_DIM),
            s_k.reshape(B, S, SWA_KV_HEADS, HEAD_DIM),
            s_v.reshape(B, S, SWA_KV_HEADS, HEAD_DIM),
            swa_sinks[l])
        mla_o = latent_attention(c_q, c_kv, k_rope, mla_q_norm_w[l], mla_kv_norm_w[l],
                                 mla_w_uq[l], mla_w_ukv[l], pos)
        mix = jnp.concatenate([ret_o, swa_o, mla_o], axis=-1) @ w_out[l]
        x = layer_norm(DEEPNORM_ALPHA * x + mix, ln1_g[l], ln1_b[l])
        ffn = grouped_moe(x, router_w, router_bias, exp_w_gate_up[l], exp_w_down[l])
        x = layer_norm(DEEPNORM_ALPHA * x + ffn, ln2_g[l], ln2_b[l])
    return x


def setup_inputs(seed=0):
    out = dict(first_inputs(seed))
    for name, value in second_inputs(seed + 1).items():
        if name != "x":
            out[name + "_2"] = value
    return out


def reference(
    x, c, positions, w_ada, b_ada, g_norm_ffn1, w_ffn1_in, w_ffn1_out, g_norm_mix, w_in, w_pool,
    pool_scale, w_pool_branch, w_attn_branch, w_out, g_norm_ffn2, w_ffn2_in, w_ffn2_out,
    g_final, w_in_2, ret_gn_w_2, swa_sinks_2, mla_q_norm_w_2, mla_kv_norm_w_2, mla_w_uq_2,
    mla_w_ukv_2, w_out_2, ln1_g_2, ln1_b_2, router_w_2, router_bias_2, exp_w_gate_up_2,
    exp_w_down_2, ln2_g_2, ln2_b_2,
):
    x = first_block(
        x, c, positions, w_ada, b_ada, g_norm_ffn1, w_ffn1_in, w_ffn1_out, g_norm_mix, w_in,
        w_pool, pool_scale, w_pool_branch, w_attn_branch, w_out, g_norm_ffn2, w_ffn2_in,
        w_ffn2_out, g_final,
    )
    return second_block(
        x, w_in_2, ret_gn_w_2, swa_sinks_2, mla_q_norm_w_2, mla_kv_norm_w_2, mla_w_uq_2,
        mla_w_ukv_2, w_out_2, ln1_g_2, ln1_b_2, router_w_2, router_bias_2, exp_w_gate_up_2,
        exp_w_down_2, ln2_g_2, ln2_b_2,
    )


_drawn_inputs = setup_inputs


def setup_inputs(seed=0):
    import zlib

    import numpy as np

    out = dict(_drawn_inputs(seed))
    spreads = {}
    factors = {'ret_gn_w_2': 3.292, 'swa_sinks_2': 5.008, 'mla_q_norm_w_2': 2.952, 'mla_kv_norm_w_2': 8.0}
    for name, (base, spread) in spreads.items():
        noise = np.random.default_rng([zlib.crc32(name.encode()), seed]).standard_normal(out[name].shape)
        drawn = base * np.exp(spread * noise) if base else spread * noise
        out[name] = __import__('jax').numpy.asarray(drawn.astype(out[name].dtype))
    for name, factor in factors.items():
        out[name] = (out[name] * factor).astype(out[name].dtype)
    return out
```

```python
from contextlib import ExitStack

import numpy as np

import concourse.bass as bass
from concourse import mybir

F32 = mybir.dt.float32
F16 = mybir.dt.float16
I32 = mybir.dt.int32
ALU = mybir.AluOpType
ACT = mybir.ActivationFunctionType
AX = mybir.AxisListType

P = 128
D = 1024
T = 256
KT = D // P
TT = T // P
F = 2816
UNIT = 2048
RING = 6
AHEAD = 3
SW, SX = 64.0, 8.0
S = SW * SX
LAYERS = 2
EXPERTS = 16
HALF = 512

RMS_EPS = 1e-6
LN_EPS = 1e-5
ALPHA = float(np.float32((2 * LAYERS) ** 0.25))

FFN_CHUNKS = F // 256
U_FFN1 = 0
U_MIX = U_FFN1 + 3 * FFN_CHUNKS
N_MIX = 30
U_FFN2 = U_MIX + N_MIX
U_L = U_FFN2 + 3 * FFN_CHUNKS
N_LMIX = 18
N_L = N_LMIX + 3 * EXPERTS
U_END = U_L + LAYERS * N_L

ADA_BLOCK = 768
ADA_BLOCKS = 9 * D // ADA_BLOCK
ADA_FIRST = 3

V_C, V_G1, V_G2, V_G3, V_GF = 0, 8, 16, 24, 32
V_LN1G, V_LN1B, V_LN2G, V_LN2B = 40, 56, 72, 88
V_QN, V_KVN, V_PS, V_N = 104, 110, 114, 116

C_IDENT, C_ROT, C_ROTM, C_ONES, C_INVF, C_EPS, C_EPSLN, C_PRIO16, C_PRIO4 = 0, 128, 256, 384, 512, 513, 514, 516, 532
C_SMALL = 536
NEG = -1e30

TWO_PI = 2 * np.pi
PI_1 = 6.28125
PI_2 = float(np.float32(np.round((TWO_PI - PI_1) * 2 ** 20) / 2 ** 20))
PI_3 = float(np.float32(TWO_PI - PI_1 - PI_2))
ROUND = 1.5 * 2 ** 23


def constants():
    small = np.zeros((P, C_SMALL), np.float32)
    small[:, C_IDENT:C_IDENT + P] = np.eye(P)
    for b in (0, 64):
        for i in range(32):
            small[b + 32 + i, C_ROT + b + i] = -1.0
            small[b + i, C_ROT + b + 32 + i] = 1.0
    for i in range(16):
        small[80 + i, C_ROTM + 64 + i] = -1.0
        small[64 + i, C_ROTM + 80 + i] = 1.0
    small[:, C_ONES:C_ONES + P] = 1.0
    inv64 = (np.float32(10000.0) ** (-np.arange(0, 64, 2, dtype=np.float32) / np.float32(64))).astype(np.float32)
    inv32 = (np.float32(10000.0) ** (-np.arange(0, 32, 2, dtype=np.float32) / np.float32(32))).astype(np.float32)
    small[:, C_INVF] = np.tile(inv64, 4)
    small[:, C_EPS] = RMS_EPS
    small[:, C_EPSLN] = LN_EPS
    small[:, C_EPSLN + 1] = LN_EPS * S * S
    small[:, C_PRIO16:C_PRIO16 + 16] = 16 - np.arange(16)
    small[:, C_PRIO4:C_PRIO4 + 4] = 4 - np.arange(4)

    t = np.arange(T)

    def by_queries(ok):
        m = np.where(ok, 0.0, NEG).astype(np.float32)
        return np.concatenate([m[:P, :P], m[P:, :]], 1)

    rel = t[:, None] - t[None, :]
    masks1 = np.concatenate([by_queries((rel >= 0) & (rel <= 128)),
                             by_queries((rel >= 0) & (rel % 4 == 0)),
                             by_queries((rel >= 0) & (rel % 16 == 0))], 1)
    count = np.zeros((P, 2, T), np.float32)
    for g, w in enumerate((2, 4, 8, 16)):
        count[64 * (g % 2):64 * (g % 2) + 64, g // 2] = 1.0 / np.minimum(t + 1, w)
    block1 = np.concatenate([masks1, count.reshape(P, 2 * T)], 1)

    ang64 = (t[None, :].astype(np.float32) * np.tile(inv64, 4)[:, None]).astype(np.float32)
    cosr, sinr = np.cos(ang64), np.sin(ang64)
    ang32 = (t[None, :].astype(np.float32) * np.tile(inv32, 2)[:, None]).astype(np.float32)
    cosm, sinm = np.ones((P, T), np.float32), np.zeros((P, T), np.float32)
    cosm[64:96], sinm[64:96] = np.cos(ang32), np.sin(ang32)
    decay = np.zeros((4, P, 384), np.float32)
    for h in range(4):
        log_g = np.log(1.0 - 2.0 ** (-5.0 - h))
        m = np.where(rel.T >= 0, np.exp(np.maximum(rel.T, 0) * log_g), 0.0) * 64 ** -0.5
        decay[h] = np.concatenate([m[:P, :], m[P:, P:]], 1)
    block2 = np.concatenate([cosr, sinr, cosm, sinm,
                             by_queries((rel >= 0) & (rel < 128)), by_queries(rel >= 0),
                             decay.transpose(1, 0, 2).reshape(P, 4 * 384)], 1)
    return small, block1.astype(np.float32), block2.astype(np.float32)


class Unit:

    def __init__(self, c, turn=0):
        self.c, self.turn = c, turn

    def __add__(self, k):
        return Unit(self.c + k, self.turn)

    @property
    def slot(self):
        return self.c % RING

    def count(self, k=0):
        return self.turn * RING + (self.c + k + RING)

    def loads(self):
        return self.turn * 16 + 16 * (self.c // RING + 1)


def build(nc, a, out):
    small_d, b1_d, b2_d = a["const_small"], a["const_block1"], a["const_block2"]
    with ExitStack() as ctx:
        def sb(name, shape, dt=F32):
            return ctx.enter_context(nc.sbuf_tensor(name, shape, dt))

        def sem(name):
            return ctx.enter_context(nc.semaphore(name))

        raw = sb("raw", [P, RING, UNIT])
        whi = sb("whi", [P, RING, UNIT], F16)
        wlo = sb("wlo", [P, RING, UNIT], F16)
        x = sb("x", [P, TT, D])
        uhi = sb("uhi", [P, KT, T], F16)
        ulo = sb("ulo", [P, KT, T], F16)
        gt = sb("gt", [P, 3, D])
        small = sb("small", [P, C_SMALL])
        vec = sb("vec", [P, V_N])
        vec8 = sb("vec8", [P, V_N])
        adacols = sb("adacols", [P, 48])
        acol = sb("acol", [P, 3, 8])
        zero8 = sb("zero8", [P, 8])
        cond = sb("cond", [P, 8])
        cosb = sb("cosb", [P, T])
        sinb = sb("sinb", [P, T])
        sinks = sb("sinks", [P, 12])
        zeros16 = sb("zeros16", [P, HALF], F16)
        stat = sb("stat", [P, 64])
        bnst_t = sb("bnst", [P, 12])
        bnst = bnst_t[:, :]
        rbias = sb("rbias", [P, 16])
        flag = sb("flag", [P, 8])
        xn = sb("xn", [P, TT, D])
        hreg = sb("hreg", [P, 2048])
        area = sb("area", [P, 15360])
        ps = ctx.enter_context(nc.psum_tensor("ps", [P, 8, HALF], F32))

        ident = small[:, C_IDENT:C_IDENT + P]
        rot = small[:, C_ROT:C_ROT + P]
        ones = small[:, C_ONES:C_ONES + P]

        s_act = hreg[:, 0:512]
        h_f32 = hreg[:, 512:1024]
        hhi = hreg[:, 1024:1536].bitcast(F16).rearrange("p (b n) -> p b n", b=2)
        hlo = hreg[:, 1536:2048].bitcast(F16).rearrange("p (b n) -> p b n", b=2)

        def region(base):
            at = [0]

            def take(n, shape=None, dt=F32):
                v = base[:, at[0]:at[0] + n]
                at[0] += n
                assert at[0] <= base.shape[1], at[0]
                if dt is not F32:
                    v = v.bitcast(dt)
                return v
            return take

        tk = region(area)
        acc = tk(9 * D)
        aring = tk(4 * 2 * ADA_BLOCK).rearrange("p (s k n) -> p s k n", s=4, k=2)
        tk = region(area)
        masks1 = tk(3 * 384).rearrange("p (g n) -> p g n", g=3)
        ptmp = tk(2048).rearrange("p (s n) -> p s n", s=4)
        q1 = tk(1536).rearrange("p (k n) -> p k n", k=6)
        k1 = tk(1536).rearrange("p (k n) -> p k n", k=6)
        rt1 = tk(2048)
        v1 = tk(1536).rearrange("p (t n) -> p t n", t=2)
        sb1 = [tk(1152).rearrange("p (g n) -> p g n", g=3) for _ in range(2)]
        pt1 = [rt1[:, 0:1152].rearrange("p (g n) -> p g n", g=3)]
        mhi = tk(1024, dt=F16).rearrange("p (k n) -> p k n", k=8)
        mlo = tk(1024, dt=F16).rearrange("p (k n) -> p k n", k=8)
        qraw1 = [rt1[:, 512 * i:512 * i + 512] for i in range(2)]
        rtmp1 = [rt1[:, 1024 + 512 * i:1536 + 512 * i] for i in range(2)]
        gtmp = [sb1[0].rearrange("p g n -> p (g n)")[:, 0:512], sb1[0].rearrange("p g n -> p (g n)")[:, 512:1024],
                sb1[1].rearrange("p g n -> p (g n)")[:, 0:512], sb1[1].rearrange("p g n -> p (g n)")[:, 512:1024]]
        yhi = hreg[:, 0:512].bitcast(F16).rearrange("p (k n) -> p k n", k=4)
        ylo = hreg[:, 512:1024].bitcast(F16).rearrange("p (k n) -> p k n", k=4)
        pT = hreg[:, 1024:1536].rearrange("p (k n) -> p k n", k=2)
        rcount = hreg[:, 1536:2048].rearrange("p (k n) -> p k n", k=2)
        wpool = gt[:, 0, 0:128].rearrange("p (k n) -> p k n", k=2)
        tk = region(area)
        tables = tk(1024).rearrange("p (k n) -> p k n", k=4)
        masks2 = tk(768).rearrange("p (k n) -> p k n", k=2)
        decay = tk(1536).rearrange("p (k n) -> p k n", k=4)
        b2const = area[:, 0:3328]
        rqk = tk(1024).rearrange("p (k n) -> p k n", k=4)
        rv = tk(512).rearrange("p (t n) -> p t n", t=2)
        rg = tk(512).rearrange("p (t n) -> p t n", t=2)
        sq = tk(768).rearrange("p (k n) -> p k n", k=3)
        sk = tk(512).rearrange("p (k n) -> p k n", k=2)
        sv = cosb[:, :].rearrange("p (t n) -> p t n", t=2)
        cT_flat = tk(2304)
        cT = cT_flat[:, 0:1280].rearrange("p (k n) -> p k n", k=5)
        rstdb = cT_flat[:, 1280:1792].rearrange("p (k n) -> p k n", k=2)
        sb2 = [cT_flat[:, 384 * i:384 * i + 384].rearrange("p (g n) -> p g n", g=1) for i in range(2)]
        pt2 = [cT_flat[:, 768 + 384 * i:1152 + 384 * i].rearrange("p (g n) -> p g n", g=1) for i in range(2)]
        dret = [cT_flat[:, 1536 + 384 * i:1920 + 384 * i] for i in range(2)]
        chi = tk(640, dt=F16).rearrange("p (k n) -> p k n", k=5)
        clo = tk(640, dt=F16).rearrange("p (k n) -> p k n", k=5)
        qm = tk(1536).rearrange("p (k n) -> p k n", k=6)
        km = tk(1536).rearrange("p (k n) -> p k n", k=6)
        rt2 = tk(2048)
        qraw2 = [rt2[:, 512 * i:512 * i + 512] for i in range(2)]
        rtmp2 = [rt2[:, 1024 + 512 * i:1536 + 512 * i] for i in range(2)]
        oret = rt2[:, 0:512]
        ocen = rt2[:, 512:1024]
        osq = rt2[:, 1024:1536]
        vm = gt[:, 2, 256:1024].rearrange("p (t n) -> p t n", t=2)
        gnw = gt[:, 2, 0:256]
        kro = xn[:, 0, 0:256]
        sqv = hreg[:, 0:1280].rearrange("p (k n) -> p k n", k=5)
        mixhi = hreg[:, 0:1024].bitcast(F16).rearrange("p (k n) -> p k n", k=8)
        mixlo = hreg[:, 1024:2048].bitcast(F16).rearrange("p (k n) -> p k n", k=8)
        gb = area[:, 3328:3328 + 4096].rearrange("p (e n) -> p e n", e=EXPERTS)
        rr = area[:, 3328 + 4096:3328 + 4096 + 640].rearrange("p (s n) -> p s n", s=20)
        gatesT = area[:, 8192:8192 + T]
        lng, lnb = gt[:, 0, :], gt[:, 1, :]
        vstack = xn[:, 0, 0:P]
        posi = xn[:, 0, 128:384].bitcast(I32)
        posf = xn[:, 0, 384:640]
        tr = [xn[:, 1, 256 * i:256 * i + 256] for i in range(4)]

        raw_in = [sem(f"raw_in{i}") for i in range(RING)]
        hi_made, lo_made, used = sem("hi_made"), sem("lo_made"), sem("used")
        const_in, x_in, stack_in, pos_in, sinks_in = (sem(n) for n in ("const_in", "x_in", "stack_in", "pos_in", "sinks_in"))
        acc_zero, acc_row, ada_sum = sem("acc_zero"), sem("acc_row"), sem("ada_sum")
        ada_in = [sem(f"ada_in{i}") for i in range(4)]
        vec_t, cond_made, vec_out, pos_f, pos_bc, ang_made, sin_made = (
            sem(n) for n in ("vec_t", "cond_made", "vec_out", "pos_f", "pos_bc", "ang_made", "sin_made"))
        mod_mm, mod_cols, gt_out = sem("mod_mm"), sem("mod_cols"), sem("gt_out")
        x_new, rms_made, var_made, xn_made, xt_made, u_hi, u_lo = (
            sem(n) for n in ("x_new", "rms_made", "var_made", "xn_made", "xt_made", "u_hi", "u_lo"))
        silu_made, h_made, h_hi, h_lo, y_done = (sem(n) for n in ("silu_made", "h_made", "h_hi", "h_lo", "y_done"))
        dve_step, act_step, pool_step = sem("dve_step"), sem("act_step"), sem("pool_step")
        b1_in, wpool_in, pool_d, pool_mm, pool_hi, pool_lo = (
            sem(n) for n in ("b1_in", "wpool_in", "pool_d", "pool_mm", "pool_hi", "pool_lo"))
        proj_out, rot_mm, rope_out = sem("proj_out"), sem("rot_mm"), sem("rope_out")
        sc_mm, sc_in, max_made, exp_made, p_made, tr_mm, tr_out, pv_mm, yo_hi, yo_lo = (
            sem(n) for n in ("sc_mm", "sc_in", "max_made", "exp_made", "p_made", "tr_mm", "tr_out", "pv_mm", "yo_hi", "yo_lo"))
        sig_made, m_made, m_hi, m_lo = sem("sig_made"), sem("m_made"), sem("m_hi"), sem("m_lo")
        b2_in, ln_in, x_upd, zero_made = sem("b2_in"), sem("ln_in"), sem("x_upd"), sem("zero_made")
        swap_mm, swap_out, gn_in = sem("swap_mm"), sem("swap_out"), sem("gn_in")
        sqr_made, ss_mm, std_made, cn_made, c_hi, c_lo, km_rope = (
            sem(n) for n in ("sqr_made", "ss_mm", "std_made", "cn_made", "c_hi", "c_lo", "km_rope"))
        ret_mm, ret_d, ret_o, ret_std, ret_y, ret_t, ret_hi, ret_lo, ret_oc, ret_var = (
            sem(n) for n in ("ret_mm", "ret_d", "ret_o", "ret_std", "ret_y", "ret_t", "ret_hi", "ret_lo", "ret_oc", "ret_var"))
        rt_mm, rt_sig, gate_made, gate_t, gateT_out, gb_mm, gb_out = (
            sem(n) for n in ("rt_mm", "rt_sig", "gate_made", "gate_t", "gateT_out", "gb_mm", "gb_out"))
        out_done, m_moe, bias_in = sem("out_done"), sem("m_moe"), sem("bias_in")
        u_f = sem("u_f")

        def ktiles(w):
            return w.rearrange("(k p) n -> p k n", p=P)

        w_in, w_in2 = ktiles(a["w_in"][0]), [ktiles(a["w_in_2"][l]) for l in range(LAYERS)]

        def mix1_units():
            cols = [w_in[:, :, 256 * i:256 * i + 256] for i in range(10)]
            for j in range(4):
                c = slice(256 * j, 256 * j + 256)
                cols += [ktiles(a["w_pool_branch"][0])[:, :, c], ktiles(a["w_attn_branch"][0])[:, :, c],
                         w_in[:, :, 2560 + 256 * j:2816 + 256 * j], w_in[:, :, 3584 + 256 * j:3840 + 256 * j]]
            return cols + [ktiles(a["w_out"][0])[:, 2 * j:2 * j + 2, :] for j in range(4)]

        def mix2_units(l):
            edges = [0, 256, 512, 768, 1024, 1280, 1536, 1664, 1920, 2048, 2304, 2336]
            cols = [w_in2[l][:, :, lo:hi] for lo, hi in zip(edges, edges[1:])]
            cols += [ktiles(a["mla_w_uq_2"][l]), ktiles(a["mla_w_ukv_2"][l])]
            cols += [ktiles(a["w_out_2"][l])[:, 2 * j:2 * j + 2, :] for j in range(4)]
            return cols + [ktiles(a["router_w_2"])]

        sources = {}
        for i, s_ in enumerate(mix1_units()):
            sources[U_MIX + i] = s_
        for l in range(LAYERS):
            for i, s_ in enumerate(mix2_units(l)):
                sources[U_L + N_L * l + i] = s_
        sizes = {u: s_.shape[1] * s_.shape[2] for u, s_ in sources.items()}

        def size(u):
            return sizes.get(u.c, UNIT) if isinstance(u.turn, int) and u.turn == 0 else UNIT

        def hi_part(act, u):
            if isinstance(u.turn, int) and u.c + RING * u.turn >= U_END:
                return
            n = size(u)
            act.wait_ge(raw_in[u.slot], u.loads())
            act.wait_ge(used, u.count(1 - RING))
            act.activation(whi[:, u.slot, 0:n], raw[:, u.slot, 0:n], ACT.Copy, scale=SW).then_inc(hi_made, 1)

        def lo_part(dve, u):
            if isinstance(u.turn, int) and u.c + RING * u.turn >= U_END:
                return
            n = size(u)
            dve.wait_ge(hi_made, u.count(1))
            dve.scalar_tensor_tensor(out=wlo[:, u.slot, 0:n], in0=raw[:, u.slot, 0:n], scalar=SW,
                                     in1=whi[:, u.slot, 0:n], op0=ALU.mult, op1=ALU.subtract).then_inc(lo_made, 1)

        def ffn_src(w_i, w_o):
            wi, wo = ktiles(w_i), w_o.rearrange("(c k p) n -> p c k n", p=P, k=2)

            def src(kind, c):
                if kind == "o":
                    return wo[:, c, :, :] if isinstance(c, int) else wo[:, bass.ds(c, 1), :, :].rearrange("p a k n -> p (a k) n")
                off = 0 if kind == "a" else F
                return wi[:, :, bass.ds(c * 256 + off, 256)]
            return src

        def moe_src(l):
            wi = a["exp_w_gate_up_2"][l].rearrange("e (k p) n -> p e k n", p=P)
            wo = a["exp_w_down_2"][l].rearrange("e (k p) n -> p e k n", p=P)

            def src(kind, c):
                w = wo if kind == "o" else wi
                v = w[:, c, :, :] if isinstance(c, int) else w[:, bass.ds(c, 1), :, :].rearrange("p a k n -> p (a k) n")
                return v if kind == "o" else v[:, :, 0:256] if kind == "a" else v[:, :, 256:512]
            return src

        class Phase:

            def __init__(self, u0, g0, n, src, ada=False, moe=False):
                self.u0, self.g0, self.n, self.src, self.ada, self.moe = u0, g0, n, src, ada, moe

        ffn1 = Phase(U_FFN1, 0, FFN_CHUNKS, ffn_src(a["w_ffn1_in"][0], a["w_ffn1_out"][0]), ada=True)
        ffn2 = Phase(U_FFN2, FFN_CHUNKS, FFN_CHUNKS, ffn_src(a["w_ffn2_in"][0], a["w_ffn2_out"][0]))
        moe = [Phase(U_L + N_L * l + N_LMIX, 2 * FFN_CHUNKS + EXPERTS * l, EXPERTS, moe_src(l), moe=True)
               for l in range(LAYERS)]

        def steps(eng, ph, body):
            n_pairs = 4 if ph.ada else (ph.n - 1) // 2
            with eng.Fori(0, n_pairs) as i:
                for j in (1, 2):
                    body(2 * i + j, Unit(ph.u0 + 3 * j - 1, i), j % 2)
            for c in range(2 * n_pairs + 1, ph.n):
                body(c, Unit(ph.u0 + 3 * c - 1), c % 2)

        block = ctx.enter_context(nc.Block())

        @block.sync
        def _(sp):
            sp.dma_start(small[:, :], small_d).then_inc(const_in, 16)
            rows = [(V_C, a["c"][0]), (V_G1, a["g_norm_ffn1"][0]), (V_G2, a["g_norm_mix"][0]),
                    (V_G3, a["g_norm_ffn2"][0]), (V_GF, a["g_final"])]
            for l in range(LAYERS):
                rows += [(V_LN1G + 8 * l, a["ln1_g_2"][l]), (V_LN1B + 8 * l, a["ln1_b_2"][l]),
                         (V_LN2G + 8 * l, a["ln2_g_2"][l]), (V_LN2B + 8 * l, a["ln2_b_2"][l]),
                         (V_QN + 3 * l, a["mla_q_norm_w_2"][l]), (V_KVN + 2 * l, a["mla_kv_norm_w_2"][l])]
            rows.append((V_PS, a["pool_scale"][0]))
            for r, v in rows:
                v = v.rearrange("(r n) -> r n", n=P)
                sp.dma_start(vstack[r:r + v.shape[0], :], v).then_inc(stack_in, 16)
            sp.dma_start(posi[0:1, :], a["positions"]).then_inc(pos_in, 16)
            for t in range(TT):
                sp.dma_start(x[:, t, :], a["x"][0, t * P:(t + 1) * P, :]).then_inc(x_in, 16)
            sp.dma_start(sinks[:, :], a["swa_sinks_2"].rearrange("l h -> (l h)").partition_broadcast(P)).then_inc(sinks_in, 16)

            sp.dma_start(rbias[:, :], a["router_bias_2"].partition_broadcast(P)).then_inc(bias_in, 16)

            def load(u, src):
                if isinstance(u.turn, int) and u.c + RING * u.turn >= U_END:
                    return
                sp.wait_ge(lo_made, u.count(1 - RING))
                k, n = src.shape[1], src.shape[2]
                sp.dma_start(raw[:, u.slot, 0:k * n].rearrange("p (k n) -> p k n", k=k), src).then_inc(raw_in[u.slot], 16)

            def phase(ph):
                load(Unit(ph.u0), ph.src("a", 0))
                load(Unit(ph.u0 + 1), ph.src("b", 0))

                def step(c, u, par):
                    load(u, ph.src("a", c))
                    load(u + 1, ph.src("b", c))
                    load(u + 2, ph.src("o", c - 1))
                steps(sp, ph, step)
                load(Unit(ph.u0 + 3 * ph.n - 1), ph.src("o", ph.n - 1))

            phase(ffn1)
            for i in range(N_MIX):
                load(Unit(U_MIX + i), sources[U_MIX + i])
            phase(ffn2)
            for l in range(LAYERS):
                for i in range(N_LMIX):
                    load(Unit(U_L + N_L * l + i), sources[U_L + N_L * l + i])
                phase(moe[l])
            for t in range(TT):
                sp.wait_ge(x_new, 6 + t + 1)
                sp.dma_start(out[0, t * P:(t + 1) * P, :], x[:, t, :]).then_inc(out_done, 16)
            sp.wait_ge(out_done, 32)

        @block.gpsimd
        def _(pool):
            n_step = [0]

            def link(ins):
                n_step[0] += 1
                ins.then_inc(pool_step, 1)
                pool.wait_ge(pool_step, n_step[0])

            pool.memset(acc, 0.0).then_inc(acc_zero, 1)
            pool.wait_ge(acc_zero, 1)
            pool.dma_start(acc[0:1, :], a["b_ada"]).then_inc(acc_row, 16)
            w_ada = ktiles(a["w_ada"][0])

            def piece(b, j):
                pool.dma_start(aring[:, j, :, :], w_ada[:, 2 * j:2 * j + 2, bass.ds(b * ADA_BLOCK, ADA_BLOCK)])\
                    .then_inc(ada_in[j], 16)
            for j in range(4):
                piece(0, j)
            for b in range(1, ADA_BLOCKS):
                for j in range(4):
                    pool.wait_ge(ada_sum, 8 * (b - 1) + 2 * j + 2)
                    piece(b, j)
            pool.wait_ge(gt_out, 6)
            pool.wait_ge(mod_cols, 2)
            pool.wait_ge(h_lo, FFN_CHUNKS)
            pool.wait_ge(y_done, 2)
            pool.dma_start(area[:, 0:1152], b1_d[:, 0:1152]).then_inc(b1_in, 16)
            pool.dma_start(hreg[:, 1536:2048], b1_d[:, 1152:1664]).then_inc(b1_in, 16)
            pool.wait_ge(x_new, 2)
            for g in range(4):
                pool.dma_start(gt[64 * (g % 2):64 * (g % 2) + 64, 0, 64 * (g // 2):64 * (g // 2) + 64],
                               a["w_pool"][0, g]).then_inc(wpool_in, 16)
            pool.wait_ge(proj_out, 1)
            pool.wait_ge(b1_in, 32)
            for k in range(2):
                src = pT[:, k, :]
                lo_w = (1, 4)[k]
                w = 1
                sums = []
                while w < (4, 16)[k]:
                    dst = ptmp[:, len(sums) % 4, 0:T] if k == 0 else ptmp[:, len(sums) % 4, 0:T]
                    link(pool.tensor_copy(dst[:, 0:w], src[:, 0:w]))
                    link(pool.tensor_tensor(dst[:, w:T], src[:, w:T], src[:, 0:T - w], ALU.add))
                    sums.append(dst)
                    src, w = dst, 2 * w
                d = ptmp[:, k, 256:512]
                for half, s_ in ((0, sums[-2]), (1, sums[-1])):
                    r = slice(64 * half, 64 * half + 64)
                    link(pool.tensor_tensor(d[r, :], s_[r, :], rcount[r, k, :], ALU.mult))
                    link(pool.tensor_tensor(d[r, :], d[r, :], pT[r, k, :], ALU.subtract))
            pool.memset(flag[:, 4:5], 0.0).then_inc(pool_d, 1)
            pool.wait_ge(y_done, 4)
            pool.wait_ge(x_new, 4)
            pool.dma_start(lng, a["g_final"].partition_broadcast(P)).then_inc(ln_in, 16)
            pool.wait_ge(x_new, 6)
            pool.dma_start(b2const, b2_d).then_inc(b2_in, 16)
            pool.dma_start(gnw, a["ret_gn_w_2"][0].partition_broadcast(P)).then_inc(gn_in, 16)
            pool.wait_ge(ln_in, 16)
            for t in range(TT):
                pool.wait_ge(xn_made, 6 + t + 1)
                pool.tensor_tensor(x[:, t, :], xn[:, t, :], lng, ALU.mult).then_inc(x_upd, 1)
            for n in range(4, 7):
                l, second = (n - 4) // 2, (n - 4) % 2
                g, b = ("ln2_g_2", "ln2_b_2") if second else ("ln1_g_2", "ln1_b_2")
                pool.wait_ge(x_upd, 2 * (n - 3))
                pool.dma_start(lng, a[g][l].partition_broadcast(P)).then_inc(ln_in, 16)
                pool.dma_start(lnb, a[b][l].partition_broadcast(P)).then_inc(ln_in, 16)
                if n == 5:
                    pool.wait_ge(ret_y, 1)
                    pool.dma_start(gnw, a["ret_gn_w_2"][1].partition_broadcast(P)).then_inc(gn_in, 16)
                pool.wait_ge(ln_in, 16 + 32 * (n - 3))
                for t in range(TT):
                    pool.wait_ge(xn_made, 2 * n + t + 1)
                    link(pool.tensor_tensor(x[:, t, :], xn[:, t, :], lng, ALU.mult))
                    pool.tensor_tensor(x[:, t, :], x[:, t, :], lnb, ALU.add).then_inc(x_upd, 1)
            pool.wait_ge(x_upd, 8)
            pool.dma_start(lng, a["ln2_g_2"][1].partition_broadcast(P)).then_inc(ln_in, 16)
            pool.dma_start(lnb, a["ln2_b_2"][1].partition_broadcast(P)).then_inc(ln_in, 16)
            pool.wait_ge(ln_in, 16 + 32 * 4)

        def attention_units(blk, l=0):
            units = []
            if blk == 1:
                for h in range(4):
                    groups = []
                    for g in range(3):
                        hh = 4 * g + h
                        r = slice(64 * (hh % 2), 64 * (hh % 2) + 64)
                        groups.append((q1[r, hh // 2, :], k1[r, hh // 2, :],
                                       [v1[:, t, 64 * hh:64 * hh + 64] for t in range(2)], masks1[:, g, :]))
                    units.append((groups, 0.125, None, (h // 2, 64 * (h % 2))))
                return units
            for h in range(6):
                r = slice(64 * (h % 2), 64 * (h % 2) + 64)
                kv = h // 3
                kk = sk[r, 0 if kv == h % 2 else 1, :]
                units.append(([(sq[r, h // 2, :], kk, [sv[:, t, 64 * kv:64 * kv + 64] for t in range(2)], masks2[:, 0, :])],
                              0.125, 6 * l + h, (2 + h // 2, 64 * (h % 2))))
            for h in range(6):
                units.append(([(qm[0:96, h, :], km[0:96, h, :], [vm[:, t, 64 * h:64 * h + 64] for t in range(2)],
                                masks2[:, 1, :])], float(96 ** -0.5), None, (5 + h // 2, 64 * (h % 2))))
            return units

        SPLIT = (slice(0, 128), slice(128, 384))

        def bases(blk, l):
            return (0, 0) if blk == 1 else (4 + 12 * l, 12 + 12 * l)

        @block.tensor
        def _(pe):
            def split_mm(o, wh, wl, xh, xl, start, stop, weights_first=True):
                prods = ((wh, xh), (wh, xl), (wl, xh)) if weights_first else ((xh, wh), (xh, wl), (xl, wh))
                for i, (st, mv) in enumerate(prods):
                    last = pe.matmul(o, st, mv, start=start and i == 0, stop=stop and i == 2, skip_group_check=True)
                return last

            def stage1(u, ph_banks):
                for side in range(2):
                    pe.wait_ge(lo_made, (u + side).count(1))
                    s_ = (u + side).slot
                    for ft in range(2):
                        for k in range(KT):
                            w = slice(k * 256 + ft * P, k * 256 + ft * P + P)
                            last = split_mm(ps[:, ph_banks + side, ft * T:(ft + 1) * T], whi[:, s_, w], wlo[:, s_, w],
                                            uhi[:, k, :], ulo[:, k, :], k == 0, k == KT - 1)
                    last.then_inc(used, 1)

            def down(u, th, tl, stop=False, done=None):
                s_ = u.slot
                for t in range(TT):
                    for n in range(2):
                        for f in range(2):
                            w = slice(f * D + n * HALF, f * D + (n + 1) * HALF)
                            last = split_mm(ps[:, 2 * t + n, :], whi[:, s_, w], wlo[:, s_, w],
                                            th[f][:, t * P:(t + 1) * P], tl[f][:, t * P:(t + 1) * P],
                                            False, stop and f == 1, weights_first=False)
                    if done is not None and t == 0:
                        last.then_inc(y_done, 1)
                if done is not None:
                    last.then_inc(y_done, 1)
                else:
                    last.then_inc(used, 1)

            def hT(par):
                return ([hhi[:, par, f * T:(f + 1) * T] for f in range(2)], [hlo[:, par, f * T:(f + 1) * T] for f in range(2)])

            def open_y():
                for b in range(4):
                    pe.matmul(ps[:, b, :], zeros16[0:1, 0:P], zeros16[0:1, :], start=True, stop=False, skip_group_check=True)

            def phase(ph, between=None, before_last=None):
                open_y()
                stage1(Unit(ph.u0), 4)
                if between is not None:
                    between()

                def step(c, u, par):
                    g = ph.g0 + c
                    pe.wait_ge(h_made, g)
                    stage1(u, 4 + 2 * par)
                    pe.wait_ge(h_lo, g)
                    pe.wait_ge(lo_made, (u + 2).count(1))
                    down(u + 2, *hT(1 - par))
                steps(pe, ph, step)
                if before_last is not None:
                    before_last()
                u = Unit(ph.u0 + 3 * ph.n - 1)
                pe.wait_ge(h_lo, ph.g0 + ph.n)
                pe.wait_ge(lo_made, u.count(1))
                down(u, *hT((ph.n - 1) % 2), stop=True, done=True)
                pe.matmul(ps[0:32, 4, 0:1], zeros16[0:1, 0:32], zeros16[0:1, 0:1], start=True, stop=True,
                          skip_group_check=True).then_inc(used, 1)

            def transposes(n):
                for t in range(TT):
                    pe.wait_ge(xn_made, 2 * n + t + 1)
                    for k in range(KT):
                        last = pe.transpose(ps[:, 4 + k // 2, (k % 2) * T + t * P:(k % 2) * T + (t + 1) * P],
                                            xn[:, t, k * P:(k + 1) * P], ident)
                        if t == TT - 1 and k % 2 == 1:
                            last.then_inc(xt_made, 1)

            def proj(u, bank, ft_cols, kt, xh, xl, w_cols, out_rows=None, done=True):
                s_ = u.slot
                for i, (c0, wd) in enumerate(ft_cols):
                    for k in range(kt):
                        w = slice(k * w_cols + c0, k * w_cols + c0 + wd)
                        r = out_rows or slice(0, wd)
                        last = split_mm(ps[r, bank, i * T:(i + 1) * T], whi[:, s_, w], wlo[:, s_, w],
                                        xh[:, k, :], xl[:, k, :], k == 0, k == kt - 1)
                if done:
                    last.then_inc(used, 1)
                return last

            def proj_tokens(u, bank, n, kt=KT):
                s_ = u.slot
                for t in range(TT):
                    for k in range(kt):
                        w = slice(k * n, (k + 1) * n)
                        last = split_mm(ps[:, bank, t * n:(t + 1) * n], whi[:, s_, w], wlo[:, s_, w],
                                        uhi[:, k, t * P:(t + 1) * P], ulo[:, k, t * P:(t + 1) * P],
                                        k == 0, k == kt - 1, weights_first=False)
                last.then_inc(used, 1)

            def attention(blk, l=0):
                units = attention_units(blk, l)
                h0, b0 = bases(blk, l)
                g_n = len(units[0][0])
                bufs, late = (pt1, 1) if blk == 1 else (pt2, 2)
                for j in range(len(units) + late):
                    if j < len(units):
                        groups = units[j][0]
                        for g, (q, k, v, m) in enumerate(groups):
                            n = j * g_n + g
                            if n >= 3:
                                pe.wait_ge(sc_in, b0 + n - 2)
                            pe.matmul(ps[:, n % 3, 0:128], q[:, 0:128], k[:, 0:128], start=True, stop=True)
                            pe.matmul(ps[:, n % 3, 128:384], q[:, 128:256], k, start=True, stop=True).then_inc(sc_mm, 1)
                    i = j - 1
                    if 0 <= i < len(units):
                        pe.wait_ge(p_made, h0 + i + 1)
                        for g in range(g_n):
                            n = i * g_n + g
                            if n >= 3:
                                pe.wait_ge(tr_out, b0 + n - 2)
                            src = (sb1 if blk == 1 else sb2)[i % 2][:, g, :]
                            for c in range(3):
                                last = pe.transpose(ps[:, 3 + n % 3, c * P:(c + 1) * P], src[:, c * P:(c + 1) * P], ident)
                            last.then_inc(tr_mm, 1)
                    i = j - late
                    if 0 <= i < len(units):
                        groups, _, _, (tile, r0) = units[i]
                        pe.wait_ge(tr_out, b0 + (i + 1) * g_n)
                        if i >= 2:
                            pe.wait_ge(yo_lo, h0 + i - 1)
                        o = ps[r0:r0 + 64, 6 + i % 2, :]
                        pt = bufs[i % len(bufs)]
                        for g in range(g_n):
                            last = pe.matmul(o[:, 0:P], groups[g][2][0], pt[:, g, 0:P], start=g == 0, stop=g == g_n - 1)
                        for g in range(g_n):
                            pe.matmul(o[:, P:T], groups[g][2][0], pt[:, g, P:2 * P], start=g == 0, stop=False)
                            last = pe.matmul(o[:, P:T], groups[g][2][1], pt[:, g, 2 * P:3 * P], start=False, stop=g == g_n - 1)
                        last.then_inc(pv_mm, 1)

            pe.wait_ge(const_in, 16)
            pe.wait_ge(stack_in, 16 * 18)
            pe.transpose(ps[:, 0, 0:V_N], vstack[0:V_N, :], small[0:V_N, C_IDENT:C_IDENT + V_N]).then_inc(vec_t, 1)
            pe.wait_ge(pos_f, 1)
            pe.matmul(ps[:, 1, 0:T], ones[0:1, :], posf[0:1, :], start=True, stop=True).then_inc(pos_bc, 1)
            pe.wait_ge(ada_sum, 8 * ADA_FIRST)
            for j in range(16):
                last = pe.matmul(ps[:, 2, j:j + 1], acc[:, j * P:(j + 1) * P], ones[:, 0:1], start=True, stop=True)
            last.then_inc(mod_mm, 1)

            def gt_rows(m, half, bank):
                c0 = m * D + half * HALF
                pe.matmul(ps[:, bank, :], ones, acc[:, c0:c0 + HALF], start=True, stop=True).then_inc(mod_mm, 1)

            def mods_before_last():
                pe.wait_ge(ada_sum, 8 * ADA_BLOCKS)
                gt_rows(2, 0, 6)
                gt_rows(2, 1, 7)

            pe.wait_ge(zero_made, 1)
            transposes(0)
            pe.wait_ge(u_lo, 4)
            phase(ffn1, before_last=mods_before_last)
            for j, m in enumerate((3, 4, 6, 7)):
                for c in range(8):
                    last = pe.matmul(ps[:, 4, 8 * j + c:8 * j + c + 1], acc[:, m * D + c * P:m * D + (c + 1) * P],
                                     ones[:, 0:1], start=True, stop=True)
            last.then_inc(mod_mm, 1)
            gt_rows(5, 0, 5)
            pe.wait_ge(gt_out, 1)
            gt_rows(5, 1, 6)
            pe.wait_ge(gt_out, 2)
            gt_rows(8, 0, 7)
            pe.wait_ge(mod_cols, 2)
            gt_rows(8, 1, 4)
            pe.wait_ge(gt_out, 6)
            transposes(1)

            pe.wait_ge(u_lo, 8)
            two = [(0, P), (P, P)]

            def rot1(r):
                pe.wait_ge(proj_out, 1 + r + 1)
                if r >= 2:
                    pe.wait_ge(rope_out, r - 1)
                pe.matmul(ps[:, 4 + r % 2, :], rot, qraw1[r % 2], start=True, stop=True).then_inc(rot_mm, 1)

            for i in range(10):
                u = Unit(U_MIX + i)
                pe.wait_ge(lo_made, u.count(1))
                if i >= 4:
                    pe.wait_ge(proj_out, i - 3)
                if i < 7:
                    proj(u, i % 4, two, KT, uhi, ulo, 256)
                else:
                    proj_tokens(u, i % 4, 256)
                if 2 <= i < 8:
                    rot1(i - 2)
            pe.wait_ge(pool_d, 1)
            pe.wait_ge(wpool_in, 64)
            for k in range(2):
                for half in range(2):
                    r = slice(64 * half, 64 * half + 64)
                    last = pe.matmul(ps[r, 6, k * T:(k + 1) * T], wpool[r, k, :], ptmp[r, k, 256:512], start=True, stop=True)
            last.then_inc(pool_mm, 1)
            pe.wait_ge(proj_out, 10)
            pe.wait_ge(rope_out, 6)
            pe.wait_ge(pool_lo, 1)
            attention(1)
            pe.wait_ge(yo_lo, 4)
            for j in range(4):
                b0 = 4 * (j % 2)
                if j >= 2:
                    pe.wait_ge(m_made, j - 1)
                for i in range(4):
                    u = Unit(U_MIX + 10 + 4 * j + i)
                    pe.wait_ge(lo_made, u.count(1))
                    if i < 2:
                        proj(u, b0 + i, two, 2, yhi[:, 2 * i:2 * i + 2, :], ylo[:, 2 * i:2 * i + 2, :], 256)
                    else:
                        proj(u, b0 + i, two, KT, uhi, ulo, 256)
            pe.wait_ge(m_made, 4)
            open_y()

            def out_proj(u0, th, tl):
                for j in range(4):
                    u = Unit(u0 + j)
                    pe.wait_ge(lo_made, u.count(1))
                    down(u, [th[:, 2 * j + f, :] for f in range(2)], [tl[:, 2 * j + f, :] for f in range(2)],
                         stop=j == 3, done=True if j == 3 else None)
                pe.matmul(ps[0:32, 4, 0:1], zeros16[0:1, 0:32], zeros16[0:1, 0:1], start=True, stop=True,
                          skip_group_check=True).then_inc(used, 1)
            pe.wait_ge(m_lo, 4)
            out_proj(U_MIX + 26, mhi, mlo)
            transposes(2)
            pe.wait_ge(u_lo, 12)
            phase(ffn2)
            transposes(3)

            for l in range(LAYERS):
                ul, pb, rb = U_L + N_L * l, 10 + 19 * l, 6 + 6 * l
                pe.wait_ge(u_lo, 16 + 8 * l)

                def free(i):
                    if i >= 4:
                        pe.wait_ge(proj_out, pb + i - 3)

                def rot2(r, i, rows, mat):
                    pe.wait_ge(proj_out, pb + i + 1)
                    if r >= 2:
                        pe.wait_ge(rope_out, rb + r - 1)
                    n = T if rows.start else HALF
                    pe.matmul(ps[rows, 4 + r % 2, 0:n], mat, qraw2[r % 2][rows, 0:n], start=True, stop=True)\
                        .then_inc(rot_mm, 1)

                for i in range(11):
                    u = Unit(ul + i)
                    pe.wait_ge(lo_made, u.count(1))
                    free(i)
                    if i in (0, 1, 4, 5, 7, 9):
                        proj(u, i % 4, two, KT, uhi, ulo, 256)
                    elif i in (2, 3):
                        proj_tokens(u, i % 4, 256)
                    elif i == 6:
                        proj_tokens(u, i % 4, 128)
                    elif i == 8:
                        proj(u, i % 4, [(0, P)], KT, uhi, ulo, 128)
                    else:
                        proj(u, i % 4, [(0, 32)], KT, uhi, ulo, 32, out_rows=slice(64, 96))
                    if i in (1, 2):
                        rot2(i - 1, i - 1, slice(0, P), rot)
                    if i == 7:
                        pe.wait_ge(proj_out, pb + 6)
                        pe.matmul(ps[0:64, 6, 0:T], ident[:, 64:128], sk[:, 0, :], start=True, stop=True)
                        pe.matmul(ps[64:128, 6, 0:T], ident[:, 0:64], sk[:, 0, :], start=True, stop=True).then_inc(swap_mm, 1)
                rot2(2, 10, slice(64, 96), small[64:96, C_ROTM + 64:C_ROTM + 96])
                pe.wait_ge(sqr_made, 2 * l + 2)
                pe.wait_ge(swap_out, l + 1)
                for b, ks in ((6, range(0, 3)), (7, range(3, 5))):
                    for k in ks:
                        last = pe.matmul(ps[:, b, 0:T], ones, sqv[:, k, :], start=k == ks[0], stop=k == ks[-1])
                last.then_inc(ss_mm, 1)
                pe.wait_ge(c_lo, 2 * (l + 1))
                u = Unit(ul + 11)
                pe.wait_ge(lo_made, u.count(1))
                for j in range(3):
                    free(11 + j)
                    proj(u, (11 + j) % 4, [(96 * (2 * j + i), 96) for i in range(2)], 3, chi[:, 0:3, :], clo[:, 0:3, :],
                         576, done=False)
                    pe.matmul(ps[0:32, 7, HALF - 1:HALF], zeros16[0:1, 0:32], zeros16[0:1, 0:1], start=True, stop=True,
                              skip_group_check=True).then_inc(rt_mm, 1)
                    if j >= 1:
                        rot2(2 + j, 10 + j, slice(0, 96), small[0:96, C_ROTM:C_ROTM + 96])
                pe.matmul(ps[0:32, 7, HALF - 1:HALF], zeros16[0:1, 0:32], zeros16[0:1, 0:1], start=True, stop=True,
                          skip_group_check=True).then_inc(used, 1)
                rot2(5, 13, slice(0, 96), small[0:96, C_ROTM:C_ROTM + 96])
                u = Unit(ul + 12)
                pe.wait_ge(lo_made, u.count(1))
                for j in range(3):
                    free(14 + j)
                    proj(u, (14 + j) % 4, [(128 * (2 * j + i), 64) for i in range(2)], 2, chi[:, 3:5, :], clo[:, 3:5, :],
                         768, done=False).then_inc(rt_mm, 1)
                for t in range(TT):
                    free(17 + t)
                    for k in range(2):
                        wv = [w[:, u.slot, k * 768:(k + 1) * 768].rearrange("p (h n) -> p h n", h=6)[:, :, 64:128]
                              for w in (whi, wlo)]
                        last = split_mm(ps[:, (17 + t) % 4, 0:384], wv[0], wv[1], chi[:, 3 + k, t * P:(t + 1) * P],
                                        clo[:, 3 + k, t * P:(t + 1) * P], k == 0, k == 1, weights_first=False)
                    last.then_inc(rt_mm, 1)
                pe.matmul(ps[0:32, 7, HALF - 1:HALF], zeros16[0:1, 0:32], zeros16[0:1, 0:1], start=True, stop=True,
                          skip_group_check=True).then_inc(used, 1)
                pe.wait_ge(proj_out, pb + 19)
                pe.wait_ge(rope_out, rb + 6)

                def ret_scores(h):
                    r = slice(64 * (h % 2), 64 * (h % 2) + 64)
                    if h >= 3:
                        pe.wait_ge(ret_d, 4 * l + h - 2)
                    q, k = rqk[r, h // 2, :], rqk[r, 2 + h // 2, :]
                    pe.matmul(ps[:, h % 3, 0:T], k[:, 0:P], q, start=True, stop=True)
                    pe.matmul(ps[:, h % 3, T:384], k[:, P:T], q[:, P:T], start=True, stop=True).then_inc(ret_mm, 1)
                ret_scores(0)
                for h in range(4):
                    if h < 3:
                        ret_scores(h + 1)
                    pe.wait_ge(ret_d, 4 * l + h + 1)
                    d, c = dret[h % 2], slice(64 * h, 64 * h + 64)
                    pe.matmul(ps[:, 6, 64 * h:64 * h + 64], d[:, 0:P], rv[:, 0, c], start=True, stop=True)
                    pe.matmul(ps[:, 6, T + 64 * h:T + 64 * h + 64], d[:, P:T], rv[:, 0, c], start=True, stop=False)
                    pe.matmul(ps[:, 6, T + 64 * h:T + 64 * h + 64], d[:, T:384], rv[:, 1, c], start=False, stop=True)\
                        .then_inc(ret_o, 1)
                pe.wait_ge(ret_y, l + 1)
                for t in range(TT):
                    for f in range(2):
                        last = pe.transpose(ps[:, 7, f * T + t * P:f * T + (t + 1) * P],
                                            oret[:, t * T + f * P:t * T + (f + 1) * P], ident)
                last.then_inc(ret_t, 1)
                pe.wait_ge(ret_lo, l + 1)
                attention(2, l)
                pe.wait_ge(yo_lo, 4 + 12 * (l + 1))
                open_y()
                out_proj(ul + 13, mixhi, mixlo)
                transposes(4 + 2 * l)

                pe.wait_ge(u_lo, 20 + 8 * l)
                u = Unit(ul + 17)
                pe.wait_ge(lo_made, u.count(1))
                for t in range(TT):
                    for k in range(KT):
                        w = slice(16 * k, 16 * k + 16)
                        last = split_mm(ps[:, 7, 16 * t:16 * t + 16], whi[:, u.slot, w], wlo[:, u.slot, w],
                                        uhi[:, k, t * P:(t + 1) * P], ulo[:, k, t * P:(t + 1) * P],
                                        k == 0, k == KT - 1, weights_first=False)
                last.then_inc(used, 1)

                def gates():
                    pe.wait_ge(gate_made, l + 1)
                    for t in range(TT):
                        last = pe.transpose(ps[0:16, 6, t * P:(t + 1) * P], rr[:, 19, 16 * t:16 * t + 16], ident)
                    last.then_inc(gate_t, 1)
                    pe.wait_ge(gateT_out, l + 1)
                    for e in range(0, EXPERTS, 2):
                        b = 6 + (e // 2) % 2
                        if e >= 4:
                            pe.wait_ge(gb_out, 8 * l + e // 2 - 1)
                        for i in range(2):
                            sel = small[0:16, C_IDENT + e + i:C_IDENT + e + i + 1].to_broadcast([16, P])
                            last = pe.matmul(ps[:, b, i * T:(i + 1) * T], sel, gatesT[0:16, :], start=True, stop=True)
                        last.then_inc(gb_mm, 1)
                    pe.wait_ge(gb_out, 8 * l + 8)
                phase(moe[l], between=gates)
                if l < LAYERS - 1:
                    transposes(5 + 2 * l)

        @block.scalar
        def _(act):
            n_step = [0]

            def link(ins):
                n_step[0] += 1
                ins.then_inc(act_step, 1)
                act.wait_ge(act_step, n_step[0])

            def ahead(u, n=1):
                for i in range(n):
                    hi_part(act, u + (AHEAD + i))

            def rms(n):
                for t in range(TT):
                    act.wait_ge(*((x_in, 32) if n == 0 else (x_new, 2 * (n - 1) + t + 1)))
                    link(act.activation(xn[:, t, :], x[:, t, :], ACT.Square, accum_out=stat[:, t:t + 1]))
                    act.activation(stat[:, 2 + t:3 + t], stat[:, t:t + 1], ACT.Sqrt, scale=1.0 / D,
                                   bias=small[:, C_EPS:C_EPS + 1]).then_inc(rms_made, 1)

            def layer_std(n):
                for t in range(TT):
                    act.wait_ge(var_made, 2 * (n - 4) + t + 1)
                    act.activation(stat[:, 2 + t:3 + t], stat[:, 9 + 4 * t:10 + 4 * t], ACT.Sqrt, scale=1.0,
                                   bias=small[:, C_EPSLN + 1:C_EPSLN + 2]).then_inc(rms_made, 1)

            def norm_out(n, acols, bcols):
                for kp in range(4):
                    act.wait_ge(xt_made, 4 * n + kp + 1)
                    if kp >= 2:
                        act.wait_ge(u_lo, 4 * n + kp - 1)
                    for i in range(2):
                        k = 2 * kp + i
                        last = act.activation(hreg[:, 512 * (kp % 2) + i * T:512 * (kp % 2) + (i + 1) * T],
                                              ps[:, 4 + kp, i * T:(i + 1) * T], ACT.Identity,
                                              scale=acols[:, k:k + 1], bias=bcols[:, k:k + 1])
                    last.then_inc(u_f, 1)

            def chunk(u_b, g, par):
                act.wait_ge(used, u_b.count(1))
                act.activation(s_act, ps[:, 4 + 2 * par, :], ACT.Silu, scale=1.0 / S).then_inc(silu_made, 1)
                act.wait_ge(h_made, g + 2)
                act.activation(hhi[:, par, :], h_f32, ACT.Copy).then_inc(h_hi, 1)

            def phase(ph, between=None):
                ahead(Unit(ph.u0), 2)
                chunk(Unit(ph.u0 + 1), ph.g0, 0) if between is None else between()

                def step(c, u, par):
                    ahead(u, 3)
                    chunk(u + 1, ph.g0 + c, par)
                steps(act, ph, step)
                ahead(Unit(ph.u0 + 3 * ph.n - 1))

            def attention(blk, l=0, extra=None):
                units = attention_units(blk, l)
                h0, b0 = bases(blk, l)
                g_n = len(units[0][0])
                scores, bufs = (sb1, pt1) if blk == 1 else (sb2, pt2)
                yh = yhi if blk == 1 else mixhi
                late = 1 if blk == 1 else 2
                for j in range(len(units) + late + 1):
                    if j < len(units):
                        act.wait_ge(max_made, h0 + j + 1)
                        st = stat[:, 20 + 10 * (j % 2):30 + 10 * (j % 2)]
                        for t in range(2):
                            s_ = scores[j % 2][:, :, SPLIT[t]]
                            last = act.activation(s_, s_, ACT.Exp, bias=st[:, 2 + t:3 + t], accum_out=st[:, 4 + t:5 + t])
                        if units[j][2] is not None:
                            for t in range(2):
                                last = act.activation(st[:, 6 + t:7 + t], sinks[:, units[j][2]:units[j][2] + 1], ACT.Exp,
                                                      bias=st[:, 2 + t:3 + t])
                        last.then_inc(exp_made, 1)
                    i = j - 1
                    if 0 <= i < len(units):
                        if i >= len(bufs):
                            act.wait_ge(pv_mm, h0 + i - len(bufs) + 1)
                        for g in range(g_n):
                            n = i * g_n + g
                            act.wait_ge(tr_mm, b0 + n + 1)
                            act.activation(bufs[i % len(bufs)][:, g, :], ps[:, 3 + n % 3, 0:384], ACT.Copy).then_inc(tr_out, 1)
                    i = j - late
                    if 0 <= i < len(units):
                        tile, r0 = units[i][3]
                        act.wait_ge(pv_mm, h0 + i + 1)
                        if blk == 1:
                            tile += 2
                        act.activation(yh[r0:r0 + 64, tile, :], ps[r0:r0 + 64, 6 + i % 2, 0:T], ACT.Copy, scale=SX)\
                            .then_inc(yo_hi, 1)

            for i in range(AHEAD):
                hi_part(act, Unit(i))
            act.wait_ge(vec_out, 1)
            act.activation(cond[:, :], vec[:, V_C:V_C + 8], ACT.Silu).then_inc(cond_made, 1)
            act.wait_ge(ang_made, 1)
            act.activation(sinb[:, :], tr[0], ACT.Sin)
            act.activation(cosb[:, :], tr[1], ACT.Sin).then_inc(sin_made, 1)
            act.wait_ge(sin_made, 1)
            rms(0)
            act.wait_ge(mod_cols, 1)
            norm_out(0, acol[:, 0, :], adacols[:, 0:8])
            phase(ffn1)
            for i, (m, half) in enumerate(((0, 0), (0, 1), (1, 0), (1, 1), (2, 0), (2, 1))):
                act.wait_ge(mod_mm, (2, 3, 5, 6, 7, 8)[i])
                act.activation(gt[:, m, half * HALF:(half + 1) * HALF], ps[:, (6, 7, 5, 6, 7, 4)[i], :], ACT.Copy,
                               scale=(0.5, 1.0, 0.5)[m] / S).then_inc(gt_out, 1)
            rms(1)
            act.wait_ge(mod_cols, 2)
            norm_out(1, acol[:, 1, :], adacols[:, 8:16])

            for i in range(10):
                u = Unit(U_MIX + i)
                ahead(u)
                act.wait_ge(used, u.count(1))
                dst, shape = None, None
                if i == 0:
                    act.wait_ge(h_lo, FFN_CHUNKS)
                    dst = pT.rearrange("p k n -> p (k n)")
                elif i < 7:
                    r = i - 1
                    if r >= 2:
                        act.wait_ge(rope_out, r - 1)
                    dst = qraw1[r % 2]
                if dst is not None:
                    act.activation(dst, ps[:, i % 4, :], ACT.Copy, scale=1.0 / S).then_inc(proj_out, 1)
                else:
                    c = 256 * (i - 7)
                    act.activation(v1[:, :, c:c + 256], ps[:, i % 4, :].rearrange("p (t n) -> p t n", t=2), ACT.Copy,
                                   scale=1.0 / S).then_inc(proj_out, 1)
            act.wait_ge(pool_mm, 1)
            for k in range(2):
                last = act.activation(yhi[:, k, :], ps[:, 6, k * T:(k + 1) * T], ACT.Copy, scale=vec8[:, V_PS + k:V_PS + k + 1])
            last.then_inc(pool_hi, 1)
            attention(1)
            for j in range(4):
                for i in range(4):
                    ahead(Unit(U_MIX + 10 + 4 * j + i))
                act.wait_ge(used, Unit(U_MIX + 10 + 4 * j + 3).count(1))
                if j:
                    act.wait_ge(m_made, j)
                b0 = 4 * (j % 2)
                for i in range(2):
                    act.activation(gtmp[i], ps[:, b0 + 2 + i, :], ACT.Sigmoid, scale=1.0 / S).then_inc(sig_made, 1)
                act.wait_ge(m_made, j + 1)
                act.activation(mhi[:, 2 * j:2 * j + 2, :], gtmp[2].rearrange("p (k n) -> p k n", k=2), ACT.Copy).then_inc(m_hi, 1)
            for j in range(4):
                ahead(Unit(U_MIX + 26 + j))
            rms(2)
            norm_out(2, acol[:, 2, :], adacols[:, 16:24])
            phase(ffn2)
            rms(3)
            norm_out(3, vec8[:, V_GF:V_GF + 8], zero8[:, :])

            for l in range(LAYERS):
                ul, pb, rb = U_L + N_L * l, 10 + 19 * l, 6 + 6 * l
                if l:
                    norm_out(5, vec8[:, V_LN2G:V_LN2G + 8], vec8[:, V_LN2B:V_LN2B + 8])

                def leave(i, dst, src, func=ACT.Copy):
                    act.activation(dst, src, func, scale=1.0 / S).then_inc(proj_out, 1)

                for i in range(11):
                    u = Unit(ul + i)
                    ahead(u)
                    act.wait_ge(used, u.count(1))
                    b = ps[:, i % 4, :]
                    if i < 2:
                        leave(i, qraw2[i % 2], b)
                    elif i < 4:
                        leave(i, (rv, rg)[i - 2], b.rearrange("p (t n) -> p t n", t=2), (ACT.Copy, ACT.Silu)[i - 2])
                    elif i == 4:
                        leave(i, sq[:, 0:2, :], b.rearrange("p (t n) -> p t n", t=2))
                    elif i == 5:
                        act.activation(sq[:, 2, :], b[:, 0:T], ACT.Copy, scale=1.0 / S)
                        leave(i, sk[:, 0, :], b[:, T:2 * T])
                    elif i == 6:
                        leave(i, sv, b[:, 0:256].rearrange("p (t n) -> p t n", t=2))
                    elif i == 7:
                        leave(i, cT[:, 0:2, :], b.rearrange("p (t n) -> p t n", t=2))
                        act.wait_ge(swap_mm, l + 1)
                        act.activation(sk[:, 1, :], ps[:, 6, 0:T], ACT.Copy).then_inc(swap_out, 1)
                    elif i == 8:
                        leave(i, cT[:, 2, :], b[:, 0:T])
                        act.wait_ge(proj_out, pb + 9)
                        act.activation(sqv[:, 0:3, :], cT[:, 0:3, :], ACT.Square).then_inc(sqr_made, 1)
                    elif i == 9:
                        leave(i, cT[:, 3:5, :], b.rearrange("p (t n) -> p t n", t=2))
                        act.wait_ge(proj_out, pb + 10)
                        act.activation(sqv[:, 3:5, :], cT[:, 3:5, :], ACT.Square).then_inc(sqr_made, 1)
                    else:
                        act.wait_ge(rope_out, rb + 1)
                        leave(i, qraw2[0][64:96, 0:T], b[64:96, 0:T])
                act.wait_ge(ss_mm, l + 1)
                for i, n in enumerate((384, 256)):
                    act.activation(rstdb[:, i, :], ps[:, 6 + i, 0:T], ACT.Sqrt, scale=1.0 / n,
                                   bias=small[:, C_EPS:C_EPS + 1]).then_inc(std_made, 1)
                for i, ks in enumerate((slice(0, 3), slice(3, 5))):
                    act.wait_ge(cn_made, 2 * l + i + 1)
                    act.activation(chi[:, ks, :], cT[:, ks, :], ACT.Copy).then_inc(c_hi, 1)
                act.wait_ge(rope_out, rb + 3)
                act.activation(km[64:96, :, :], kro[64:96, :].unsqueeze(1).to_broadcast([32, 6, T]), ACT.Copy).then_inc(km_rope, 1)
                ahead(Unit(ul + 11))
                for j in range(3):
                    act.wait_ge(rt_mm, 8 * l + j + 1)
                    act.wait_ge(rope_out, rb + 2 + j)
                    leave(11 + j, qraw2[(3 + j) % 2][0:96, :], ps[0:96, (11 + j) % 4, :])
                ahead(Unit(ul + 12))
                for j in range(3):
                    act.wait_ge(rt_mm, 8 * l + 4 + j)
                    leave(14 + j, km[0:64, 2 * j:2 * j + 2, :], ps[0:64, (14 + j) % 4, :].rearrange("p (k n) -> p k n", k=2))
                for t in range(TT):
                    act.wait_ge(rt_mm, 8 * l + 7 + t)
                    leave(17 + t, vm[:, t, :], ps[:, (17 + t) % 4, 0:384])
                act.wait_ge(ret_oc, l + 1)
                act.activation(osq, ocen, ACT.Square).then_inc(ret_std, 1)
                act.wait_ge(ret_var, l + 1)
                act.activation(stat[:, 48:56], stat[:, 40:48], ACT.Sqrt, scale=1.0 / 64,
                               bias=small[:, C_EPSLN:C_EPSLN + 1]).then_inc(ret_std, 1)
                act.wait_ge(ret_t, l + 1)
                act.activation(mixhi[:, 0:2, :], ps[:, 7, :].rearrange("p (k n) -> p k n", k=2), ACT.Copy, scale=SX)\
                    .then_inc(ret_hi, 1)
                attention(2, l)
                for j in range(4):
                    ahead(Unit(ul + 13 + j))
                n = 4 + 2 * l
                layer_std(n)
                norm_out(n, vec8[:, V_LN1G + 8 * l:V_LN1G + 8 * l + 8], vec8[:, V_LN1B + 8 * l:V_LN1B + 8 * l + 8])
                ahead(Unit(ul + 17))
                act.wait_ge(used, Unit(ul + 17).count(1))
                act.activation(rr[:, 0, :], ps[:, 7, 0:32], ACT.Sigmoid, scale=1.0 / S).then_inc(rt_sig, 1)

                def gates():
                    act.wait_ge(gate_t, l + 1)
                    act.activation(gatesT[0:16, :], ps[0:16, 6, 0:T], ACT.Copy).then_inc(gateT_out, 1)
                    for e in range(0, EXPERTS, 2):
                        act.wait_ge(gb_mm, 8 * l + e // 2 + 1)
                        act.activation(gb[:, e:e + 2, :], ps[:, 6 + (e // 2) % 2, :].rearrange("p (k n) -> p k n", k=2),
                                       ACT.Copy).then_inc(gb_out, 1)
                    chunk(Unit(moe[l].u0 + 1), moe[l].g0, 0)
                phase(moe[l], between=gates)
                layer_std(n + 1)

        @block.vector
        def _(dve):
            n_step = [0]

            def link(ins):
                n_step[0] += 1
                ins.then_inc(dve_step, 1)
                dve.wait_ge(dve_step, n_step[0])

            def ahead(u, n=1):
                for i in range(n):
                    lo_part(dve, u + (AHEAD + i))

            def new_x(n):
                gate = gt[:, n - 1, :]
                dve.wait_ge(gt_out, 2 * n)
                for t in range(TT):
                    dve.wait_ge(y_done, 2 * (n - 1) + t + 1)
                    for hf in range(2):
                        c = slice(hf * HALF, (hf + 1) * HALF)
                        link(dve.tensor_tensor(xn[:, t, c], ps[:, 2 * t + hf, :], gate[:, c], ALU.mult))
                    dve.tensor_tensor(x[:, t, :], x[:, t, :], xn[:, t, :], ALU.add).then_inc(x_new, 1)

            def rms_xn(n):
                for t in range(TT):
                    dve.wait_ge(rms_made, 2 * n + t + 1)
                    link(dve.reciprocal(stat[:, 4 + t:5 + t], stat[:, 2 + t:3 + t]))
                    dve.tensor_scalar(xn[:, t, :], x[:, t, :], stat[:, 4 + t:5 + t], None, ALU.mult).then_inc(xn_made, 1)

            def layer_xn(n):
                for t in range(TT):
                    dve.wait_ge(y_done, 2 * (n - 1) + t + 1)
                    dve.wait_ge(x_upd, 2 * (n - 4) + t + 1)
                    for hf in range(2):
                        c = slice(hf * HALF, (hf + 1) * HALF)
                        link(dve.scalar_tensor_tensor(out=x[:, t, c], in0=x[:, t, c], scalar=S * ALPHA,
                                                      in1=ps[:, 2 * t + hf, :], op0=ALU.mult, op1=ALU.add))
                        link(dve.bn_stats(bnst[:, 6 * hf:6 * hf + 6], x[:, t, c]))
                    dve.bn_aggr(stat[:, 8 + 4 * t:10 + 4 * t], bnst).then_inc(var_made, 1)
                    dve.wait_ge(var_made, 2 * (n - 4) + t + 1)
                for t in range(TT):
                    dve.wait_ge(rms_made, 2 * n + t + 1)
                    link(dve.reciprocal(stat[:, 4 + t:5 + t], stat[:, 2 + t:3 + t]))
                    dve.tensor_scalar(xn[:, t, :], x[:, t, :], stat[:, 8 + 4 * t:9 + 4 * t], stat[:, 4 + t:5 + t],
                                      ALU.subtract, ALU.mult).then_inc(xn_made, 1)

            def norm_split(n):
                for kp in range(4):
                    dve.wait_ge(u_f, 4 * n + kp + 1)
                    uf = hreg[:, 512 * (kp % 2):512 * (kp % 2) + 512].rearrange("p (k n) -> p k n", k=2)
                    dve.tensor_copy(uhi[:, 2 * kp:2 * kp + 2, :], uf).then_inc(u_hi, 1)
                    dve.wait_ge(u_hi, 4 * n + kp + 1)
                    dve.tensor_tensor(ulo[:, 2 * kp:2 * kp + 2, :], uf, uhi[:, 2 * kp:2 * kp + 2, :], ALU.subtract)\
                        .then_inc(u_lo, 1)

            def chunk(ph, c, g, par):
                dve.wait_ge(silu_made, g + 1)
                if not (isinstance(g, int) and g == 0):
                    dve.wait_ge(h_lo, g)
                if ph.moe:
                    link_free = dve.scalar_tensor_tensor(out=h_f32, in0=ps[:, 5 + 2 * par, :], scalar=SX / S, in1=s_act,
                                                         op0=ALU.mult, op1=ALU.mult)
                    link_free.then_inc(m_moe, 1)
                    dve.wait_ge(m_moe, g - 2 * FFN_CHUNKS + 1)
                    gate = gb[:, c, :] if isinstance(c, int) else gb[:, bass.ds(c, 1), :].rearrange("p a n -> p (a n)")
                    hv = h_f32.rearrange("p (k n) -> p k n", k=2)
                    dve.tensor_tensor(hv, hv, gate.unsqueeze(1).to_broadcast([P, 2, T]), ALU.mult).then_inc(h_made, 1)
                else:
                    dve.scalar_tensor_tensor(out=h_f32, in0=ps[:, 5 + 2 * par, :], scalar=SX / S, in1=s_act,
                                             op0=ALU.mult, op1=ALU.mult).then_inc(h_made, 1)

            def chunk_lo(g, par):
                dve.wait_ge(h_hi, g + 1)
                dve.tensor_tensor(hlo[:, par, :], h_f32, hhi[:, par, :], ALU.subtract).then_inc(h_lo, 1)

            def ada_sums(b, k0, k1):
                for k in range(k0, k1):
                    if k % 2 == 0:
                        dve.wait_ge(ada_in[k // 2], 16 * b + 16)
                    if not (isinstance(b, int) and b == 0 and k == 0):
                        dve.wait_ge(ada_sum, 8 * b + k)
                    v = acc[:, bass.ds(b * ADA_BLOCK, ADA_BLOCK)]
                    dve.scalar_tensor_tensor(out=v, in0=aring[:, k // 2, k % 2, :], scalar=cond[:, k:k + 1], in1=v,
                                             op0=ALU.mult, op1=ALU.add).then_inc(ada_sum, 1)

            def phase(ph, between=None):
                ahead(Unit(ph.u0), 2)
                if between is not None:
                    between()
                chunk(ph, 0, ph.g0, 0)
                chunk_lo(ph.g0, 0)

                def step(c, u, par):
                    ahead(u, 3)
                    ada = ph.ada and not (isinstance(c, int) and c > ADA_BLOCKS - ADA_FIRST)
                    if ada:
                        ada_sums(c + (ADA_FIRST - 1), 0, 4)
                    chunk(ph, c, ph.g0 + c, par)
                    chunk_lo(ph.g0 + c, par)
                    if ada:
                        ada_sums(c + (ADA_FIRST - 1), 4, 8)
                steps(dve, ph, step)
                ahead(Unit(ph.u0 + 3 * ph.n - 1))

            def rope(r, base, rows, cos, sin, raw_pair, tmp, dst, k):
                dve.wait_ge(rot_mm, base + r + 1)
                n = k * T

                def v3(v):
                    return v[rows, 0:n].rearrange("p (k n) -> p k n", k=k)
                cb, sbc = (v[rows, :].unsqueeze(1).to_broadcast([rows.stop - rows.start, k, T]) for v in (cos, sin))
                dve.tensor_tensor(v3(tmp[0]), v3(ps[:, 4 + r % 2, :]), sbc, ALU.mult).then_inc(dve_step, 1)
                n_step[0] += 1
                link(dve.tensor_tensor(v3(tmp[1]), v3(raw_pair), cb, ALU.mult))
                dve.tensor_tensor(dst, v3(tmp[0]), v3(tmp[1]), ALU.add).then_inc(rope_out, 1)
                dve.wait_ge(rope_out, base + r + 1)

            def attention(blk, l=0):
                units = attention_units(blk, l)
                h0, b0 = bases(blk, l)
                g_n = len(units[0][0])
                scores = sb1 if blk == 1 else sb2
                yh, yl = (yhi, ylo) if blk == 1 else (mixhi, mixlo)
                late = 1 if blk == 1 else 2
                for j in range(len(units) + late + 1):
                    if j < len(units):
                        groups, scale, sink, _ = units[j]
                        st = stat[:, 20 + 10 * (j % 2):30 + 10 * (j % 2)]
                        if j >= 2:
                            dve.wait_ge(tr_mm, b0 + (j - 1) * g_n)
                        for g in range(g_n):
                            n = j * g_n + g
                            dve.wait_ge(sc_mm, b0 + n + 1)
                            dve.scalar_tensor_tensor(out=scores[j % 2][:, g, :], in0=ps[:, n % 3, 0:384], scalar=scale,
                                                     in1=groups[g][3], op0=ALU.mult, op1=ALU.add).then_inc(sc_in, 1)
                        dve.wait_ge(sc_in, b0 + (j + 1) * g_n)
                        for t in range(2):
                            ins = dve.tensor_reduce(st[:, t:t + 1], scores[j % 2][:, :, SPLIT[t]],
                                                    AX.XY if g_n > 1 else AX.X, ALU.max) if g_n > 1 else \
                                dve.tensor_reduce(st[:, t:t + 1], scores[j % 2][:, 0, SPLIT[t]], AX.X, ALU.max)
                            if t == 0:
                                ins.then_inc(dve_step, 1)
                                n_step[0] += 1
                        link(ins)
                        if sink is not None:
                            link(dve.tensor_scalar(st[:, 0:2], st[:, 0:2], sinks[:, sink:sink + 1], None, ALU.max))
                        dve.tensor_scalar(st[:, 2:4], st[:, 0:2], -1.0, None, ALU.mult).then_inc(max_made, 1)
                    i = j - 1
                    if 0 <= i < len(units):
                        st = stat[:, 20 + 10 * (i % 2):30 + 10 * (i % 2)]
                        dve.wait_ge(exp_made, h0 + i + 1)
                        if units[i][2] is not None:
                            link(dve.tensor_tensor(st[:, 4:6], st[:, 4:6], st[:, 6:8], ALU.add))
                        link(dve.reciprocal(st[:, 8:10], st[:, 4:6]))
                        for t in range(2):
                            s_ = scores[i % 2][:, :, SPLIT[t]]
                            ins = dve.tensor_scalar(s_, s_, st[:, 8 + t:9 + t], None, ALU.mult)
                            if t == 0:
                                ins.then_inc(dve_step, 1)
                                n_step[0] += 1
                        ins.then_inc(p_made, 1)
                    i = j - late
                    if 0 <= i < len(units):
                        tile, r0 = units[i][3]
                        if blk == 1:
                            tile += 2
                        dve.wait_ge(yo_hi, h0 + i + 1)
                        dve.scalar_tensor_tensor(out=yl[r0:r0 + 64, tile, :], in0=ps[r0:r0 + 64, 6 + i % 2, 0:T], scalar=SX,
                                                 in1=yh[r0:r0 + 64, tile, :], op0=ALU.mult, op1=ALU.subtract).then_inc(yo_lo, 1)

            dve.memset(zeros16[:, :], 0.0).then_inc(lo_made, RING)
            dve.memset(stat[:, 0:32], 0.0).then_inc(used, RING)
            dve.memset(stat[:, 32:64], 0.0).then_inc(h_made, 1)
            dve.memset(flag[:, 0:1], 0.0).then_inc(hi_made, RING)
            dve.memset(zero8[:, :], 0.0).then_inc(zero_made, 1)
            dve.wait_ge(pos_in, 16)
            dve.tensor_copy(posf[0:1, :], posi[0:1, :]).then_inc(pos_f, 1)
            for i in range(AHEAD):
                lo_part(dve, Unit(i))
            dve.wait_ge(vec_t, 1)
            dve.tensor_copy(vec[:, :], ps[:, 0, 0:V_N]).then_inc(vec_out, 1)
            dve.wait_ge(vec_out, 1)
            link(dve.tensor_scalar(vec8[:, :], vec[:, :], SX, None, ALU.mult))
            dve.wait_ge(pos_bc, 1)
            link(dve.tensor_scalar(tr[0], ps[:, 1, 0:T], small[:, C_INVF:C_INVF + 1], None, ALU.mult))
            link(dve.tensor_scalar(tr[1], tr[0], float(1 / TWO_PI), ROUND, ALU.mult, ALU.add))
            link(dve.tensor_scalar(tr[1], tr[1], -ROUND, None, ALU.add))
            for part in (PI_1, PI_2, PI_3):
                link(dve.scalar_tensor_tensor(out=tr[0], in0=tr[1], scalar=-part, in1=tr[0], op0=ALU.mult, op1=ALU.add))
            link(dve.tensor_scalar(tr[1], tr[0], float(np.pi / 2), None, ALU.add))
            link(dve.tensor_scalar(tr[2], tr[1], float(np.pi), -TWO_PI, ALU.is_gt, ALU.mult))
            link(dve.tensor_tensor(tr[1], tr[1], tr[2], ALU.add))
            pi = float(np.nextafter(np.float32(np.pi), np.float32(0)))
            for i in range(2):
                ins = dve.tensor_scalar(tr[i], tr[i], pi, -pi, ALU.min, ALU.max)
                ins.then_inc(dve_step, 1)
                n_step[0] += 1
            dve.wait_ge(dve_step, n_step[0])
            dve.memset(flag[:, 1:2], 0.0).then_inc(ang_made, 1)
            dve.wait_ge(cond_made, 1)
            dve.wait_ge(acc_row, 16)
            for b in range(ADA_FIRST):
                ada_sums(b, 0, 8)

            def mod_columns(i, ps_sh, ps_sc, g):
                link(dve.tensor_scalar(adacols[:, 8 * i:8 * i + 8], ps_sh, SX, None, ALU.mult))
                link(dve.tensor_scalar(acol[:, i, :], ps_sc, 1.0, None, ALU.add))
                link(dve.tensor_tensor(acol[:, i, :], acol[:, i, :], vec8[:, g:g + 8], ALU.mult))
            dve.wait_ge(sin_made, 1)
            rms_xn(0)
            dve.wait_ge(mod_mm, 1)
            mod_columns(0, ps[:, 2, 0:8], ps[:, 2, 8:16], V_G1)
            dve.memset(flag[:, 2:3], 0.0).then_inc(mod_cols, 1)
            norm_split(0)
            phase(ffn1)
            new_x(1)
            dve.wait_ge(mod_mm, 4)
            mod_columns(1, ps[:, 4, 0:8], ps[:, 4, 8:16], V_G2)
            mod_columns(2, ps[:, 4, 16:24], ps[:, 4, 24:32], V_G3)
            dve.memset(flag[:, 2:3], 0.0).then_inc(mod_cols, 1)
            rms_xn(1)
            norm_split(1)

            for i in range(10):
                ahead(Unit(U_MIX + i))
                if 2 <= i < 8:
                    r = i - 2
                    dst = (q1, k1)[r // 3][:, 2 * (r % 3):2 * (r % 3) + 2, :]
                    rope(r, 0, slice(0, P), cosb, sinb, qraw1[r % 2], rtmp1, dst, 2)
            dve.wait_ge(pool_hi, 1)
            for k in range(2):
                ins = dve.scalar_tensor_tensor(out=ylo[:, k, :], in0=ps[:, 6, k * T:(k + 1) * T],
                                               scalar=vec8[:, V_PS + k:V_PS + k + 1], in1=yhi[:, k, :],
                                               op0=ALU.mult, op1=ALU.subtract)
            ins.then_inc(pool_lo, 1)
            dve.wait_ge(b1_in, 32)
            attention(1)
            for j in range(4):
                for i in range(4):
                    ahead(Unit(U_MIX + 10 + 4 * j + i))
                b0 = 4 * (j % 2)
                dve.wait_ge(sig_made, 2 * j + 2)
                if j:
                    dve.wait_ge(m_hi, j)
                for i in range(2):
                    link(dve.scalar_tensor_tensor(out=gtmp[2 + i], in0=ps[:, b0 + i, :], scalar=SX / S, in1=gtmp[i],
                                                  op0=ALU.mult, op1=ALU.mult))
                dve.tensor_tensor(gtmp[2], gtmp[2], gtmp[3], ALU.add).then_inc(m_made, 1)
                dve.wait_ge(m_hi, j + 1)
                dve.tensor_tensor(mlo[:, 2 * j:2 * j + 2, :], gtmp[2].rearrange("p (k n) -> p k n", k=2),
                                  mhi[:, 2 * j:2 * j + 2, :], ALU.subtract).then_inc(m_lo, 1)
                dve.wait_ge(m_lo, j + 1)
            for j in range(4):
                ahead(Unit(U_MIX + 26 + j))
            new_x(2)
            rms_xn(2)
            norm_split(2)
            phase(ffn2)
            new_x(3)
            rms_xn(3)
            norm_split(3)

            for l in range(LAYERS):
                ul, rb = U_L + N_L * l, 6 + 6 * l
                if l:
                    norm_split(5)
                else:
                    dve.wait_ge(b2_in, 16)
                full, mla = slice(0, P), slice(0, 96)
                for i in range(11):
                    ahead(Unit(ul + i))
                    if i in (1, 2):
                        r = i - 1
                        rope(r, rb, full, tables[:, 0, :], tables[:, 1, :], qraw2[r % 2], rtmp2, rqk[:, 2 * r:2 * r + 2, :], 2)
                dve.wait_ge(x_upd, 2 * (2 * l + 1))
                rope(2, rb, slice(64, 96), tables[:, 2, :], tables[:, 3, :], qraw2[0], rtmp2,
                     kro[64:96, :].unsqueeze(1), 1)
                for i, (ks, v) in enumerate((((0, 1, 2), V_QN + 3 * l), ((3, 4), V_KVN + 2 * l))):
                    dve.wait_ge(std_made, 2 * l + i + 1)
                    link(dve.reciprocal(rstdb[:, i, :], rstdb[:, i, :]))
                    for k in ks:
                        c = v + k - ks[0]
                        ins = dve.scalar_tensor_tensor(out=cT[:, k, :], in0=cT[:, k, :], scalar=vec8[:, c:c + 1],
                                                       in1=rstdb[:, i, :], op0=ALU.mult, op1=ALU.mult)
                        if k != ks[-1]:
                            ins.then_inc(dve_step, 1)
                            n_step[0] += 1
                    ins.then_inc(cn_made, 1)
                for i, ks in enumerate((slice(0, 3), slice(3, 5))):
                    dve.wait_ge(c_hi, 2 * l + i + 1)
                    dve.tensor_tensor(clo[:, ks, :], cT[:, ks, :], chi[:, ks, :], ALU.subtract).then_inc(c_lo, 1)
                ahead(Unit(ul + 11))
                for j in range(3):
                    rope(3 + j, rb, mla, tables[:, 2, :], tables[:, 3, :], qraw2[(3 + j) % 2], rtmp2,
                         qm[0:96, 2 * j:2 * j + 2, :], 2)
                ahead(Unit(ul + 12))
                for h in range(4):
                    dve.wait_ge(ret_mm, 4 * l + h + 1)
                    if h >= 2:
                        dve.wait_ge(ret_o, 4 * l + h - 1)
                    dve.tensor_tensor(dret[h % 2], ps[:, h % 3, 0:384], decay[:, h, :], ALU.mult).then_inc(ret_d, 1)
                dve.wait_ge(ret_o, 4 * l + 4)

                def heads(v):
                    return v.rearrange("p (h n) -> p h n", n=64)

                def wide(v):
                    return v.unsqueeze(2).to_broadcast([P, 8, 64])
                link(dve.tensor_reduce(stat[:, 56:64], heads(ps[:, 6, :]), AX.X, ALU.add))
                link(dve.tensor_scalar(stat[:, 56:64], stat[:, 56:64], 1.0 / 64, None, ALU.mult))
                dve.tensor_tensor(heads(ocen), heads(ps[:, 6, :]), wide(stat[:, 56:64]), ALU.subtract).then_inc(ret_oc, 1)
                dve.wait_ge(ret_std, 2 * l + 1)
                dve.tensor_reduce(stat[:, 40:48], heads(osq), AX.X, ALU.add).then_inc(ret_var, 1)
                dve.wait_ge(ret_std, 2 * l + 2)
                link(dve.reciprocal(stat[:, 48:56], stat[:, 48:56]))
                link(dve.tensor_tensor(heads(ocen), heads(ocen), wide(stat[:, 48:56]), ALU.mult))
                dve.wait_ge(gn_in, 16 * (l + 1))
                o3 = ocen.rearrange("p (t n) -> p t n", t=2)
                link(dve.tensor_tensor(o3, o3, gnw.unsqueeze(1).to_broadcast([P, 2, T]), ALU.mult))
                dve.tensor_tensor(oret.rearrange("p (t n) -> p t n", t=2), o3, rg, ALU.mult).then_inc(ret_y, 1)
                dve.wait_ge(ret_hi, l + 1)
                dve.scalar_tensor_tensor(out=mixlo[:, 0:2, :], in0=ps[:, 7, :].rearrange("p (k n) -> p k n", k=2), scalar=SX,
                                         in1=mixhi[:, 0:2, :], op0=ALU.mult, op1=ALU.subtract).then_inc(ret_lo, 1)
                dve.wait_ge(sinks_in, 16)
                attention(2, l)
                for j in range(4):
                    ahead(Unit(ul + 13 + j))
                n = 4 + 2 * l
                layer_xn(n)
                norm_split(n)
                ahead(Unit(ul + 17))

                def gates():
                    sc = rr[:, 0, :]
                    v3 = lambda i: rr[:, i, :].rearrange("p (t e) -> p t e", t=2)
                    v4 = lambda i: rr[:, i, :].rearrange("p (t g e) -> p t g e", t=2, g=4)
                    small8 = lambda i: rr[:, i, 0:8].rearrange("p (t g) -> p t g", t=2)
                    one2 = lambda i: rr[:, i, 0:2].unsqueeze(2)
                    prio16 = small[:, C_PRIO16:C_PRIO16 + 16].unsqueeze(1).to_broadcast([P, 2, 16])
                    prio4 = small[:, C_PRIO4:C_PRIO4 + 4].unsqueeze(1).to_broadcast([P, 2, 4])
                    TTO, TS = dve.tensor_tensor, dve.tensor_scalar
                    dve.wait_ge(bias_in, 16)
                    dve.wait_ge(rt_sig, l + 1)
                    link(TTO(v3(1), v3(0), rbias[:, :].unsqueeze(1).to_broadcast([P, 2, 16]), ALU.add))
                    b = v4(1)
                    pairs = [(i, j) for i in range(4) for j in range(i + 1, 4)]
                    for n_, (i, j) in enumerate(pairs):
                        link(TTO(small8(2).unsqueeze(3), b[:, :, :, i:i + 1], b[:, :, :, j:j + 1], ALU.add) if n_ == 0 else
                             TTO(small8(3).unsqueeze(3), b[:, :, :, i:i + 1], b[:, :, :, j:j + 1], ALU.add))
                        if n_:
                            link(TTO(small8(2), small8(2), small8(3), ALU.max))

                    def first_best(v, n, prio, view, src, tmp, dst):
                        link(dve.tensor_reduce(rr[:, tmp, 0:2], view(src), AX.X, ALU.max))
                        link(TTO(view(dst), view(src), one2(tmp).to_broadcast([P, 2, n]), ALU.is_ge))
                        link(TTO(view(dst), view(dst), prio, ALU.mult))
                        link(dve.tensor_reduce(rr[:, tmp, 0:2], view(dst), AX.X, ALU.max))
                        link(TTO(view(dst), view(dst), one2(tmp).to_broadcast([P, 2, n]), ALU.is_equal))
                    first_best(None, 4, prio4, small8, 2, 4, 5)
                    link(TS(rr[:, 6, 0:8], rr[:, 5, 0:8], -1.0, -NEG, ALU.add, ALU.mult))
                    gsel = small8(5).unsqueeze(3).to_broadcast([P, 2, 4, 4])
                    gneg = small8(6).unsqueeze(3).to_broadcast([P, 2, 4, 4])
                    link(TTO(v4(7), v4(1), gsel, ALU.mult))
                    link(TTO(v4(7), v4(7), gneg, ALU.add))
                    first_best(None, 16, prio16, v3, 7, 4, 8)
                    link(dve.scalar_tensor_tensor(out=rr[:, 9, :], in0=rr[:, 8, :], scalar=3 * NEG, in1=rr[:, 7, :],
                                                  op0=ALU.mult, op1=ALU.add))
                    first_best(None, 16, prio16, v3, 9, 4, 10)
                    link(TTO(rr[:, 11, :], rr[:, 8, :], rr[:, 10, :], ALU.add))
                    link(TTO(rr[:, 12, :], rr[:, 11, :], rr[:, 0, :], ALU.mult))
                    link(dve.tensor_reduce(rr[:, 13, 0:2], v3(12), AX.X, ALU.add))
                    link(dve.reciprocal(rr[:, 14, 0:2], rr[:, 13, 0:2]))
                    TTO(v3(19), v3(12), one2(14).to_broadcast([P, 2, 16]), ALU.mult).then_inc(gate_made, 1)
                    dve.wait_ge(gb_out, 8 * l + 8)
                phase(moe[l], between=gates)
                layer_xn(n + 1)
            dve.wait_ge(ln_in, 16 + 32 * 4)
            for t in range(TT):
                dve.wait_ge(xn_made, 14 + t + 1)
                link(dve.tensor_tensor(x[:, t, :], xn[:, t, :], lng, ALU.mult))
                dve.tensor_tensor(x[:, t, :], x[:, t, :], lnb, ALU.add).then_inc(x_new, 1)


_INS = ["x", "c", "positions", "w_ada", "b_ada", "g_norm_ffn1", "w_ffn1_in", "w_ffn1_out", "g_norm_mix", "w_in", "w_pool",
        "pool_scale", "w_pool_branch", "w_attn_branch", "w_out", "g_norm_ffn2", "w_ffn2_in", "w_ffn2_out", "g_final",
        "w_in_2", "ret_gn_w_2", "swa_sinks_2", "mla_q_norm_w_2", "mla_kv_norm_w_2", "mla_w_uq_2", "mla_w_ukv_2", "w_out_2",
        "ln1_g_2", "ln1_b_2", "router_w_2", "router_bias_2", "exp_w_gate_up_2", "exp_w_down_2", "ln2_g_2", "ln2_b_2"]


def kernel(**inputs):
    import concourse.bacc as _bacc
    from concourse.bass_utils import run_bass_kernel_spmd as _run

    nc = _bacc.Bacc("TRN2", target_bir_lowering=False, num_devices=1)
    arrays = {f"in_{n}_dram": np.ascontiguousarray(inputs[n]) for n in _INS}
    for name, table in zip(("const_small", "const_block1", "const_block2"), constants()):
        arrays[f"in_{name}_dram"] = table
    args = {k[3:-5]: nc.dram_tensor(k, v.shape, mybir.dt.from_np(v.dtype), kind="ExternalInput").ap()
            for k, v in arrays.items()}
    out = nc.dram_tensor("out_0_dram", (1, T, D), F32, kind="ExternalOutput").ap()
    build(nc, args, out)
    r = _run(nc, [arrays], core_ids=[0])
    return r.results[0]["out_0_dram"]
```

```python
from contextlib import ExitStack

import numpy as np

import concourse.bass as bass
from concourse import mybir

F32 = mybir.dt.float32
F16 = mybir.dt.float16
I32 = mybir.dt.int32
ALU = mybir.AluOpType
ACT = mybir.ActivationFunctionType
AX = mybir.AxisListType

P = 128
D = 1024
T = 256
KT = D // P
TT = T // P
F = 2816
UNIT = 2048
RING = 6
AHEAD = 3
SW, SX = 64.0, 8.0
S = SW * SX
LAYERS = 2
EXPERTS = 16
HALF = 512

RMS_EPS = 1e-6
LN_EPS = 1e-5
ALPHA = float(np.float32((2 * LAYERS) ** 0.25))

FFN_CHUNKS = F // 256
U_FFN1 = 0
U_MIX = U_FFN1 + 3 * FFN_CHUNKS
N_MIX = 30
U_FFN2 = U_MIX + N_MIX
U_L = U_FFN2 + 3 * FFN_CHUNKS
N_LMIX = 18
IN_UNITS = ("ret q", "ret k", "ret v", "latents 01", "latent 2", "latents 34", "key rope", "ret gate", "swa q",
            "swa q k", "swa v")
IN_COLS = (0, 1, 2, 7, 8, 9, 10, 3, 4, 5, 6)
N_L = N_LMIX + 3 * EXPERTS
U_END = U_L + LAYERS * N_L

ADA_BLOCK = 768
ADA_BLOCKS = 9 * D // ADA_BLOCK
ADA_FIRST = 3

V_C, V_G1, V_G2, V_G3, V_GF = 0, 8, 16, 24, 32
V_LN1G, V_LN1B, V_LN2G, V_LN2B = 40, 56, 72, 88
V_QN, V_KVN, V_PS, V_N = 104, 110, 114, 116

C_IDENT, C_ROT, C_ROTM, C_ONES, C_INVF, C_EPS, C_EPSLN, C_PRIO16, C_PRIO4 = 0, 128, 256, 384, 512, 513, 514, 516, 532
C_SMALL = 536
NEG = -1e30

TWO_PI = 2 * np.pi
PI_1 = 6.28125
PI_2 = float(np.float32(np.round((TWO_PI - PI_1) * 2 ** 20) / 2 ** 20))
PI_3 = float(np.float32(TWO_PI - PI_1 - PI_2))
ROUND = 1.5 * 2 ** 23


def constants():
    small = np.zeros((P, C_SMALL), np.float32)
    small[:, C_IDENT:C_IDENT + P] = np.eye(P)
    for b in (0, 64):
        for i in range(32):
            small[b + 32 + i, C_ROT + b + i] = -1.0
            small[b + i, C_ROT + b + 32 + i] = 1.0
    for i in range(16):
        small[80 + i, C_ROTM + 64 + i] = -1.0
        small[64 + i, C_ROTM + 80 + i] = 1.0
    small[:, C_ONES:C_ONES + P] = 1.0
    inv64 = (np.float32(10000.0) ** (-np.arange(0, 64, 2, dtype=np.float32) / np.float32(64))).astype(np.float32)
    inv32 = (np.float32(10000.0) ** (-np.arange(0, 32, 2, dtype=np.float32) / np.float32(32))).astype(np.float32)
    small[:, C_INVF] = np.tile(inv64, 4)
    small[:, C_EPS] = RMS_EPS
    small[:, C_EPSLN] = LN_EPS
    small[:, C_EPSLN + 1] = LN_EPS * S * S
    small[:, C_PRIO16:C_PRIO16 + 16] = 16 - np.arange(16)
    small[:, C_PRIO4:C_PRIO4 + 4] = 4 - np.arange(4)

    t = np.arange(T)

    def by_queries(ok):
        m = np.where(ok, 0.0, NEG).astype(np.float32)
        return np.concatenate([m[:P, :P], m[P:, :]], 1)

    rel = t[:, None] - t[None, :]
    masks1 = np.concatenate([by_queries((rel >= 0) & (rel <= 128)),
                             by_queries((rel >= 0) & (rel % 4 == 0)),
                             by_queries((rel >= 0) & (rel % 16 == 0))], 1)
    count = np.zeros((P, 2, T), np.float32)
    for g, w in enumerate((2, 4, 8, 16)):
        count[64 * (g % 2):64 * (g % 2) + 64, g // 2] = 1.0 / np.minimum(t + 1, w)
    block1 = np.concatenate([masks1, count.reshape(P, 2 * T)], 1)

    ang64 = (t[None, :].astype(np.float32) * np.tile(inv64, 4)[:, None]).astype(np.float32)
    cosr, sinr = np.cos(ang64), np.sin(ang64)
    ang32 = (t[None, :].astype(np.float32) * np.tile(inv32, 2)[:, None]).astype(np.float32)
    cosm, sinm = np.ones((P, T), np.float32), np.zeros((P, T), np.float32)
    cosm[64:96], sinm[64:96] = np.cos(ang32), np.sin(ang32)
    decay = np.zeros((4, P, 384), np.float32)
    for h in range(4):
        log_g = np.log(1.0 - 2.0 ** (-5.0 - h))
        m = np.where(rel.T >= 0, np.exp(np.maximum(rel.T, 0) * log_g), 0.0) * 64 ** -0.5
        decay[h] = np.concatenate([m[:P, :], m[P:, P:]], 1)
    block2 = np.concatenate([cosr, sinr, cosm, sinm,
                             by_queries((rel >= 0) & (rel < 128)), by_queries(rel >= 0),
                             decay.transpose(1, 0, 2).reshape(P, 4 * 384)], 1)
    slots = np.concatenate([np.triu(np.ones((P, P)), 1), np.tile(np.arange(P), (P, 1))], 1)
    return small, block1.astype(np.float32), block2.astype(np.float32), slots.astype(np.float32)


class Unit:

    def __init__(self, c, turn=0):
        self.c, self.turn = c, turn

    def __add__(self, k):
        return Unit(self.c + k, self.turn)

    @property
    def slot(self):
        return self.c % RING

    def count(self, k=0):
        return self.turn * RING + (self.c + k + RING)

    def loads(self):
        return self.turn * 16 + 16 * (self.c // RING + 1)


def build(nc, a, out):
    small_d, b1_d, b2_d = a["const_small"], a["const_block1"], a["const_block2"]
    with ExitStack() as ctx:
        def sb(name, shape, dt=F32):
            return ctx.enter_context(nc.sbuf_tensor(name, shape, dt))

        def sem(name):
            return ctx.enter_context(nc.semaphore(name))

        raw = sb("raw", [P, RING, UNIT])
        whi = sb("whi", [P, RING, UNIT], F16)
        wlo = sb("wlo", [P, RING, UNIT], F16)
        x = sb("x", [P, TT, D])
        uhi = sb("uhi", [P, KT, T], F16)
        ulo = sb("ulo", [P, KT, T], F16)
        gt = sb("gt", [P, 3, D])
        small = sb("small", [P, C_SMALL])
        vec = sb("vec", [P, V_N])
        vec8 = sb("vec8", [P, V_N])
        adacols = sb("adacols", [P, 48])
        acol = sb("acol", [P, 3, 8])
        zero8 = sb("zero8", [P, 8])
        cond = sb("cond", [P, 8])
        cosb = sb("cosb", [P, T])
        sinb = sb("sinb", [P, T])
        sinks = sb("sinks", [P, 12])
        zeros16 = sb("zeros16", [P, HALF], F16)
        stat = sb("stat", [P, 64])
        bnst_t = sb("bnst", [P, 12])
        bnst = bnst_t[:, :]
        rbias = sb("rbias", [P, 16])
        flag = sb("flag", [P, 8])
        xn = sb("xn", [P, TT, D])
        hreg = sb("hreg", [P, 2048])
        area = sb("area", [P, 15360])
        ps = ctx.enter_context(nc.psum_tensor("ps", [P, 8, HALF], F32))

        ident = small[:, C_IDENT:C_IDENT + P]
        rot = small[:, C_ROT:C_ROT + P]
        ones = small[:, C_ONES:C_ONES + P]

        s_act = hreg[:, 0:512]
        h_f32 = hreg[:, 512:1024]
        hhi = hreg[:, 1024:1536].bitcast(F16).rearrange("p (b n) -> p b n", b=2)
        hlo = hreg[:, 1536:2048].bitcast(F16).rearrange("p (b n) -> p b n", b=2)

        def region(base):
            at = [0]

            def take(n, shape=None, dt=F32):
                v = base[:, at[0]:at[0] + n]
                at[0] += n
                assert at[0] <= base.shape[1], at[0]
                if dt is not F32:
                    v = v.bitcast(dt)
                return v
            return take

        tk = region(area)
        acc = tk(9 * D)
        aring = tk(4 * 2 * ADA_BLOCK).rearrange("p (s k n) -> p s k n", s=4, k=2)
        tk = region(area)
        masks1 = tk(3 * 384).rearrange("p (g n) -> p g n", g=3)
        ptmp = tk(2048).rearrange("p (s n) -> p s n", s=4)
        q1 = tk(1536).rearrange("p (k n) -> p k n", k=6)
        k1 = tk(1536).rearrange("p (k n) -> p k n", k=6)
        rt1 = tk(2048)
        v1 = tk(1536).rearrange("p (t n) -> p t n", t=2)
        sb1 = [tk(1152).rearrange("p (g n) -> p g n", g=3) for _ in range(2)]
        pt1 = [rt1[:, 0:1152].rearrange("p (g n) -> p g n", g=3)]
        mhi = tk(1024, dt=F16).rearrange("p (k n) -> p k n", k=8)
        mlo = tk(1024, dt=F16).rearrange("p (k n) -> p k n", k=8)
        qraw1 = [rt1[:, 512 * i:512 * i + 512] for i in range(2)]
        rtmp1 = [rt1[:, 1024 + 512 * i:1536 + 512 * i] for i in range(2)]
        gtmp = [sb1[0].rearrange("p g n -> p (g n)")[:, 0:512], sb1[0].rearrange("p g n -> p (g n)")[:, 512:1024],
                sb1[1].rearrange("p g n -> p (g n)")[:, 0:512], sb1[1].rearrange("p g n -> p (g n)")[:, 512:1024]]
        yhi = hreg[:, 0:512].bitcast(F16).rearrange("p (k n) -> p k n", k=4)
        ylo = hreg[:, 512:1024].bitcast(F16).rearrange("p (k n) -> p k n", k=4)
        pT = hreg[:, 1024:1536].rearrange("p (k n) -> p k n", k=2)
        rcount = hreg[:, 1536:2048].rearrange("p (k n) -> p k n", k=2)
        wpool = gt[:, 0, 0:128].rearrange("p (k n) -> p k n", k=2)
        tk = region(area)
        tables = tk(1024).rearrange("p (k n) -> p k n", k=4)
        masks2 = tk(768).rearrange("p (k n) -> p k n", k=2)
        decay = tk(1536).rearrange("p (k n) -> p k n", k=4)
        b2const = area[:, 0:3328]
        rqk = tk(1024).rearrange("p (k n) -> p k n", k=4)
        rv = tk(512).rearrange("p (t n) -> p t n", t=2)
        rg = tk(512).rearrange("p (t n) -> p t n", t=2)
        sq = tk(768).rearrange("p (k n) -> p k n", k=3)
        sk = tk(512).rearrange("p (k n) -> p k n", k=2)
        sv = cosb[:, :].rearrange("p (t n) -> p t n", t=2)
        cT_flat = tk(2304)
        cT = cT_flat[:, 0:1280].rearrange("p (k n) -> p k n", k=5)
        rstdb = cT_flat[:, 1280:1792].rearrange("p (k n) -> p k n", k=2)
        sb2 = [cT_flat[:, 384 * i:384 * i + 384].rearrange("p (g n) -> p g n", g=1) for i in range(2)]
        pt2 = [cT_flat[:, 768 + 384 * i:1152 + 384 * i].rearrange("p (g n) -> p g n", g=1) for i in range(2)]
        chi = tk(640, dt=F16).rearrange("p (k n) -> p k n", k=5)
        clo = tk(640, dt=F16).rearrange("p (k n) -> p k n", k=5)
        qm_flat, km_flat = tk(1536), tk(1536)
        qm, km = (v.rearrange("p (k n) -> p k n", k=6) for v in (qm_flat, km_flat))
        dret = [qm_flat[:, 384 * i:384 * i + 384] for i in range(4)]
        ocen, osq, oret = (km_flat[:, HALF * i:HALF * i + HALF] for i in range(3))
        rt2 = tk(2048)
        qraw2 = [rt2[:, 512 * i:512 * i + 512] for i in range(2)]
        rtmp2 = [rt2[:, 1024 + 512 * i:1536 + 512 * i] for i in range(2)]
        vm = gt[:, 2, 256:1024].rearrange("p (t n) -> p t n", t=2)
        gnw = gt[:, 2, 0:256]
        kro = xn[:, 0, 0:256]
        sqv = [hreg[:, 256:1024].rearrange("p (k n) -> p k n", k=3), hreg[:, 1280:1792].rearrange("p (k n) -> p k n", k=2)]
        mixhi = hreg[:, 0:1024].bitcast(F16).rearrange("p (k n) -> p k n", k=8)
        mixlo = hreg[:, 1024:2048].bitcast(F16).rearrange("p (k n) -> p k n", k=8)
        gb = area[:, 3328:3328 + 4096].rearrange("p (e n) -> p e n", e=EXPERTS)
        rr = area[:, 3328 + 4096:3328 + 4096 + 640].rearrange("p (s n) -> p s n", s=20)
        gatesT = area[:, 8192:8192 + T]
        cosb2 = sinb
        tk = region(area[:, 8448:15360])
        p32_ysplit3 = tk(1024)
        p32 = p32_ysplit3.rearrange("p (t n) -> p t n", t=2)
        p16 = tk(512, dt=F16).rearrange("p (t n) -> p t n", t=2)
        pT16 = tk(512, dt=F16).rearrange("p (g n) -> p g n", g=4)
        gslots = tk(512)
        ident16 = tk(64, dt=F16)
        ysplit = [tk(1024) for _ in range(3)] + [p32_ysplit3]
        ysh = [v[:, 0:512].bitcast(F16) for v in ysplit]
        ysl = [v[:, 512:1024].bitcast(F16) for v in ysplit]
        tk = region(area[:, 3328:3328 + 4096])
        gbs = tk(2048).rearrange("p (e n) -> p e n", e=EXPERTS)
        xh = tk(1024, dt=F16).rearrange("p (t n) -> p t n", t=2)
        xl = tk(1024, dt=F16).rearrange("p (t n) -> p t n", t=2)
        earlier, slot_no = cosb2[:, 0:P], cosb2[:, P:T]
        uq4 = [hreg[:, 256:512].rearrange("p (k n) -> p k n", k=2), hreg[:, 768:1024].rearrange("p (k n) -> p k n", k=2)]
        lng, lnb = gt[:, 0, :], gt[:, 1, :]
        vstack = hreg[:, 0:P]
        posi = hreg[:, 128:384].bitcast(I32)
        posf = hreg[:, 384:640]
        tr = [hreg[:, 1024 + 256 * i:1280 + 256 * i] for i in range(4)]

        raw_in = [sem(f"raw_in{i}") for i in range(RING)]
        hi_made, lo_made, used = sem("hi_made"), sem("lo_made"), sem("used")
        const_in, x_in, stack_in, pos_in, sinks_in = (sem(n) for n in ("const_in", "x_in", "stack_in", "pos_in", "sinks_in"))
        acc_zero, acc_row, ada_sum = sem("acc_zero"), sem("acc_row"), sem("ada_sum")
        ada_in = [sem(f"ada_in{i}") for i in range(4)]
        ada_late = [sem(f"ada_late{i}") for i in range(4)]
        vec_t, cond_made, vec_out, pos_f, pos_bc, ang_made, sin_made = (
            sem(n) for n in ("vec_t", "cond_made", "vec_out", "pos_f", "pos_bc", "ang_made", "sin_made"))
        mod_mm, mod_cols, gt_out = sem("mod_mm"), sem("mod_cols"), sem("gt_out")
        x_new, rms_made, var_made, xn_made, xt_made, u_hi, u_lo = (
            sem(n) for n in ("x_new", "rms_made", "var_made", "xn_made", "xt_made", "u_hi", "u_lo"))
        silu_made, h_made, h_hi, h_lo, y_done = (sem(n) for n in ("silu_made", "h_made", "h_hi", "h_lo", "y_done"))
        dve_step, act_step, pool_step = sem("dve_step"), sem("act_step"), sem("pool_step")
        b1_in, wpool_in, pool_d, pool_mm, pool_hi, pool_lo = (
            sem(n) for n in ("b1_in", "wpool_in", "pool_d", "pool_mm", "pool_hi", "pool_lo"))
        proj_out, rot_mm, rope_out = sem("proj_out"), sem("rot_mm"), sem("rope_out")
        sc_mm, sc_in, max_made, exp_made, p_made, tr_mm, tr_out, pv_mm, yo_hi, yo_lo = (
            sem(n) for n in ("sc_mm", "sc_in", "max_made", "exp_made", "p_made", "tr_mm", "tr_out", "pv_mm", "yo_hi", "yo_lo"))
        sig_made, m_made, m_hi, m_lo = sem("sig_made"), sem("m_made"), sem("m_hi"), sem("m_lo")
        b2_in, ln_in, x_upd, zero_made = sem("b2_in"), sem("ln_in"), sem("x_upd"), sem("zero_made")
        swap_mm, swap_out, gn_in = sem("swap_mm"), sem("swap_out"), sem("gn_in")
        sqr_made, ss_mm, std_made, cn_made, c_hi, c_lo, km_rope = (
            sem(n) for n in ("sqr_made", "ss_mm", "std_made", "cn_made", "c_hi", "c_lo", "km_rope"))
        ret_mm, ret_d, ret_o, ret_std, ret_y, ret_t, ret_hi, ret_lo, ret_oc, ret_var = (
            sem(n) for n in ("ret_mm", "ret_d", "ret_o", "ret_std", "ret_y", "ret_t", "ret_hi", "ret_lo", "ret_oc", "ret_var"))
        latent_mm, router_sig, gate_made = (sem(n) for n in ("latent_mm", "router_sig", "gate_made"))
        out_done, m_moe, bias_in = sem("out_done"), sem("m_moe"), sem("bias_in")
        u_f = sem("u_f")
        rank_mm, rank_out, x_hi, x_lo = sem("rank_mm"), sem("rank_out"), sem("x_hi"), sem("x_lo")
        slots_in = sem("slots_in")

        def by_layer(name):
            return [sem(f"{name}_{l}") for l in range(LAYERS)]
        gate_t, gateT_out, gb_mm, gb_out = (by_layer(n) for n in ("gate_t", "gateT_out", "gb_mm", "gb_out"))
        p_step, p16_made, pT_mm, pT_out, gs_mm, gs_out = (
            by_layer(n) for n in ("p_step", "p16_made", "pT_mm", "pT_out", "gs_mm", "gs_out"))
        gbs_mm, gbs_out, ga_mm, ga_f, ga_hi, ga_lo, ys_hi, ys_lo, yg_mm = (
            by_layer(n) for n in ("gbs_mm", "gbs_out", "ga_mm", "ga_f", "ga_hi", "ga_lo", "ys_hi", "ys_lo", "yg_mm"))

        def ktiles(w):
            return w.rearrange("(k p) n -> p k n", p=P)

        w_in, w_in2 = ktiles(a["w_in"][0]), [ktiles(a["w_in_2"][l]) for l in range(LAYERS)]

        def mix1_units():
            cols = [w_in[:, :, 256 * i:256 * i + 256] for i in range(10)]
            for j in range(4):
                c = slice(256 * j, 256 * j + 256)
                cols += [ktiles(a["w_pool_branch"][0])[:, :, c], ktiles(a["w_attn_branch"][0])[:, :, c],
                         w_in[:, :, 2560 + 256 * j:2816 + 256 * j], w_in[:, :, 3584 + 256 * j:3840 + 256 * j]]
            return cols + [ktiles(a["w_out"][0])[:, 2 * j:2 * j + 2, :] for j in range(4)]

        def mix2_units(l):
            edges = [0, 256, 512, 768, 1024, 1280, 1536, 1664, 1920, 2048, 2304, 2336]
            cols = [w_in2[l][:, :, edges[i]:edges[i + 1]] for i in IN_COLS]
            cols += [ktiles(a["mla_w_uq_2"][l]), ktiles(a["mla_w_ukv_2"][l])]
            cols += [ktiles(a["w_out_2"][l])[:, 2 * j:2 * j + 2, :] for j in range(4)]
            return cols + [ktiles(a["router_w_2"])]

        sources = {}
        for i, s_ in enumerate(mix1_units()):
            sources[U_MIX + i] = s_
        for l in range(LAYERS):
            for i, s_ in enumerate(mix2_units(l)):
                sources[U_L + N_L * l + i] = s_
        sizes = {u: s_.shape[1] * s_.shape[2] for u, s_ in sources.items()}

        def size(u):
            return sizes.get(u.c, UNIT) if isinstance(u.turn, int) and u.turn == 0 else UNIT

        def hi_part(act, u):
            if isinstance(u.turn, int) and u.c + RING * u.turn >= U_END:
                return
            n = size(u)
            act.wait_ge(raw_in[u.slot], u.loads())
            act.wait_ge(used, u.count(1 - RING))
            act.activation(whi[:, u.slot, 0:n], raw[:, u.slot, 0:n], ACT.Copy, scale=SW).then_inc(hi_made, 1)

        def lo_part(dve, u):
            if isinstance(u.turn, int) and u.c + RING * u.turn >= U_END:
                return
            n = size(u)
            dve.wait_ge(hi_made, u.count(1))
            dve.scalar_tensor_tensor(out=wlo[:, u.slot, 0:n], in0=raw[:, u.slot, 0:n], scalar=SW,
                                     in1=whi[:, u.slot, 0:n], op0=ALU.mult, op1=ALU.subtract).then_inc(lo_made, 1)

        def ffn_src(w_i, w_o):
            wi, wo = ktiles(w_i), w_o.rearrange("(c k p) n -> p c k n", p=P, k=2)

            def src(kind, c):
                if kind == "o":
                    return wo[:, c, :, :] if isinstance(c, int) else wo[:, bass.ds(c, 1), :, :].rearrange("p a k n -> p (a k) n")
                off = 0 if kind == "a" else F
                return wi[:, :, bass.ds(c * 256 + off, 256)]
            return src

        def moe_src(l):
            wi = a["exp_w_gate_up_2"][l].rearrange("e (k p) n -> p e k n", p=P)
            wo = a["exp_w_down_2"][l].rearrange("e (k p) n -> p e k n", p=P)

            def src(kind, c):
                w = wo if kind == "o" else wi
                v = w[:, c, :, :] if isinstance(c, int) else w[:, bass.ds(c, 1), :, :].rearrange("p a k n -> p (a k) n")
                return v if kind == "o" else v[:, :, 0:256] if kind == "a" else v[:, :, 256:512]
            return src

        class Phase:

            def __init__(self, u0, g0, n, src, ada=False, moe=False):
                self.u0, self.g0, self.n, self.src, self.ada, self.moe = u0, g0, n, src, ada, moe

        ffn1 = Phase(U_FFN1, 0, FFN_CHUNKS, ffn_src(a["w_ffn1_in"][0], a["w_ffn1_out"][0]), ada=True)
        ffn2 = Phase(U_FFN2, FFN_CHUNKS, FFN_CHUNKS, ffn_src(a["w_ffn2_in"][0], a["w_ffn2_out"][0]))
        moe = [Phase(U_L + N_L * l + N_LMIX, 2 * FFN_CHUNKS + EXPERTS * l, EXPERTS, moe_src(l), moe=True)
               for l in range(LAYERS)]

        def steps(eng, ph, body):
            n_pairs = 4 if ph.ada else (ph.n - 1) // 2
            with eng.Fori(0, n_pairs) as i:
                for j in (1, 2):
                    body(2 * i + j, Unit(ph.u0 + 3 * j - 1, i), j % 2)
            for c in range(2 * n_pairs + 1, ph.n):
                body(c, Unit(ph.u0 + 3 * c - 1), c % 2)

        w_ada = ktiles(a["w_ada"][0])

        def ada_block(eng, b):
            for j in range(4):
                if b:
                    eng.wait_ge(ada_sum, 8 * (b - 1) + 2 * j + 2)
                eng.dma_start(aring[:, j, :, :], w_ada[:, 2 * j:2 * j + 2, b * ADA_BLOCK:(b + 1) * ADA_BLOCK])\
                    .then_inc((ada_in if b < ADA_FIRST else ada_late)[j], 16)

        block = ctx.enter_context(nc.Block())

        @block.sync
        def _(sp):
            sp.dma_start(small[:, :], small_d).then_inc(const_in, 16)
            rows = [(V_C, a["c"][0]), (V_G1, a["g_norm_ffn1"][0]), (V_G2, a["g_norm_mix"][0]),
                    (V_G3, a["g_norm_ffn2"][0]), (V_GF, a["g_final"])]
            for l in range(LAYERS):
                rows += [(V_LN1G + 8 * l, a["ln1_g_2"][l]), (V_LN1B + 8 * l, a["ln1_b_2"][l]),
                         (V_LN2G + 8 * l, a["ln2_g_2"][l]), (V_LN2B + 8 * l, a["ln2_b_2"][l]),
                         (V_QN + 3 * l, a["mla_q_norm_w_2"][l]), (V_KVN + 2 * l, a["mla_kv_norm_w_2"][l])]
            rows.append((V_PS, a["pool_scale"][0]))
            for r, v in rows:
                v = v.rearrange("(r n) -> r n", n=P)
                sp.dma_start(vstack[r:r + v.shape[0], :], v).then_inc(stack_in, 16)
            sp.dma_start(posi[0:1, :], a["positions"]).then_inc(pos_in, 16)
            for t in range(TT):
                sp.dma_start(x[:, t, :], a["x"][0, t * P:(t + 1) * P, :]).then_inc(x_in, 16)
            sp.dma_start(sinks[:, :], a["swa_sinks_2"].rearrange("l h -> (l h)").partition_broadcast(P)).then_inc(sinks_in, 16)

            sp.dma_start(rbias[:, :], a["router_bias_2"].partition_broadcast(P)).then_inc(bias_in, 16)

            def load(u, src):
                if isinstance(u.turn, int) and u.c + RING * u.turn >= U_END:
                    return
                sp.wait_ge(lo_made, u.count(1 - RING))
                k, n = src.shape[1], src.shape[2]
                sp.dma_start(raw[:, u.slot, 0:k * n].rearrange("p (k n) -> p k n", k=k), src).then_inc(raw_in[u.slot], 16)

            def phase(ph):
                load(Unit(ph.u0), ph.src("a", 0))
                load(Unit(ph.u0 + 1), ph.src("b", 0))

                def step(c, u, par):
                    load(u, ph.src("a", c))
                    load(u + 1, ph.src("b", c))
                    load(u + 2, ph.src("o", c - 1))
                steps(sp, ph, step)
                load(Unit(ph.u0 + 3 * ph.n - 1), ph.src("o", ph.n - 1))

            sp.wait_ge(ada_sum, 16)
            phase(ffn1)
            for i in range(N_MIX):
                load(Unit(U_MIX + i), sources[U_MIX + i])
            phase(ffn2)
            for l in range(LAYERS):
                for i in range(N_LMIX):
                    load(Unit(U_L + N_L * l + i), sources[U_L + N_L * l + i])
                phase(moe[l])
            for t in range(TT):
                sp.wait_ge(x_new, 6 + t + 1)
                sp.dma_start(out[0, t * P:(t + 1) * P, :], x[:, t, :]).then_inc(out_done, 16)
            sp.wait_ge(out_done, 32)

        @block.gpsimd
        def _(pool):
            n_step = [0]

            def link(ins):
                n_step[0] += 1
                ins.then_inc(pool_step, 1)
                pool.wait_ge(pool_step, n_step[0])

            pool.memset(acc[:, ADA_FIRST * ADA_BLOCK:], 0.0).then_inc(acc_zero, 1)
            pool.wait_ge(acc_zero, 2)
            pool.dma_start(acc[0:1, :], a["b_ada"]).then_inc(acc_row, 16)
            for b in range(ADA_FIRST, ADA_BLOCKS):
                ada_block(pool, b)
            pool.wait_ge(gt_out, 6)
            pool.wait_ge(mod_cols, 2)
            pool.wait_ge(h_lo, FFN_CHUNKS)
            pool.wait_ge(y_done, 2)
            pool.dma_start(area[:, 0:1152], b1_d[:, 0:1152]).then_inc(b1_in, 16)
            pool.dma_start(hreg[:, 1536:2048], b1_d[:, 1152:1664]).then_inc(b1_in, 16)
            pool.wait_ge(x_new, 2)
            for g in range(4):
                pool.dma_start(gt[64 * (g % 2):64 * (g % 2) + 64, 0, 64 * (g // 2):64 * (g // 2) + 64],
                               a["w_pool"][0, g]).then_inc(wpool_in, 16)
            pool.wait_ge(proj_out, 1)
            pool.wait_ge(b1_in, 32)
            for k in range(2):
                src = pT[:, k, :]
                w = 1
                sums = []
                while w < (4, 16)[k]:
                    dst = ptmp[:, len(sums) % 4, 0:T] if k == 0 else ptmp[:, len(sums) % 4, 0:T]
                    link(pool.tensor_copy(dst[:, 0:w], src[:, 0:w]))
                    link(pool.tensor_tensor(dst[:, w:T], src[:, w:T], src[:, 0:T - w], ALU.add))
                    sums.append(dst)
                    src, w = dst, 2 * w
                d = ptmp[:, k, 256:512]
                for half, s_ in ((0, sums[-2]), (1, sums[-1])):
                    r = slice(64 * half, 64 * half + 64)
                    link(pool.tensor_tensor(d[r, :], s_[r, :], rcount[r, k, :], ALU.mult))
                    link(pool.tensor_tensor(d[r, :], d[r, :], pT[r, k, :], ALU.subtract))
            pool.memset(flag[:, 4:5], 0.0).then_inc(pool_d, 1)
            pool.wait_ge(y_done, 4)
            pool.wait_ge(x_new, 4)
            pool.dma_start(lng, a["g_final"].partition_broadcast(P)).then_inc(ln_in, 16)
            pool.wait_ge(x_new, 6)
            pool.dma_start(b2const, b2_d).then_inc(b2_in, 16)
            pool.dma_start(cosb2[:, :], a["const_slots"]).then_inc(slots_in, 16)
            pool.dma_start(gnw, a["ret_gn_w_2"][0].partition_broadcast(P)).then_inc(gn_in, 16)
            pool.wait_ge(ln_in, 16)
            for t in range(TT):
                pool.wait_ge(xn_made, 6 + t + 1)
                pool.tensor_tensor(x[:, t, :], xn[:, t, :], lng, ALU.mult).then_inc(x_upd, 1)
            for n in range(4, 7):
                l, second = (n - 4) // 2, (n - 4) % 2
                g, b = ("ln2_g_2", "ln2_b_2") if second else ("ln1_g_2", "ln1_b_2")
                pool.wait_ge(x_upd, 2 * (n - 3))
                pool.dma_start(lng, a[g][l].partition_broadcast(P)).then_inc(ln_in, 16)
                pool.dma_start(lnb, a[b][l].partition_broadcast(P)).then_inc(ln_in, 16)
                if n == 5:
                    pool.wait_ge(ret_y, 1)
                    pool.dma_start(gnw, a["ret_gn_w_2"][1].partition_broadcast(P)).then_inc(gn_in, 16)
                pool.wait_ge(ln_in, 16 + 32 * (n - 3))
                for t in range(TT):
                    pool.wait_ge(xn_made, 2 * n + t + 1)
                    link(pool.tensor_tensor(x[:, t, :], xn[:, t, :], lng, ALU.mult))
                    pool.tensor_tensor(x[:, t, :], x[:, t, :], lnb, ALU.add).then_inc(x_upd, 1)
            pool.wait_ge(x_upd, 8)
            pool.dma_start(lng, a["ln2_g_2"][1].partition_broadcast(P)).then_inc(ln_in, 16)
            pool.dma_start(lnb, a["ln2_b_2"][1].partition_broadcast(P)).then_inc(ln_in, 16)
            pool.wait_ge(ln_in, 16 + 32 * 4)

        def attention_units(blk, l=0):
            units = []
            if blk == 1:
                for h in range(4):
                    groups = []
                    for g in range(3):
                        hh = 4 * g + h
                        r = slice(64 * (hh % 2), 64 * (hh % 2) + 64)
                        groups.append((q1[r, hh // 2, :], k1[r, hh // 2, :],
                                       [v1[:, t, 64 * hh:64 * hh + 64] for t in range(2)], masks1[:, g, :]))
                    units.append((groups, 0.125, None, (h // 2, 64 * (h % 2))))
                return units
            for h in range(6):
                r = slice(64 * (h % 2), 64 * (h % 2) + 64)
                kv = h // 3
                kk = sk[r, 0 if kv == h % 2 else 1, :]
                units.append(([(sq[r, h // 2, :], kk, [sv[:, t, 64 * kv:64 * kv + 64] for t in range(2)], masks2[:, 0, :])],
                              0.125, 6 * l + h, (2 + h // 2, 64 * (h % 2))))
            for h in range(6):
                units.append(([(qm[0:96, h, :], km[0:96, h, :], [vm[:, t, 64 * h:64 * h + 64] for t in range(2)],
                                masks2[:, 1, :])], float(96 ** -0.5), None, (5 + h // 2, 64 * (h % 2))))
            return units

        SPLIT = (slice(0, 128), slice(128, 384))

        def bases(blk, l):
            return (0, 0) if blk == 1 else (4 + 12 * l, 12 + 12 * l)

        @block.tensor
        def _(pe):
            def split_mm(o, wh, wl, xh, xl, start, stop, weights_first=True):
                prods = ((wh, xh), (wh, xl), (wl, xh)) if weights_first else ((xh, wh), (xh, wl), (xl, wh))
                for i, (st, mv) in enumerate(prods):
                    last = pe.matmul(o, st, mv, start=start and i == 0, stop=stop and i == 2, skip_group_check=True)
                return last

            def norm_tiles(norm, k):
                if norm is not None and k % 2 == 0:
                    pe.wait_ge(u_lo, 4 * norm + k // 2 + 1)

            def stage1(u, ph_banks, norm=None):
                for side in range(2):
                    pe.wait_ge(lo_made, (u + side).count(1))
                    s_ = (u + side).slot
                    for ft in range(2):
                        for k in range(KT):
                            if side == 0 and ft == 0:
                                norm_tiles(norm, k)
                            w = slice(k * 256 + ft * P, k * 256 + ft * P + P)
                            last = split_mm(ps[:, ph_banks + side, ft * T:(ft + 1) * T], whi[:, s_, w], wlo[:, s_, w],
                                            uhi[:, k, :], ulo[:, k, :], k == 0, k == KT - 1)
                    last.then_inc(used, 1)

            def down(u, th, tl, stop=False, done=None):
                s_ = u.slot
                for t in range(TT):
                    for n in range(2):
                        for f in range(2):
                            w = slice(f * D + n * HALF, f * D + (n + 1) * HALF)
                            last = split_mm(ps[:, 2 * t + n, :], whi[:, s_, w], wlo[:, s_, w],
                                            th[f][:, t * P:(t + 1) * P], tl[f][:, t * P:(t + 1) * P],
                                            False, stop and f == 1, weights_first=False)
                    if done is not None and t == 0:
                        last.then_inc(y_done, 1)
                if done is not None:
                    last.then_inc(y_done, 1)
                else:
                    last.then_inc(used, 1)

            def hT(par):
                return ([hhi[:, par, f * T:(f + 1) * T] for f in range(2)], [hlo[:, par, f * T:(f + 1) * T] for f in range(2)])

            def open_y():
                for b in range(4):
                    pe.matmul(ps[:, b, :], zeros16[0:1, 0:P], zeros16[0:1, :], start=True, stop=False, skip_group_check=True)

            def phase(ph, between=None, before_last=None, norm=None):
                if norm is not None:
                    pe.wait_ge(u_lo, 4 * norm + 1)
                    pe.wait_ge(u_f, 4 * norm + 2)
                open_y()
                stage1(Unit(ph.u0), 4, norm)
                if between is not None:
                    between()

                def step(c, u, par):
                    g = ph.g0 + c
                    pe.wait_ge(h_made, g)
                    stage1(u, 4 + 2 * par)
                    pe.wait_ge(h_lo, g)
                    pe.wait_ge(lo_made, (u + 2).count(1))
                    down(u + 2, *hT(1 - par))
                steps(pe, ph, step)
                if before_last is not None:
                    before_last()
                u = Unit(ph.u0 + 3 * ph.n - 1)
                pe.wait_ge(h_lo, ph.g0 + ph.n)
                pe.wait_ge(lo_made, u.count(1))
                down(u, *hT((ph.n - 1) % 2), stop=True, done=True)
                pe.matmul(ps[0:32, 4, 0:1], zeros16[0:1, 0:32], zeros16[0:1, 0:1], start=True, stop=True,
                          skip_group_check=True).then_inc(used, 1)

            def transposes(n):
                for t in range(TT):
                    pe.wait_ge(xn_made, 2 * n + t + 1)
                    for k in range(KT):
                        last = pe.transpose(ps[:, 4 + k // 2, (k % 2) * T + t * P:(k % 2) * T + (t + 1) * P],
                                            xn[:, t, k * P:(k + 1) * P], ident)
                        if t == TT - 1 and k % 2 == 1:
                            last.then_inc(xt_made, 1)

            def proj(u, bank, ft_cols, kt, xh, xl, w_cols, out_rows=None, done=True, norm=None):
                s_ = u.slot
                for i, (c0, wd) in enumerate(ft_cols):
                    for k in range(kt):
                        if i == 0:
                            norm_tiles(norm, k)
                        w = slice(k * w_cols + c0, k * w_cols + c0 + wd)
                        r = out_rows or slice(0, wd)
                        last = split_mm(ps[r, bank, i * T:(i + 1) * T], whi[:, s_, w], wlo[:, s_, w],
                                        xh[:, k, :], xl[:, k, :], k == 0, k == kt - 1)
                if done:
                    last.then_inc(used, 1)
                return last

            def proj_tokens(u, bank, n, kt=KT):
                s_ = u.slot
                for t in range(TT):
                    for k in range(kt):
                        w = slice(k * n, (k + 1) * n)
                        last = split_mm(ps[:, bank, t * n:(t + 1) * n], whi[:, s_, w], wlo[:, s_, w],
                                        uhi[:, k, t * P:(t + 1) * P], ulo[:, k, t * P:(t + 1) * P],
                                        k == 0, k == kt - 1, weights_first=False)
                last.then_inc(used, 1)

            def attention(blk, l=0):
                units = attention_units(blk, l)
                h0, b0 = bases(blk, l)
                g_n = len(units[0][0])
                bufs, late = (pt1, 1) if blk == 1 else (pt2, 2)
                for j in range(-1, len(units) + late):
                    if j + 1 < len(units):
                        groups = units[j + 1][0]
                        for g, (q, k, v, m) in enumerate(groups):
                            n = (j + 1) * g_n + g
                            if n >= 3:
                                pe.wait_ge(sc_in, b0 + n - 2)
                            pe.matmul(ps[:, n % 3, 0:128], q[:, 0:128], k[:, 0:128], start=True, stop=True)
                            pe.matmul(ps[:, n % 3, 128:384], q[:, 128:256], k, start=True, stop=True).then_inc(sc_mm, 1)
                    i = j - 1
                    if 0 <= i < len(units):
                        pe.wait_ge(p_made, h0 + i + 1)
                        for g in range(g_n):
                            n = i * g_n + g
                            if n >= 3:
                                pe.wait_ge(tr_out, b0 + n - 2)
                            src = (sb1 if blk == 1 else sb2)[i % 2][:, g, :]
                            for c in range(3):
                                last = pe.transpose(ps[:, 3 + n % 3, c * P:(c + 1) * P], src[:, c * P:(c + 1) * P], ident)
                            last.then_inc(tr_mm, 1)
                    i = j - late
                    if 0 <= i < len(units):
                        groups, _, _, (tile, r0) = units[i]
                        pe.wait_ge(tr_out, b0 + (i + 1) * g_n)
                        if i >= 2:
                            pe.wait_ge(yo_lo, h0 + i - 1)
                        o = ps[r0:r0 + 64, 6 + i % 2, :]
                        pt = bufs[i % len(bufs)]
                        for g in range(g_n):
                            last = pe.matmul(o[:, 0:P], groups[g][2][0], pt[:, g, 0:P], start=g == 0, stop=g == g_n - 1)
                        for g in range(g_n):
                            pe.matmul(o[:, P:T], groups[g][2][0], pt[:, g, P:2 * P], start=g == 0, stop=False)
                            last = pe.matmul(o[:, P:T], groups[g][2][1], pt[:, g, 2 * P:3 * P], start=False, stop=g == g_n - 1)
                        last.then_inc(pv_mm, 1)

            pe.wait_ge(const_in, 16)
            pe.wait_ge(stack_in, 16 * 18)
            pe.transpose(ps[:, 0, 0:V_N], vstack[0:V_N, :], small[0:V_N, C_IDENT:C_IDENT + V_N]).then_inc(vec_t, 1)
            pe.wait_ge(pos_f, 1)
            pe.matmul(ps[:, 1, 0:T], ones[0:1, :], posf[0:1, :], start=True, stop=True).then_inc(pos_bc, 1)
            pe.wait_ge(ada_sum, 8 * ADA_FIRST)
            for j in range(16):
                last = pe.matmul(ps[:, 2, j:j + 1], acc[:, j * P:(j + 1) * P], ones[:, 0:1], start=True, stop=True)
            last.then_inc(mod_mm, 1)

            def gt_rows(m, half, bank):
                c0 = m * D + half * HALF
                pe.matmul(ps[:, bank, :], ones, acc[:, c0:c0 + HALF], start=True, stop=True).then_inc(mod_mm, 1)

            def mods_before_last():
                pe.wait_ge(ada_sum, 8 * ADA_BLOCKS)
                gt_rows(2, 0, 6)
                gt_rows(2, 1, 7)

            pe.wait_ge(zero_made, 1)
            transposes(0)
            pe.wait_ge(mod_cols, 1)
            phase(ffn1, before_last=mods_before_last, norm=0)
            for j, m in enumerate((3, 4, 6, 7)):
                for c in range(8):
                    last = pe.matmul(ps[:, 4, 8 * j + c:8 * j + c + 1], acc[:, m * D + c * P:m * D + (c + 1) * P],
                                     ones[:, 0:1], start=True, stop=True)
            last.then_inc(mod_mm, 1)
            gt_rows(5, 0, 5)
            pe.wait_ge(gt_out, 1)
            gt_rows(5, 1, 6)
            pe.wait_ge(gt_out, 2)
            gt_rows(8, 0, 7)
            pe.wait_ge(mod_cols, 2)
            gt_rows(8, 1, 4)
            pe.wait_ge(gt_out, 6)
            transposes(1)

            two = [(0, P), (P, P)]

            def rot1(r):
                pe.wait_ge(proj_out, 1 + r + 1)
                if r >= 2:
                    pe.wait_ge(rope_out, r - 1)
                pe.matmul(ps[:, 4 + r % 2, :], rot, qraw1[r % 2], start=True, stop=True).then_inc(rot_mm, 1)

            for i in range(10):
                u = Unit(U_MIX + i)
                pe.wait_ge(lo_made, u.count(1))
                if i >= 4:
                    pe.wait_ge(proj_out, i - 3)
                if i < 7:
                    proj(u, i % 4, two, KT, uhi, ulo, 256, norm=1 if i == 0 else None)
                else:
                    proj_tokens(u, i % 4, 256)
                if 2 <= i < 8:
                    rot1(i - 2)
            pe.wait_ge(pool_d, 1)
            pe.wait_ge(wpool_in, 64)
            for k in range(2):
                for half in range(2):
                    r = slice(64 * half, 64 * half + 64)
                    last = pe.matmul(ps[r, 6, k * T:(k + 1) * T], wpool[r, k, :], ptmp[r, k, 256:512], start=True, stop=True)
            last.then_inc(pool_mm, 1)
            pe.wait_ge(proj_out, 10)
            pe.wait_ge(rope_out, 6)
            pe.wait_ge(pool_lo, 1)
            attention(1)
            pe.wait_ge(yo_lo, 4)
            for j in range(4):
                b0 = 4 * (j % 2)
                if j >= 2:
                    pe.wait_ge(m_made, j - 1)
                for i in range(4):
                    u = Unit(U_MIX + 10 + 4 * j + i)
                    pe.wait_ge(lo_made, u.count(1))
                    if i < 2:
                        proj(u, b0 + i, two, 2, yhi[:, 2 * i:2 * i + 2, :], ylo[:, 2 * i:2 * i + 2, :], 256)
                    else:
                        proj(u, b0 + i, two, KT, uhi, ulo, 256)
            pe.wait_ge(m_made, 4)
            open_y()

            def out_proj(u0, th, tl):
                for j in range(4):
                    u = Unit(u0 + j)
                    pe.wait_ge(lo_made, u.count(1))
                    down(u, [th[:, 2 * j + f, :] for f in range(2)], [tl[:, 2 * j + f, :] for f in range(2)],
                         stop=j == 3, done=True if j == 3 else None)
                pe.matmul(ps[0:32, 4, 0:1], zeros16[0:1, 0:32], zeros16[0:1, 0:1], start=True, stop=True,
                          skip_group_check=True).then_inc(used, 1)
            pe.wait_ge(m_lo, 4)
            out_proj(U_MIX + 26, mhi, mlo)
            transposes(2)
            phase(ffn2, norm=2)
            transposes(3)

            for l in range(LAYERS):
                ul, pb, rb = U_L + N_L * l, 10 + 19 * l, 6 + 6 * l
                def free(i):
                    if i >= 4:
                        pe.wait_ge(proj_out, pb + i - 3)

                def rot2(r, i, rows, mat):
                    pe.wait_ge(proj_out, pb + i + 1)
                    if r >= 2:
                        pe.wait_ge(rope_out, rb + r - 1)
                    n = T if rows.start else HALF
                    pe.matmul(ps[rows, 4 + r % 2, 0:n], mat, qraw2[r % 2][rows, 0:n], start=True, stop=True)\
                        .then_inc(rot_mm, 1)

                def ret_scores(h):
                    r = slice(64 * (h % 2), 64 * (h % 2) + 64)
                    if h == 0:
                        pe.wait_ge(rope_out, rb + 2)
                    if h >= 2:
                        pe.wait_ge(ret_d, 4 * l + h - 1)
                    q, k, b = rqk[r, h // 2, :], rqk[r, 2 + h // 2, :], 6 + h % 2
                    pe.matmul(ps[:, b, 0:T], k[:, 0:P], q, start=True, stop=True)
                    pe.matmul(ps[:, b, T:384], k[:, P:T], q[:, P:T], start=True, stop=True).then_inc(ret_mm, 1)

                def ret_out(h):
                    pe.wait_ge(ret_d, 4 * l + h + 1)
                    d, c = dret[h], slice(64 * h, 64 * h + 64)
                    pe.matmul(ps[:, 5, 64 * h:64 * h + 64], d[:, 0:P], rv[:, 0, c], start=True, stop=True)
                    pe.matmul(ps[:, 5, T + 64 * h:T + 64 * h + 64], d[:, P:T], rv[:, 0, c], start=True, stop=False)
                    pe.matmul(ps[:, 5, T + 64 * h:T + 64 * h + 64], d[:, T:384], rv[:, 1, c], start=False, stop=True)\
                        .then_inc(ret_o, 1)

                for i, kind in enumerate(IN_UNITS):
                    u = Unit(ul + i)
                    pe.wait_ge(lo_made, u.count(1))
                    free(i)
                    if kind in ("ret q", "ret k", "swa q", "swa q k", "latents 01", "latents 34"):
                        proj(u, i % 4, two, KT, uhi, ulo, 256, norm=3 + 2 * l if i == 0 else None)
                    elif kind in ("ret v", "ret gate"):
                        proj_tokens(u, i % 4, 256)
                    elif kind == "swa v":
                        proj_tokens(u, i % 4, 128)
                    elif kind == "latent 2":
                        proj(u, i % 4, [(0, P)], KT, uhi, ulo, 128)
                    else:
                        proj(u, i % 4, [(0, 32)], KT, uhi, ulo, 32, out_rows=slice(64, 96))
                    if i in (1, 2):
                        rot2(i - 1, i - 1, slice(0, P), rot)
                    elif i == 3:
                        ret_scores(0)
                        ret_scores(1)
                    elif i in (4, 5):
                        ret_out(i - 4)
                        ret_scores(i - 2)
                    elif i == 6:
                        pe.wait_ge(sqr_made, 2 * l + 2)
                        pe.wait_ge(ret_d, 4 * l + 3)
                        for b in range(2):
                            n = (3, 2)[b]
                            for k in range(n):
                                last = pe.matmul(ps[:, 6, b * T:(b + 1) * T], ones, sqv[b][:, k, :],
                                                 start=k == 0, stop=k == n - 1)
                        last.then_inc(ss_mm, 1)
                    elif i == 7:
                        ret_out(2)
                        ret_out(3)
                        rot2(2, 6, slice(64, 96), small[64:96, C_ROTM + 64:C_ROTM + 96])
                pe.wait_ge(c_lo, 2 * (l + 1))
                u = Unit(ul + 11)
                pe.wait_ge(lo_made, u.count(1))
                for j in range(3):
                    free(11 + j)
                    proj(u, (11 + j) % 4, [(96 * (2 * j + i), 96) for i in range(2)], 3, chi[:, 0:3, :], clo[:, 0:3, :],
                         576, done=False)
                    pe.matmul(ps[0:32, 6, HALF - 1:HALF], zeros16[0:1, 0:32], zeros16[0:1, 0:1], start=True, stop=True,
                              skip_group_check=True).then_inc(latent_mm, 1)
                    if j == 0:
                        pe.wait_ge(proj_out, pb + 10)
                        pe.wait_ge(rope_out, rb + 3)
                        pe.matmul(ps[0:64, 4, 0:T], ident[:, 64:128], sk[:, 0, :], start=True, stop=True)
                        pe.matmul(ps[64:128, 4, 0:T], ident[:, 0:64], sk[:, 0, :], start=True, stop=True).then_inc(swap_mm, 1)
                    if j == 1:
                        pe.wait_ge(ret_y, l + 1)
                        for t in range(TT):
                            for f in range(2):
                                last = pe.transpose(ps[:, 7, f * T + t * P:f * T + (t + 1) * P],
                                                    oret[:, t * T + f * P:t * T + (f + 1) * P], ident)
                        last.then_inc(ret_t, 1)
                    if j == 2:
                        pe.wait_ge(swap_out, l + 1)
                    if j >= 1:
                        rot2(2 + j, 10 + j, slice(0, 96), small[0:96, C_ROTM:C_ROTM + 96])
                pe.matmul(ps[0:32, 6, HALF - 1:HALF], zeros16[0:1, 0:32], zeros16[0:1, 0:1], start=True, stop=True,
                          skip_group_check=True).then_inc(used, 1)
                rot2(5, 13, slice(0, 96), small[0:96, C_ROTM:C_ROTM + 96])
                u = Unit(ul + 12)
                pe.wait_ge(lo_made, u.count(1))
                for j in range(3):
                    free(14 + j)
                    proj(u, (14 + j) % 4, [(128 * (2 * j + i), 64) for i in range(2)], 2, chi[:, 3:5, :], clo[:, 3:5, :],
                         768, done=False).then_inc(latent_mm, 1)
                for t in range(TT):
                    free(17 + t)
                    for k in range(2):
                        wv = [w[:, u.slot, k * 768:(k + 1) * 768].rearrange("p (h n) -> p h n", h=6)[:, :, 64:128]
                              for w in (whi, wlo)]
                        last = split_mm(ps[:, (17 + t) % 4, 0:384], wv[0], wv[1], chi[:, 3 + k, t * P:(t + 1) * P],
                                        clo[:, 3 + k, t * P:(t + 1) * P], k == 0, k == 1, weights_first=False)
                    last.then_inc(latent_mm, 1)
                pe.matmul(ps[0:32, 6, HALF - 1:HALF], zeros16[0:1, 0:32], zeros16[0:1, 0:1], start=True, stop=True,
                          skip_group_check=True).then_inc(used, 1)
                pe.wait_ge(proj_out, pb + 19)
                pe.wait_ge(rope_out, rb + 6)
                pe.wait_ge(ret_lo, l + 1)
                attention(2, l)
                pe.wait_ge(yo_lo, 4 + 12 * (l + 1))
                open_y()
                out_proj(ul + 13, mixhi, mixlo)
                transposes(4 + 2 * l)

                pe.wait_ge(u_lo, 20 + 8 * l)
                u = Unit(ul + 17)
                pe.wait_ge(lo_made, u.count(1))
                for t in range(TT):
                    for k in range(KT):
                        w = slice(16 * k, 16 * k + 16)
                        last = split_mm(ps[:, 7, 16 * t:16 * t + 16], whi[:, u.slot, w], wlo[:, u.slot, w],
                                        uhi[:, k, t * P:(t + 1) * P], ulo[:, k, t * P:(t + 1) * P],
                                        k == 0, k == KT - 1, weights_first=False)
                last.then_inc(used, 1)

                pe.wait_ge(gate_made, l + 1)
                pe.wait_ge(slots_in, 16)
                g0, g1 = rr[:, 5, 0:4], rr[:, 5, 4:8]
                pe.matmul(ps[:, 6, 0:4], earlier, g0, start=True, stop=True)
                pe.matmul(ps[:, 6, 4:8], ones, g0, start=True, stop=False)
                pe.matmul(ps[:, 6, 4:8], earlier, g1, start=False, stop=True)
                pe.matmul(ps[:, 6, 8:12], ones, g0, start=True, stop=False)
                pe.matmul(ps[:, 6, 8:12], ones, g1, start=False, stop=True).then_inc(rank_mm, 1)

                def gates():
                    for t in range(TT):
                        last = pe.transpose(ps[0:16, 6, t * P:(t + 1) * P], rr[:, 19, 16 * t:16 * t + 16], ident)
                    last.then_inc(gate_t[l], 1)
                    pe.wait_ge(gateT_out[l], 1)
                    for e in range(0, EXPERTS, 2):
                        b = 6 + (e // 2) % 2
                        if e >= 4:
                            pe.wait_ge(gb_out[l], e // 2 - 1)
                        for i in range(2):
                            sel = small[0:16, C_IDENT + e + i:C_IDENT + e + i + 1].to_broadcast([16, P])
                            last = pe.matmul(ps[:, b, i * T:(i + 1) * T], sel, gatesT[0:16, :], start=True, stop=True)
                        last.then_inc(gb_mm[l], 1)
                    pe.wait_ge(gb_out[l], 8)

                def slots_setup():
                    pe.wait_ge(p16_made[l], 1)
                    for g in range(4):
                        for t in range(TT):
                            last = pe.transpose(ps[:, 4, :].bitcast(F16)[:, (2 * g + t) * P:(2 * g + t + 1) * P],
                                                p16[:, t, g * P:(g + 1) * P], ident16)
                    last.then_inc(pT_mm[l], 1)
                    for t in range(TT):
                        last = pe.matmul(ps[0:16, 7, :], rr[:, 19, 16 * t:16 * t + 16], p32[:, t, :],
                                         start=t == 0, stop=t == TT - 1)
                    last.then_inc(gs_mm[l], 1)

                def gather(g):
                    if g >= 2:
                        pe.wait_ge(ys_lo[l], 2 * (g - 1))
                    for k in range(KT):
                        o = ps[:, 2 * (g % 2) + k // 4, (k % 4) * P:(k % 4 + 1) * P]
                        for t in range(TT):
                            for i, v in enumerate((xh, xl)):
                                last = pe.matmul(o, v[:, t, k * P:(k + 1) * P], p16[:, t, g * P:(g + 1) * P],
                                                 start=t == 0 and i == 0, stop=t == 1 and i == 1)
                        if k % 4 == 3:
                            last.then_inc(ga_mm[l], 1)

                def slot_gates():
                    pe.wait_ge(gs_out[l], 1)
                    pe.wait_ge(pT_out[l], 1)
                    for g in range(4):
                        b = 6 + g % 2
                        if g >= 2:
                            pe.wait_ge(gbs_out[l], g - 1)
                        for i in range(4):
                            e = 4 * g + i
                            sel = small[0:16, C_IDENT + e:C_IDENT + e + 1].to_broadcast([16, P])
                            last = pe.matmul(ps[:, b, i * P:(i + 1) * P], sel, gslots[0:16, g * P:(g + 1) * P],
                                             start=True, stop=True)
                        last.then_inc(gbs_mm[l], 1)

                def slots_stage1(u, c):
                    g, b0 = c // 4, 4 + 2 * (c % 2)
                    for side in range(2):
                        pe.wait_ge(lo_made, (u + side).count(1))
                        s_ = (u + side).slot
                        for ft in range(2):
                            for k in range(KT):
                                w = slice(k * 256 + ft * P, k * 256 + ft * P + P)
                                xs = slice((g % 2) * P, (g % 2 + 1) * P)
                                last = split_mm(ps[:, b0 + side, ft * P:(ft + 1) * P], whi[:, s_, w], wlo[:, s_, w],
                                                uhi[:, k, xs], ulo[:, k, xs], k == 0, k == KT - 1)
                        last.then_inc(used, 1)

                def slots_down(u, c):
                    pe.wait_ge(h_lo, moe[l].g0 + c + 1)
                    pe.wait_ge(lo_made, u.count(1))
                    g, par, s_ = c // 4, c % 2, u.slot
                    for n in range(2):
                        for f in range(2):
                            w = slice(f * D + n * HALF, f * D + (n + 1) * HALF)
                            last = split_mm(ps[:, 2 * (g % 2) + n, :], whi[:, s_, w], wlo[:, s_, w],
                                            hhi[:, par, f * P:(f + 1) * P], hlo[:, par, f * P:(f + 1) * P],
                                            c % 4 == 0 and f == 0, c % 4 == 3 and f == 1, weights_first=False)
                    last.then_inc(used, 1)

                def sparse(ph):
                    slots_setup()
                    pe.wait_ge(x_lo, l + 1)
                    gather(0)
                    slot_gates()
                    pe.wait_ge(ga_lo[l], 4)
                    pe.wait_ge(gbs_out[l], 4)
                    slots_stage1(Unit(ph.u0), 0)
                    for c in range(1, ph.n):
                        u = Unit(ph.u0 + 3 * c - 1)
                        pe.wait_ge(h_made, ph.g0 + c)
                        if c % 4 == 0:
                            pe.wait_ge(ga_lo[l], c + 4)
                        slots_stage1(u, c)
                        slots_down(u + 2, c - 1)
                        if c % 4 == 2 and c < 12:
                            gather(c // 4 + 1)
                    slots_down(Unit(ph.u0 + 3 * ph.n - 1), ph.n - 1)
                    pe.wait_ge(ys_lo[l], 8)
                    for t in range(TT):
                        for n in range(2):
                            for g in range(4):
                                for i, v in enumerate((ysh, ysl)):
                                    last = pe.matmul(ps[:, 2 * t + n, :], pT16[:, g, t * P:(t + 1) * P],
                                                     v[g][:, n * HALF:(n + 1) * HALF], start=g == 0 and i == 0,
                                                     stop=g == 3 and i == 1)
                        last.then_inc(y_done, 1)

                pe.wait_ge(rank_out, l + 1)
                count = pe.value_load(rr[0:1, 17, 0:1].bitcast(I32))
                with pe.If(count > P):
                    phase(moe[l], between=gates)
                with pe.Else():
                    sparse(moe[l])
                if l < LAYERS - 1:
                    transposes(5 + 2 * l)

        @block.scalar
        def _(act):
            n_step = [0]

            def link(ins):
                n_step[0] += 1
                ins.then_inc(act_step, 1)
                act.wait_ge(act_step, n_step[0])

            def ahead(u, n=1):
                for i in range(n):
                    hi_part(act, u + (AHEAD + i))

            def rms(n):
                for t in range(TT):
                    act.wait_ge(*((x_in, 32) if n == 0 else (x_new, 2 * (n - 1) + t + 1)))
                    link(act.activation(xn[:, t, :], x[:, t, :], ACT.Square, accum_out=stat[:, t:t + 1]))
                    act.activation(stat[:, 2 + t:3 + t], stat[:, t:t + 1], ACT.Sqrt, scale=1.0 / D,
                                   bias=small[:, C_EPS:C_EPS + 1]).then_inc(rms_made, 1)

            def layer_std(n):
                for t in range(TT):
                    act.wait_ge(var_made, 2 * (n - 4) + t + 1)
                    act.activation(stat[:, 2 + t:3 + t], stat[:, 9 + 4 * t:10 + 4 * t], ACT.Sqrt, scale=1.0,
                                   bias=small[:, C_EPSLN + 1:C_EPSLN + 2]).then_inc(rms_made, 1)

            def norm_out(n, acols, bcols):
                for kp in range(4):
                    act.wait_ge(xt_made, 4 * n + kp + 1)
                    if kp >= 2:
                        act.wait_ge(u_lo, 4 * n + kp - 1)
                    for i in range(2):
                        k = 2 * kp + i
                        last = act.activation(hreg[:, 512 * (kp % 2) + i * T:512 * (kp % 2) + (i + 1) * T],
                                              ps[:, 4 + kp, i * T:(i + 1) * T], ACT.Identity,
                                              scale=acols[:, k:k + 1], bias=bcols[:, k:k + 1])
                    last.then_inc(u_f, 1)

            def chunk(u_b, g, par):
                act.wait_ge(used, u_b.count(1))
                act.activation(s_act, ps[:, 4 + 2 * par, :], ACT.Silu, scale=1.0 / S).then_inc(silu_made, 1)
                act.wait_ge(h_made, g + 2)
                act.activation(hhi[:, par, :], h_f32, ACT.Copy).then_inc(h_hi, 1)

            def phase(ph, between=None):
                ahead(Unit(ph.u0), 2)
                chunk(Unit(ph.u0 + 1), ph.g0, 0) if between is None else between()

                def step(c, u, par):
                    ahead(u, 3)
                    chunk(u + 1, ph.g0 + c, par)
                steps(act, ph, step)
                ahead(Unit(ph.u0 + 3 * ph.n - 1))

            def attention(blk, l=0):
                units = attention_units(blk, l)
                h0, b0 = bases(blk, l)
                g_n = len(units[0][0])
                scores, bufs = (sb1, pt1) if blk == 1 else (sb2, pt2)
                yh = yhi if blk == 1 else mixhi
                late = 1 if blk == 1 else 2
                for j in range(len(units) + late + 1):
                    if j < len(units):
                        act.wait_ge(max_made, h0 + j + 1)
                        st = stat[:, 20 + 10 * (j % 2):30 + 10 * (j % 2)]
                        for t in range(2):
                            s_ = scores[j % 2][:, :, SPLIT[t]]
                            last = act.activation(s_, s_, ACT.Exp, bias=st[:, 2 + t:3 + t], accum_out=st[:, 4 + t:5 + t])
                        if units[j][2] is not None:
                            for t in range(2):
                                last = act.activation(st[:, 6 + t:7 + t], sinks[:, units[j][2]:units[j][2] + 1], ACT.Exp,
                                                      bias=st[:, 2 + t:3 + t])
                        last.then_inc(exp_made, 1)
                    i = j - late - 1
                    if 0 <= i < len(units):
                        tile, r0 = units[i][3]
                        act.wait_ge(pv_mm, h0 + i + 1)
                        if blk == 1:
                            tile += 2
                        act.activation(yh[r0:r0 + 64, tile, :], ps[r0:r0 + 64, 6 + i % 2, 0:T], ACT.Copy, scale=SX)\
                            .then_inc(yo_hi, 1)
                    i = j - 1
                    if 0 <= i < len(units):
                        if i >= len(bufs):
                            act.wait_ge(pv_mm, h0 + i - len(bufs) + 1)
                        for g in range(g_n):
                            n = i * g_n + g
                            act.wait_ge(tr_mm, b0 + n + 1)
                            act.activation(bufs[i % len(bufs)][:, g, :], ps[:, 3 + n % 3, 0:384], ACT.Copy).then_inc(tr_out, 1)

            ada_block(act, 0)
            act.wait_ge(vec_out, 1)
            act.activation(cond[:, :], vec[:, V_C:V_C + 8], ACT.Silu).then_inc(cond_made, 1)
            ada_block(act, 1)
            rms(0)
            ada_block(act, 2)
            act.wait_ge(ang_made, 1)
            act.activation(sinb[:, :], tr[0], ACT.Sin)
            act.activation(cosb[:, :], tr[1], ACT.Sin).then_inc(sin_made, 1)
            hi_part(act, Unit(0))
            act.wait_ge(mod_cols, 1)
            norm_out(0, acol[:, 0, :], adacols[:, 0:8])
            for i in range(1, AHEAD):
                hi_part(act, Unit(i))
            phase(ffn1)
            for i, (m, half) in enumerate(((0, 0), (0, 1), (1, 0), (1, 1), (2, 0), (2, 1))):
                act.wait_ge(mod_mm, (2, 3, 5, 6, 7, 8)[i])
                act.activation(gt[:, m, half * HALF:(half + 1) * HALF], ps[:, (6, 7, 5, 6, 7, 4)[i], :], ACT.Copy,
                               scale=(0.5, 1.0, 0.5)[m] / S).then_inc(gt_out, 1)
            rms(1)
            act.wait_ge(mod_cols, 2)
            norm_out(1, acol[:, 1, :], adacols[:, 8:16])

            for i in range(10):
                u = Unit(U_MIX + i)
                ahead(u)
                act.wait_ge(used, u.count(1))
                dst, shape = None, None
                if i == 0:
                    act.wait_ge(h_lo, FFN_CHUNKS)
                    dst = pT.rearrange("p k n -> p (k n)")
                elif i < 7:
                    r = i - 1
                    if r >= 2:
                        act.wait_ge(rope_out, r - 1)
                    dst = qraw1[r % 2]
                if dst is not None:
                    act.activation(dst, ps[:, i % 4, :], ACT.Copy, scale=1.0 / S).then_inc(proj_out, 1)
                else:
                    c = 256 * (i - 7)
                    act.activation(v1[:, :, c:c + 256], ps[:, i % 4, :].rearrange("p (t n) -> p t n", t=2), ACT.Copy,
                                   scale=1.0 / S).then_inc(proj_out, 1)
            act.wait_ge(pool_mm, 1)
            for k in range(2):
                last = act.activation(yhi[:, k, :], ps[:, 6, k * T:(k + 1) * T], ACT.Copy, scale=vec8[:, V_PS + k:V_PS + k + 1])
            last.then_inc(pool_hi, 1)
            attention(1)
            for j in range(4):
                for i in range(4):
                    ahead(Unit(U_MIX + 10 + 4 * j + i))
                act.wait_ge(used, Unit(U_MIX + 10 + 4 * j + 3).count(1))
                if j:
                    act.wait_ge(m_made, j)
                b0 = 4 * (j % 2)
                for i in range(2):
                    act.activation(gtmp[i], ps[:, b0 + 2 + i, :], ACT.Sigmoid, scale=1.0 / S).then_inc(sig_made, 1)
                act.wait_ge(m_made, j + 1)
                act.activation(mhi[:, 2 * j:2 * j + 2, :], gtmp[2].rearrange("p (k n) -> p k n", k=2), ACT.Copy).then_inc(m_hi, 1)
            for j in range(4):
                ahead(Unit(U_MIX + 26 + j))
            rms(2)
            norm_out(2, acol[:, 2, :], adacols[:, 16:24])
            phase(ffn2)
            rms(3)
            norm_out(3, vec8[:, V_GF:V_GF + 8], zero8[:, :])

            for l in range(LAYERS):
                ul, pb, rb = U_L + N_L * l, 10 + 19 * l, 6 + 6 * l
                if l:
                    norm_out(5, vec8[:, V_LN2G:V_LN2G + 8], vec8[:, V_LN2B:V_LN2B + 8])

                def leave(i, dst, src, func=ACT.Copy):
                    act.activation(dst, src, func, scale=1.0 / S).then_inc(proj_out, 1)

                for i, kind in enumerate(IN_UNITS):
                    u = Unit(ul + i)
                    ahead(u)
                    act.wait_ge(used, u.count(1))
                    b = ps[:, i % 4, :]
                    two_tiles = b.rearrange("p (t n) -> p t n", t=2)
                    if kind in ("ret q", "ret k"):
                        leave(i, qraw2[i % 2], b)
                    elif kind == "ret v":
                        leave(i, rv, two_tiles)
                    elif kind == "ret gate":
                        leave(i, rg, two_tiles, ACT.Silu)
                        act.wait_ge(ss_mm, l + 1)
                        for j, n in enumerate((384, 256)):
                            act.activation(rstdb[:, j, :], ps[:, 6, j * T:(j + 1) * T], ACT.Sqrt, scale=1.0 / n,
                                           bias=small[:, C_EPS:C_EPS + 1]).then_inc(std_made, 1)
                    elif kind == "swa q":
                        leave(i, sq[:, 0:2, :], two_tiles)
                        for j, ks in enumerate((slice(0, 3), slice(3, 5))):
                            act.wait_ge(cn_made, 2 * l + j + 1)
                            act.activation(chi[:, ks, :], cT[:, ks, :], ACT.Copy).then_inc(c_hi, 1)
                    elif kind == "swa q k":
                        act.activation(sq[:, 2, :], b[:, 0:T], ACT.Copy, scale=1.0 / S)
                        leave(i, sk[:, 0, :], b[:, T:2 * T])
                        act.wait_ge(ret_oc, l + 1)
                        act.activation(osq, ocen, ACT.Square).then_inc(ret_std, 1)
                    elif kind == "swa v":
                        leave(i, sv, b[:, 0:256].rearrange("p (t n) -> p t n", t=2))
                        act.wait_ge(ret_var, l + 1)
                        act.activation(stat[:, 48:56], stat[:, 40:48], ACT.Sqrt, scale=1.0 / 64,
                                       bias=small[:, C_EPSLN:C_EPSLN + 1]).then_inc(ret_std, 1)
                    elif kind == "latents 01":
                        leave(i, cT[:, 0:2, :], two_tiles)
                    elif kind == "latent 2":
                        leave(i, cT[:, 2, :], b[:, 0:T])
                        act.wait_ge(proj_out, pb + i + 1)
                        act.activation(sqv[0], cT[:, 0:3, :], ACT.Square).then_inc(sqr_made, 1)
                    elif kind == "latents 34":
                        leave(i, cT[:, 3:5, :], two_tiles)
                        act.wait_ge(proj_out, pb + i + 1)
                        act.activation(sqv[1], cT[:, 3:5, :], ACT.Square).then_inc(sqr_made, 1)
                    else:
                        act.wait_ge(rope_out, rb + 1)
                        leave(i, qraw2[0][64:96, 0:T], b[64:96, 0:T])
                ahead(Unit(ul + 11))
                for j in range(3):
                    act.wait_ge(latent_mm, 8 * l + j + 1)
                    act.wait_ge(rope_out, rb + 2 + j)
                    leave(11 + j, qraw2[(3 + j) % 2][0:96, :], ps[0:96, (11 + j) % 4, :])
                    if j == 0:
                        act.wait_ge(swap_mm, l + 1)
                        act.activation(sk[:, 1, :], ps[:, 4, 0:T], ACT.Copy).then_inc(swap_out, 1)
                act.wait_ge(ret_t, l + 1)
                act.activation(mixhi[:, 0:2, :], ps[:, 7, :].rearrange("p (k n) -> p k n", k=2), ACT.Copy, scale=SX)\
                    .then_inc(ret_hi, 1)
                act.wait_ge(rope_out, rb + 3)
                act.activation(km[64:96, :, :], kro[64:96, :].unsqueeze(1).to_broadcast([32, 6, T]), ACT.Copy).then_inc(km_rope, 1)
                ahead(Unit(ul + 12))
                for j in range(3):
                    act.wait_ge(latent_mm, 8 * l + 4 + j)
                    leave(14 + j, km[0:64, 2 * j:2 * j + 2, :], ps[0:64, (14 + j) % 4, :].rearrange("p (k n) -> p k n", k=2))
                for t in range(TT):
                    act.wait_ge(latent_mm, 8 * l + 7 + t)
                    leave(17 + t, vm[:, t, :], ps[:, (17 + t) % 4, 0:384])
                attention(2, l)
                for j in range(4):
                    ahead(Unit(ul + 13 + j))
                n = 4 + 2 * l
                layer_std(n)
                norm_out(n, vec8[:, V_LN1G + 8 * l:V_LN1G + 8 * l + 8], vec8[:, V_LN1B + 8 * l:V_LN1B + 8 * l + 8])
                ahead(Unit(ul + 17))
                act.wait_ge(used, Unit(ul + 17).count(1))
                act.activation(rr[:, 0, :], ps[:, 7, 0:32], ACT.Sigmoid, scale=1.0 / S).then_inc(router_sig, 1)

                def gates():
                    act.wait_ge(gate_t[l], 1)
                    act.activation(gatesT[0:16, :], ps[0:16, 6, 0:T], ACT.Copy).then_inc(gateT_out[l], 1)
                    for e in range(0, EXPERTS, 2):
                        act.wait_ge(gb_mm[l], e // 2 + 1)
                        act.activation(gb[:, e:e + 2, :], ps[:, 6 + (e // 2) % 2, :].rearrange("p (k n) -> p k n", k=2),
                                       ACT.Copy).then_inc(gb_out[l], 1)
                    chunk(Unit(moe[l].u0 + 1), moe[l].g0, 0)

                def gather(g):
                    for kp in range(4):
                        if kp % 2 == 0:
                            act.wait_ge(ga_mm[l], 2 * g + kp // 2 + 1)
                        if 4 * g + kp >= 2:
                            act.wait_ge(ga_lo[l], 4 * g + kp - 1)
                        for i in range(2):
                            k = 2 * kp + i
                            last = act.activation(uq4[kp % 2][:, i, :],
                                                  ps[:, 2 * (g % 2) + k // 4, (k % 4) * P:(k % 4 + 1) * P], ACT.Identity,
                                                  scale=vec[:, V_LN1G + 8 * l + k:V_LN1G + 8 * l + k + 1],
                                                  bias=vec8[:, V_LN1B + 8 * l + k:V_LN1B + 8 * l + k + 1])
                        last.then_inc(ga_f[l], 1)

                def slots_chunk(c):
                    g, b0 = moe[l].g0 + c, 4 + 2 * (c % 2)
                    u_b = Unit(moe[l].u0 + (1 if c == 0 else 3 * c))
                    act.wait_ge(used, u_b.count(1))
                    act.activation(s_act[:, 0:T], ps[:, b0, 0:T], ACT.Silu, scale=1.0 / S).then_inc(silu_made, 1)
                    act.wait_ge(h_made, g + 2)
                    act.activation(hhi[:, c % 2, 0:T], h_f32[:, 0:T], ACT.Copy).then_inc(h_hi, 1)

                def group_out(g):
                    act.wait_ge(used, Unit(moe[l].u0 + min(12 * g + 13, 47)).count(1))
                    for n in range(2):
                        if g == 3:
                            act.wait_ge(gs_mm[l], 1)
                        act.activation(ysh[g][:, n * HALF:(n + 1) * HALF], ps[:, 2 * (g % 2) + n, :], ACT.Copy,
                                       scale=SX / S).then_inc(ys_hi[l], 1)

                def sparse(ph):
                    act.wait_ge(pT_mm[l], 1)
                    act.activation(pT16.rearrange("p g n -> p (g n)"), ps[:, 4, :].bitcast(F16), ACT.Copy, scale=S / SX)\
                        .then_inc(pT_out[l], 1)
                    act.wait_ge(gs_mm[l], 1)
                    act.activation(gslots[0:16, :], ps[0:16, 7, :], ACT.Copy).then_inc(gs_out[l], 1)
                    gather(0)
                    for g in range(4):
                        act.wait_ge(gbs_mm[l], g + 1)
                        act.activation(gbs[:, 4 * g:4 * g + 4, :], ps[:, 6 + g % 2, :].rearrange("p (k n) -> p k n", k=4),
                                       ACT.Copy).then_inc(gbs_out[l], 1)
                    ahead(Unit(ph.u0), 2)
                    slots_chunk(0)
                    for c in range(1, ph.n):
                        ahead(Unit(ph.u0 + 3 * c - 1), 3)
                        slots_chunk(c)
                        if c % 4 == 2 and c < 12:
                            gather(c // 4 + 1)
                        if c % 4 == 0:
                            group_out(c // 4 - 1)
                    ahead(Unit(ph.u0 + 3 * ph.n - 1))
                    group_out(3)

                act.wait_ge(xn_made, 2 * n + 2)
                act.activation(xh, xn[:, :, :], ACT.Copy, scale=SX).then_inc(x_hi, 1)
                act.wait_ge(rank_out, l + 1)
                count = act.value_load(rr[0:1, 17, 0:1].bitcast(I32))
                with act.If(count > P):
                    phase(moe[l], between=gates)
                with act.Else():
                    sparse(moe[l])
                layer_std(n + 1)

        @block.vector
        def _(dve):
            n_step = [0]

            def link(ins):
                n_step[0] += 1
                ins.then_inc(dve_step, 1)
                dve.wait_ge(dve_step, n_step[0])

            def ahead(u, n=1):
                for i in range(n):
                    lo_part(dve, u + (AHEAD + i))

            def new_x(n):
                gate = gt[:, n - 1, :]
                dve.wait_ge(gt_out, 2 * n)
                for t in range(TT):
                    dve.wait_ge(y_done, 2 * (n - 1) + t + 1)
                    for hf in range(2):
                        c = slice(hf * HALF, (hf + 1) * HALF)
                        link(dve.tensor_tensor(xn[:, t, c], ps[:, 2 * t + hf, :], gate[:, c], ALU.mult))
                    dve.tensor_tensor(x[:, t, :], x[:, t, :], xn[:, t, :], ALU.add).then_inc(x_new, 1)

            def rms_xn(n):
                for t in range(TT):
                    dve.wait_ge(rms_made, 2 * n + t + 1)
                    link(dve.reciprocal(stat[:, 4 + t:5 + t], stat[:, 2 + t:3 + t]))
                    dve.tensor_scalar(xn[:, t, :], x[:, t, :], stat[:, 4 + t:5 + t], None, ALU.mult).then_inc(xn_made, 1)

            def layer_xn(n):
                for t in range(TT):
                    dve.wait_ge(y_done, 2 * (n - 1) + t + 1)
                    dve.wait_ge(x_upd, 2 * (n - 4) + t + 1)
                    for hf in range(2):
                        c = slice(hf * HALF, (hf + 1) * HALF)
                        link(dve.scalar_tensor_tensor(out=x[:, t, c], in0=x[:, t, c], scalar=S * ALPHA,
                                                      in1=ps[:, 2 * t + hf, :], op0=ALU.mult, op1=ALU.add))
                        link(dve.bn_stats(bnst[:, 6 * hf:6 * hf + 6], x[:, t, c]))
                    dve.bn_aggr(stat[:, 8 + 4 * t:10 + 4 * t], bnst).then_inc(var_made, 1)
                    dve.wait_ge(var_made, 2 * (n - 4) + t + 1)
                for t in range(TT):
                    dve.wait_ge(rms_made, 2 * n + t + 1)
                    link(dve.reciprocal(stat[:, 4 + t:5 + t], stat[:, 2 + t:3 + t]))
                    dve.tensor_scalar(xn[:, t, :], x[:, t, :], stat[:, 8 + 4 * t:9 + 4 * t], stat[:, 4 + t:5 + t],
                                      ALU.subtract, ALU.mult).then_inc(xn_made, 1)

            def norm_split(n):
                for kp in range(4):
                    dve.wait_ge(u_f, 4 * n + kp + 1)
                    uf = hreg[:, 512 * (kp % 2):512 * (kp % 2) + 512].rearrange("p (k n) -> p k n", k=2)
                    dve.tensor_copy(uhi[:, 2 * kp:2 * kp + 2, :], uf).then_inc(u_hi, 1)
                    dve.wait_ge(u_hi, 4 * n + kp + 1)
                    dve.tensor_tensor(ulo[:, 2 * kp:2 * kp + 2, :], uf, uhi[:, 2 * kp:2 * kp + 2, :], ALU.subtract)\
                        .then_inc(u_lo, 1)

            def chunk(ph, c, g, par):
                dve.wait_ge(silu_made, g + 1)
                if not (isinstance(g, int) and g == 0):
                    dve.wait_ge(h_lo, g)
                if ph.moe:
                    link_free = dve.scalar_tensor_tensor(out=h_f32, in0=ps[:, 5 + 2 * par, :], scalar=SX / S, in1=s_act,
                                                         op0=ALU.mult, op1=ALU.mult)
                    link_free.then_inc(m_moe, 1)
                    dve.wait_ge(m_moe, g - 2 * FFN_CHUNKS + 1)
                    gate = gb[:, c, :] if isinstance(c, int) else gb[:, bass.ds(c, 1), :].rearrange("p a n -> p (a n)")
                    hv = h_f32.rearrange("p (k n) -> p k n", k=2)
                    dve.tensor_tensor(hv, hv, gate.unsqueeze(1).to_broadcast([P, 2, T]), ALU.mult).then_inc(h_made, 1)
                else:
                    dve.scalar_tensor_tensor(out=h_f32, in0=ps[:, 5 + 2 * par, :], scalar=SX / S, in1=s_act,
                                             op0=ALU.mult, op1=ALU.mult).then_inc(h_made, 1)

            def chunk_lo(g, par):
                dve.wait_ge(h_hi, g + 1)
                dve.tensor_tensor(hlo[:, par, :], h_f32, hhi[:, par, :], ALU.subtract).then_inc(h_lo, 1)

            def ada_sums(b, k0, k1, first=False):
                for k in range(k0, k1):
                    if k % 2 == 0 and first:
                        dve.wait_ge(ada_in[k // 2], 16 * b + 16)
                    elif k % 2 == 0:
                        dve.wait_ge(ada_late[k // 2], 16 * (b - ADA_FIRST) + 16)
                    if not (isinstance(b, int) and b == 0 and k == 0):
                        dve.wait_ge(ada_sum, 8 * b + k)
                    v = acc[:, bass.ds(b * ADA_BLOCK, ADA_BLOCK)]
                    dve.scalar_tensor_tensor(out=v, in0=aring[:, k // 2, k % 2, :], scalar=cond[:, k:k + 1], in1=v,
                                             op0=ALU.mult, op1=ALU.add).then_inc(ada_sum, 1)

            def phase(ph, between=None):
                ahead(Unit(ph.u0), 2)
                if between is not None:
                    between()
                chunk(ph, 0, ph.g0, 0)
                chunk_lo(ph.g0, 0)

                def step(c, u, par):
                    ahead(u, 3)
                    ada = ph.ada and not (isinstance(c, int) and c > ADA_BLOCKS - ADA_FIRST)
                    if ada:
                        ada_sums(c + (ADA_FIRST - 1), 0, 4)
                    chunk(ph, c, ph.g0 + c, par)
                    chunk_lo(ph.g0 + c, par)
                    if ada:
                        ada_sums(c + (ADA_FIRST - 1), 4, 8)
                steps(dve, ph, step)
                ahead(Unit(ph.u0 + 3 * ph.n - 1))

            def rope(r, base, rows, cos, sin, raw_pair, tmp, dst, k):
                dve.wait_ge(rot_mm, base + r + 1)
                n = k * T

                def v3(v):
                    return v[rows, 0:n].rearrange("p (k n) -> p k n", k=k)
                cb, sbc = (v[rows, :].unsqueeze(1).to_broadcast([rows.stop - rows.start, k, T]) for v in (cos, sin))
                dve.tensor_tensor(v3(tmp[0]), v3(ps[:, 4 + r % 2, :]), sbc, ALU.mult).then_inc(dve_step, 1)
                n_step[0] += 1
                link(dve.tensor_tensor(v3(tmp[1]), v3(raw_pair), cb, ALU.mult))
                dve.tensor_tensor(dst, v3(tmp[0]), v3(tmp[1]), ALU.add).then_inc(rope_out, 1)
                dve.wait_ge(rope_out, base + r + 1)

            def attention(blk, l=0):
                units = attention_units(blk, l)
                h0, b0 = bases(blk, l)
                g_n = len(units[0][0])
                scores = sb1 if blk == 1 else sb2
                yh, yl = (yhi, ylo) if blk == 1 else (mixhi, mixlo)
                late = 1 if blk == 1 else 2
                for j in range(len(units) + late + 1):
                    if j < len(units):
                        groups, scale, sink, _ = units[j]
                        st = stat[:, 20 + 10 * (j % 2):30 + 10 * (j % 2)]
                        if j >= 2:
                            dve.wait_ge(tr_mm, b0 + (j - 1) * g_n)
                        for g in range(g_n):
                            n = j * g_n + g
                            dve.wait_ge(sc_mm, b0 + n + 1)
                            dve.scalar_tensor_tensor(out=scores[j % 2][:, g, :], in0=ps[:, n % 3, 0:384], scalar=scale,
                                                     in1=groups[g][3], op0=ALU.mult, op1=ALU.add).then_inc(sc_in, 1)
                        dve.wait_ge(sc_in, b0 + (j + 1) * g_n)
                        for t in range(2):
                            ins = dve.tensor_reduce(st[:, t:t + 1], scores[j % 2][:, :, SPLIT[t]],
                                                    AX.XY if g_n > 1 else AX.X, ALU.max) if g_n > 1 else \
                                dve.tensor_reduce(st[:, t:t + 1], scores[j % 2][:, 0, SPLIT[t]], AX.X, ALU.max)
                            if t == 0:
                                ins.then_inc(dve_step, 1)
                                n_step[0] += 1
                        link(ins)
                        if sink is not None:
                            link(dve.tensor_scalar(st[:, 0:2], st[:, 0:2], sinks[:, sink:sink + 1], None, ALU.max))
                        dve.tensor_scalar(st[:, 2:4], st[:, 0:2], -1.0, None, ALU.mult).then_inc(max_made, 1)
                    i = j - 1
                    if 0 <= i < len(units):
                        st = stat[:, 20 + 10 * (i % 2):30 + 10 * (i % 2)]
                        dve.wait_ge(exp_made, h0 + i + 1)
                        if units[i][2] is not None:
                            link(dve.tensor_tensor(st[:, 4:6], st[:, 4:6], st[:, 6:8], ALU.add))
                        link(dve.reciprocal(st[:, 8:10], st[:, 4:6]))
                        for t in range(2):
                            s_ = scores[i % 2][:, :, SPLIT[t]]
                            ins = dve.tensor_scalar(s_, s_, st[:, 8 + t:9 + t], None, ALU.mult)
                            if t == 0:
                                ins.then_inc(dve_step, 1)
                                n_step[0] += 1
                        ins.then_inc(p_made, 1)
                    i = j - late - 1
                    if 0 <= i < len(units):
                        tile, r0 = units[i][3]
                        if blk == 1:
                            tile += 2
                        dve.wait_ge(yo_hi, h0 + i + 1)
                        dve.scalar_tensor_tensor(out=yl[r0:r0 + 64, tile, :], in0=ps[r0:r0 + 64, 6 + i % 2, 0:T], scalar=SX,
                                                 in1=yh[r0:r0 + 64, tile, :], op0=ALU.mult, op1=ALU.subtract).then_inc(yo_lo, 1)

            dve.memset(zeros16[:, :], 0.0).then_inc(lo_made, RING)
            dve.memset(stat[:, 0:32], 0.0).then_inc(used, RING)
            dve.memset(stat[:, 32:64], 0.0).then_inc(h_made, 1)
            dve.memset(flag[:, 0:1], 0.0).then_inc(hi_made, RING)
            dve.memset(zero8[:, :], 0.0).then_inc(zero_made, 1)
            dve.wait_ge(pos_in, 16)
            dve.tensor_copy(posf[0:1, :], posi[0:1, :]).then_inc(pos_f, 1)
            dve.memset(acc[:, 0:ADA_FIRST * ADA_BLOCK], 0.0).then_inc(acc_zero, 1)
            dve.wait_ge(vec_t, 1)
            dve.tensor_copy(vec[:, :], ps[:, 0, 0:V_N]).then_inc(vec_out, 1)
            dve.wait_ge(vec_out, 1)
            link(dve.tensor_scalar(vec8[:, :], vec[:, :], SX, None, ALU.mult))
            dve.wait_ge(cond_made, 1)
            dve.wait_ge(acc_row, 16)
            ada_sums(0, 0, 8, first=True)
            dve.wait_ge(pos_bc, 1)
            link(dve.tensor_scalar(tr[0], ps[:, 1, 0:T], small[:, C_INVF:C_INVF + 1], None, ALU.mult))
            link(dve.tensor_scalar(tr[1], tr[0], float(1 / TWO_PI), ROUND, ALU.mult, ALU.add))
            link(dve.tensor_scalar(tr[1], tr[1], -ROUND, None, ALU.add))
            for part in (PI_1, PI_2, PI_3):
                link(dve.scalar_tensor_tensor(out=tr[0], in0=tr[1], scalar=-part, in1=tr[0], op0=ALU.mult, op1=ALU.add))
            link(dve.tensor_scalar(tr[1], tr[0], float(np.pi / 2), None, ALU.add))
            link(dve.tensor_scalar(tr[2], tr[1], float(np.pi), -TWO_PI, ALU.is_gt, ALU.mult))
            link(dve.tensor_tensor(tr[1], tr[1], tr[2], ALU.add))
            pi = float(np.nextafter(np.float32(np.pi), np.float32(0)))
            for i in range(2):
                ins = dve.tensor_scalar(tr[i], tr[i], pi, -pi, ALU.min, ALU.max)
                ins.then_inc(dve_step, 1)
                n_step[0] += 1
            dve.wait_ge(dve_step, n_step[0])
            dve.memset(flag[:, 1:2], 0.0).then_inc(ang_made, 1)
            for b in range(1, ADA_FIRST):
                ada_sums(b, 0, 8, first=True)

            def mod_columns(i, ps_sh, ps_sc, g):
                link(dve.tensor_scalar(adacols[:, 8 * i:8 * i + 8], ps_sh, SX, None, ALU.mult))
                link(dve.tensor_scalar(acol[:, i, :], ps_sc, 1.0, None, ALU.add))
                link(dve.tensor_tensor(acol[:, i, :], acol[:, i, :], vec8[:, g:g + 8], ALU.mult))
            dve.wait_ge(sin_made, 1)
            rms_xn(0)
            dve.wait_ge(mod_mm, 1)
            mod_columns(0, ps[:, 2, 0:8], ps[:, 2, 8:16], V_G1)
            dve.memset(flag[:, 2:3], 0.0).then_inc(mod_cols, 1)
            lo_part(dve, Unit(0))
            norm_split(0)
            for i in range(1, AHEAD):
                lo_part(dve, Unit(i))
            phase(ffn1)
            new_x(1)
            dve.wait_ge(mod_mm, 4)
            mod_columns(1, ps[:, 4, 0:8], ps[:, 4, 8:16], V_G2)
            mod_columns(2, ps[:, 4, 16:24], ps[:, 4, 24:32], V_G3)
            dve.memset(flag[:, 2:3], 0.0).then_inc(mod_cols, 1)
            rms_xn(1)
            norm_split(1)

            for i in range(10):
                ahead(Unit(U_MIX + i))
                if 2 <= i < 8:
                    r = i - 2
                    dst = (q1, k1)[r // 3][:, 2 * (r % 3):2 * (r % 3) + 2, :]
                    rope(r, 0, slice(0, P), cosb, sinb, qraw1[r % 2], rtmp1, dst, 2)
            dve.wait_ge(pool_hi, 1)
            for k in range(2):
                ins = dve.scalar_tensor_tensor(out=ylo[:, k, :], in0=ps[:, 6, k * T:(k + 1) * T],
                                               scalar=vec8[:, V_PS + k:V_PS + k + 1], in1=yhi[:, k, :],
                                               op0=ALU.mult, op1=ALU.subtract)
            ins.then_inc(pool_lo, 1)
            dve.wait_ge(b1_in, 32)
            attention(1)
            for j in range(4):
                for i in range(4):
                    ahead(Unit(U_MIX + 10 + 4 * j + i))
                b0 = 4 * (j % 2)
                dve.wait_ge(sig_made, 2 * j + 2)
                if j:
                    dve.wait_ge(m_hi, j)
                for i in range(2):
                    link(dve.scalar_tensor_tensor(out=gtmp[2 + i], in0=ps[:, b0 + i, :], scalar=SX / S, in1=gtmp[i],
                                                  op0=ALU.mult, op1=ALU.mult))
                dve.tensor_tensor(gtmp[2], gtmp[2], gtmp[3], ALU.add).then_inc(m_made, 1)
                dve.wait_ge(m_hi, j + 1)
                dve.tensor_tensor(mlo[:, 2 * j:2 * j + 2, :], gtmp[2].rearrange("p (k n) -> p k n", k=2),
                                  mhi[:, 2 * j:2 * j + 2, :], ALU.subtract).then_inc(m_lo, 1)
                dve.wait_ge(m_lo, j + 1)
            for j in range(4):
                ahead(Unit(U_MIX + 26 + j))
            new_x(2)
            rms_xn(2)
            norm_split(2)
            phase(ffn2)
            new_x(3)
            rms_xn(3)
            norm_split(3)

            for l in range(LAYERS):
                ul, rb = U_L + N_L * l, 6 + 6 * l
                if l:
                    norm_split(5)
                else:
                    dve.wait_ge(b2_in, 16)
                full, mla = slice(0, P), slice(0, 96)

                def heads(v):
                    return v.rearrange("p (h n) -> p h n", n=64)

                def wide(v):
                    return v.unsqueeze(2).to_broadcast([P, 8, 64])
                for i in range(len(IN_UNITS)):
                    ahead(Unit(ul + i))
                    if i in (1, 2):
                        r = i - 1
                        rope(r, rb, full, tables[:, 0, :], tables[:, 1, :], qraw2[r % 2], rtmp2, rqk[:, 2 * r:2 * r + 2, :], 2)
                    for h in {4: (0, 1), 5: (2,), 6: (3,)}.get(i, ()):
                        dve.wait_ge(ret_mm, 4 * l + h + 1)
                        dve.tensor_tensor(dret[h], ps[:, 6 + h % 2, 0:384], decay[:, h, :], ALU.mult).then_inc(ret_d, 1)
                    if i == 8:
                        for j, (ks, v) in enumerate((((0, 1, 2), V_QN + 3 * l), ((3, 4), V_KVN + 2 * l))):
                            dve.wait_ge(std_made, 2 * l + j + 1)
                            link(dve.reciprocal(rstdb[:, j, :], rstdb[:, j, :]))
                            for k in ks:
                                c = v + k - ks[0]
                                ins = dve.scalar_tensor_tensor(out=cT[:, k, :], in0=cT[:, k, :], scalar=vec8[:, c:c + 1],
                                                               in1=rstdb[:, j, :], op0=ALU.mult, op1=ALU.mult)
                                if k != ks[-1]:
                                    ins.then_inc(dve_step, 1)
                                    n_step[0] += 1
                            ins.then_inc(cn_made, 1)
                        dve.wait_ge(ret_o, 4 * l + 4)
                        link(dve.tensor_reduce(stat[:, 56:64], heads(ps[:, 5, :]), AX.X, ALU.add))
                        link(dve.tensor_scalar(stat[:, 56:64], stat[:, 56:64], 1.0 / 64, None, ALU.mult))
                        dve.tensor_tensor(heads(ocen), heads(ps[:, 5, :]), wide(stat[:, 56:64]), ALU.subtract).then_inc(ret_oc, 1)
                    elif i == 9:
                        for j, ks in enumerate((slice(0, 3), slice(3, 5))):
                            dve.wait_ge(c_hi, 2 * l + j + 1)
                            dve.tensor_tensor(clo[:, ks, :], cT[:, ks, :], chi[:, ks, :], ALU.subtract).then_inc(c_lo, 1)
                        dve.wait_ge(x_upd, 2 * (2 * l + 1))
                        rope(2, rb, slice(64, 96), tables[:, 2, :], tables[:, 3, :], qraw2[0], rtmp2,
                             kro[64:96, :].unsqueeze(1), 1)
                        dve.wait_ge(ret_std, 2 * l + 1)
                        dve.tensor_reduce(stat[:, 40:48], heads(osq), AX.X, ALU.add).then_inc(ret_var, 1)
                    elif i == 10:
                        dve.wait_ge(ret_std, 2 * l + 2)
                        link(dve.reciprocal(stat[:, 48:56], stat[:, 48:56]))
                        link(dve.tensor_tensor(heads(ocen), heads(ocen), wide(stat[:, 48:56]), ALU.mult))
                        dve.wait_ge(gn_in, 16 * (l + 1))
                        o3 = ocen.rearrange("p (t n) -> p t n", t=2)
                        link(dve.tensor_tensor(o3, o3, gnw.unsqueeze(1).to_broadcast([P, 2, T]), ALU.mult))
                        dve.wait_ge(proj_out, 10 + 19 * l + 8)
                        dve.tensor_tensor(oret.rearrange("p (t n) -> p t n", t=2), o3, rg, ALU.mult).then_inc(ret_y, 1)
                ahead(Unit(ul + 11))
                for j in range(3):
                    rope(3 + j, rb, mla, tables[:, 2, :], tables[:, 3, :], qraw2[(3 + j) % 2], rtmp2,
                         qm[0:96, 2 * j:2 * j + 2, :], 2)
                ahead(Unit(ul + 12))
                dve.wait_ge(ret_hi, l + 1)
                dve.scalar_tensor_tensor(out=mixlo[:, 0:2, :], in0=ps[:, 7, :].rearrange("p (k n) -> p k n", k=2), scalar=SX,
                                         in1=mixhi[:, 0:2, :], op0=ALU.mult, op1=ALU.subtract).then_inc(ret_lo, 1)
                dve.wait_ge(sinks_in, 16)
                attention(2, l)
                for j in range(4):
                    ahead(Unit(ul + 13 + j))
                n = 4 + 2 * l
                layer_xn(n)
                norm_split(n)
                ahead(Unit(ul + 17))

                def gates():
                    sc = rr[:, 0, :]
                    v3 = lambda i: rr[:, i, :].rearrange("p (t e) -> p t e", t=2)
                    v4 = lambda i: rr[:, i, :].rearrange("p (t g e) -> p t g e", t=2, g=4)
                    small8 = lambda i: rr[:, i, 0:8].rearrange("p (t g) -> p t g", t=2)
                    one2 = lambda i: rr[:, i, 0:2].unsqueeze(2)
                    prio16 = small[:, C_PRIO16:C_PRIO16 + 16].unsqueeze(1).to_broadcast([P, 2, 16])
                    prio4 = small[:, C_PRIO4:C_PRIO4 + 4].unsqueeze(1).to_broadcast([P, 2, 4])
                    TTO, TS = dve.tensor_tensor, dve.tensor_scalar
                    dve.wait_ge(bias_in, 16)
                    dve.wait_ge(router_sig, l + 1)
                    link(TTO(v3(1), v3(0), rbias[:, :].unsqueeze(1).to_broadcast([P, 2, 16]), ALU.add))
                    b = v4(1)
                    pairs = [(i, j) for i in range(4) for j in range(i + 1, 4)]
                    for n_, (i, j) in enumerate(pairs):
                        link(TTO(small8(2).unsqueeze(3), b[:, :, :, i:i + 1], b[:, :, :, j:j + 1], ALU.add) if n_ == 0 else
                             TTO(small8(3).unsqueeze(3), b[:, :, :, i:i + 1], b[:, :, :, j:j + 1], ALU.add))
                        if n_:
                            link(TTO(small8(2), small8(2), small8(3), ALU.max))

                    def first_best(v, n, prio, view, src, tmp, dst):
                        link(dve.tensor_reduce(rr[:, tmp, 0:2], view(src), AX.X, ALU.max))
                        link(TTO(view(dst), view(src), one2(tmp).to_broadcast([P, 2, n]), ALU.is_ge))
                        link(TTO(view(dst), view(dst), prio, ALU.mult))
                        link(dve.tensor_reduce(rr[:, tmp, 0:2], view(dst), AX.X, ALU.max))
                        link(TTO(view(dst), view(dst), one2(tmp).to_broadcast([P, 2, n]), ALU.is_equal))
                    first_best(None, 4, prio4, small8, 2, 4, 5)
                    link(TS(rr[:, 6, 0:8], rr[:, 5, 0:8], -1.0, -NEG, ALU.add, ALU.mult))
                    gsel = small8(5).unsqueeze(3).to_broadcast([P, 2, 4, 4])
                    gneg = small8(6).unsqueeze(3).to_broadcast([P, 2, 4, 4])
                    link(TTO(v4(7), v4(1), gsel, ALU.mult))
                    link(TTO(v4(7), v4(7), gneg, ALU.add))
                    first_best(None, 16, prio16, v3, 7, 4, 8)
                    link(dve.scalar_tensor_tensor(out=rr[:, 9, :], in0=rr[:, 8, :], scalar=3 * NEG, in1=rr[:, 7, :],
                                                  op0=ALU.mult, op1=ALU.add))
                    first_best(None, 16, prio16, v3, 9, 4, 10)
                    link(TTO(rr[:, 11, :], rr[:, 8, :], rr[:, 10, :], ALU.add))
                    link(TTO(rr[:, 12, :], rr[:, 11, :], rr[:, 0, :], ALU.mult))
                    link(dve.tensor_reduce(rr[:, 13, 0:2], v3(12), AX.X, ALU.add))
                    link(dve.reciprocal(rr[:, 14, 0:2], rr[:, 13, 0:2]))
                    TTO(v3(19), v3(12), one2(14).to_broadcast([P, 2, 16]), ALU.mult).then_inc(gate_made, 1)

                def gather(g):
                    xs = slice((g % 2) * P, (g % 2 + 1) * P)
                    for kp in range(4):
                        dve.wait_ge(ga_f[l], 4 * g + kp + 1)
                        dve.tensor_copy(uhi[:, 2 * kp:2 * kp + 2, xs], uq4[kp % 2]).then_inc(ga_hi[l], 1)
                        dve.wait_ge(ga_hi[l], 4 * g + kp + 1)
                        dve.tensor_tensor(ulo[:, 2 * kp:2 * kp + 2, xs], uq4[kp % 2], uhi[:, 2 * kp:2 * kp + 2, xs],
                                          ALU.subtract).then_inc(ga_lo[l], 1)

                def slots_chunk(c):
                    g, b0 = moe[l].g0 + c, 4 + 2 * (c % 2)
                    dve.wait_ge(silu_made, g + 1)
                    dve.wait_ge(h_lo, g)
                    dve.scalar_tensor_tensor(out=h_f32[:, 0:T], in0=ps[:, b0 + 1, 0:T], scalar=SX / S, in1=s_act[:, 0:T],
                                             op0=ALU.mult, op1=ALU.mult).then_inc(m_moe, 1)
                    dve.wait_ge(m_moe, g - 2 * FFN_CHUNKS + 1)
                    hv = h_f32[:, 0:T].rearrange("p (k n) -> p k n", k=2)
                    dve.tensor_tensor(hv, hv, gbs[:, c, :].unsqueeze(1).to_broadcast([P, 2, P]), ALU.mult).then_inc(h_made, 1)
                    dve.wait_ge(h_hi, g + 1)
                    dve.tensor_tensor(hlo[:, c % 2, 0:T], h_f32[:, 0:T], hhi[:, c % 2, 0:T], ALU.subtract).then_inc(h_lo, 1)

                def group_out(g):
                    for n in range(2):
                        h = slice(n * HALF, (n + 1) * HALF)
                        dve.wait_ge(ys_hi[l], 2 * g + n + 1)
                        dve.scalar_tensor_tensor(out=ysl[g][:, h], in0=ps[:, 2 * (g % 2) + n, :], scalar=SX / S,
                                                 in1=ysh[g][:, h], op0=ALU.mult, op1=ALU.subtract).then_inc(ys_lo[l], 1)

                def sparse(ph):
                    for t in range(TT):
                        for g in range(4):
                            r = 4 * t + g
                            last = dve.tensor_scalar(p32[:, t, g * P:(g + 1) * P], slot_no, rr[:, 15, r:r + 1],
                                                     rr[:, 5, r:r + 1], ALU.is_equal, ALU.mult)
                            last.then_inc(p_step[l], 1)
                    dve.tensor_copy(ident16, ident).then_inc(p_step[l], 1)
                    dve.wait_ge(p_step[l], 9)
                    dve.tensor_copy(p16, p32).then_inc(p16_made[l], 1)
                    dve.wait_ge(x_hi, l + 1)
                    gather(0)
                    ahead(Unit(ph.u0), 2)
                    dve.wait_ge(gbs_out[l], 4)
                    slots_chunk(0)
                    for c in range(1, ph.n):
                        ahead(Unit(ph.u0 + 3 * c - 1), 3)
                        slots_chunk(c)
                        if c % 4 == 2 and c < 12:
                            gather(c // 4 + 1)
                        if c % 4 == 0:
                            group_out(c // 4 - 1)
                    ahead(Unit(ph.u0 + 3 * ph.n - 1))
                    group_out(3)

                gates()
                dve.wait_ge(x_hi, l + 1)
                dve.scalar_tensor_tensor(out=xl, in0=xn[:, :, :], scalar=SX, in1=xh, op0=ALU.mult, op1=ALU.subtract)\
                    .then_inc(x_lo, 1)
                dve.wait_ge(rank_mm, l + 1)
                link(dve.tensor_copy(rr[:, 15, 0:12], ps[:, 6, 0:12]))
                link(dve.tensor_reduce(rr[:, 16, 0:1], rr[:, 15, 8:12], AX.X, ALU.max))
                dve.tensor_copy(rr[:, 17, 0:1].bitcast(I32), rr[:, 16, 0:1]).then_inc(rank_out, 1)
                dve.wait_ge(rank_out, l + 1)
                count = dve.value_load(rr[0:1, 17, 0:1].bitcast(I32))
                with dve.If(count > P):
                    dve.wait_ge(gb_out[l], 8)
                    phase(moe[l])
                with dve.Else():
                    sparse(moe[l])
                layer_xn(n + 1)
            dve.wait_ge(ln_in, 16 + 32 * 4)
            for t in range(TT):
                dve.wait_ge(xn_made, 14 + t + 1)
                link(dve.tensor_tensor(x[:, t, :], xn[:, t, :], lng, ALU.mult))
                dve.tensor_tensor(x[:, t, :], x[:, t, :], lnb, ALU.add).then_inc(x_new, 1)


_INS = ["x", "c", "positions", "w_ada", "b_ada", "g_norm_ffn1", "w_ffn1_in", "w_ffn1_out", "g_norm_mix", "w_in", "w_pool",
        "pool_scale", "w_pool_branch", "w_attn_branch", "w_out", "g_norm_ffn2", "w_ffn2_in", "w_ffn2_out", "g_final",
        "w_in_2", "ret_gn_w_2", "swa_sinks_2", "mla_q_norm_w_2", "mla_kv_norm_w_2", "mla_w_uq_2", "mla_w_ukv_2", "w_out_2",
        "ln1_g_2", "ln1_b_2", "router_w_2", "router_bias_2", "exp_w_gate_up_2", "exp_w_down_2", "ln2_g_2", "ln2_b_2"]


def kernel(**inputs):
    import concourse.bacc as _bacc
    from concourse.bass_utils import run_bass_kernel_spmd as _run

    nc = _bacc.Bacc("TRN2", target_bir_lowering=False, num_devices=1)
    arrays = {f"in_{n}_dram": np.ascontiguousarray(inputs[n]) for n in _INS}
    for name, table in zip(("const_small", "const_block1", "const_block2", "const_slots"), constants()):
        arrays[f"in_{name}_dram"] = table
    args = {k[3:-5]: nc.dram_tensor(k, v.shape, mybir.dt.from_np(v.dtype), kind="ExternalInput").ap()
            for k, v in arrays.items()}
    out = nc.dram_tensor("out_0_dram", (1, T, D), F32, kind="ExternalOutput").ap()
    build(nc, args, out)
    r = _run(nc, [arrays], core_ids=[0])
    return r.results[0]["out_0_dram"]
```
